# Optimizing a Trainium2 kernel written in Bass

```python
import math
import jax
import jax.numpy as jnp
from jax import lax
import numpy as np

D_MODEL = 1024
BATCH = 1
SEQ = 256
DEPTH = 1

MEM_LEN = 256
NSA_HEAD_DIM = 64
NSA_WIDTH = D_MODEL // 2
NSA_HEADS = NSA_WIDTH // NSA_HEAD_DIM
NSA_KV_GROUPS = 2
NSA_Q_PER_KV = NSA_HEADS // NSA_KV_GROUPS
CMP_BLOCK = 32
CMP_STRIDE = 16
CMP_HIDDEN = 2 * NSA_HEAD_DIM
SLC_BLOCK = 64
SLC_TOPN = 16
SLC_QBLOCK = 64
WIN = 512
WIN_QBLOCK = 128
FORCE_SCORE = 1e4
HG_DK = 128
HG_DV = HG_DK
HG_HEADS = (D_MODEL - NSA_WIDTH) // HG_DK
HG_CHUNK = 64
XA_HEADS = 4
XA_HEAD_DIM = D_MODEL // XA_HEADS
PEER_HEADS = 8
PEER_NKEYS = 128
PEER_N_EXPERTS = PEER_NKEYS * PEER_NKEYS
PEER_DKEY = 128
PEER_TOPK = 16
PEER_TOKEN_BLOCK = 128
IN_SPLITS = (NSA_WIDTH,) + (NSA_KV_GROUPS * NSA_HEAD_DIM,) * 6 + (NSA_HEADS * 3,) + (HG_HEADS * HG_DK, HG_HEADS * HG_DK, HG_HEADS * HG_DV, HG_HEADS * HG_DV)
IN_COLS = sum(IN_SPLITS)
LN_EPS = 1e-5
NEG_INF = -1e30
DEEPNORM_ALPHA = (2.0 * DEPTH) ** 0.25
DEEPNORM_BETA = (8.0 * DEPTH) ** -0.25

kernel_name = 'nsa_hgrn2_peer_deepnorm_hybrid'

def _layer_norm(x, g, b):
    xf = x.astype(jnp.float32)
    mu = jnp.mean(xf, axis=-1, keepdims=True)
    var = jnp.mean(jnp.square(xf - mu), axis=-1, keepdims=True)
    y = (xf - mu) * lax.rsqrt(var + LN_EPS)
    return (y * g.astype(jnp.float32) + b.astype(jnp.float32)).astype(x.dtype)

def _masked_softmax(s, mask):
    return jax.nn.softmax(jnp.where(mask, s, NEG_INF), axis=-1)

def _compress(blocks, pos_emb, w1, w2):
    b, nc, l, g, dh = blocks.shape
    h = (blocks + pos_emb[None, None, :, None, :]).transpose(0, 1, 3, 2, 4).reshape(b, nc, g, l * dh)
    return jax.nn.gelu(h @ w1) @ w2

def _nsa(q, k_cmp, v_cmp, k_slc, v_slc, k_win, v_win, gate_logits, cmp_pos, cmp_w1, cmp_w2):
    B, S = q.shape[0], q.shape[1]
    G, R, Dh = NSA_KV_GROUPS, NSA_Q_PER_KV, NSA_HEAD_DIM
    scale = Dh ** -0.5
    qg = q.reshape(B, S, G, R, Dh)
    pos = np.arange(S)

    n_cmp = (S - CMP_BLOCK) // CMP_STRIDE + 1
    cmp_idx = np.arange(n_cmp)[:, None] * CMP_STRIDE + np.arange(CMP_BLOCK)[None, :]
    kc = _compress(k_cmp[:, cmp_idx], cmp_pos[0], cmp_w1[0], cmp_w2[0])
    vc = _compress(v_cmp[:, cmp_idx], cmp_pos[1], cmp_w1[1], cmp_w2[1])
    cmp_valid = cmp_idx[:, -1][None, :] <= pos[:, None]
    s_cmp = jnp.einsum('bsgrd,bngd->bgrsn', qg, kc).astype(jnp.float32) * scale
    p_cmp = _masked_softmax(s_cmp, cmp_valid) * cmp_valid.any(-1)[:, None]
    o_cmp = jnp.einsum('bgrsn,bngd->bsgrd', p_cmp.astype(vc.dtype), vc)

    n_slc = S // SLC_BLOCK
    n_top = min(SLC_TOPN, n_slc)
    slc_start = np.arange(n_slc) * SLC_BLOCK
    cmp_start = np.arange(n_cmp) * CMP_STRIDE
    overlap = ((cmp_start[:, None] < slc_start[None, :] + SLC_BLOCK)
               & (cmp_start[:, None] + CMP_BLOCK > slc_start[None, :])).astype(np.float32)
    imp = jnp.einsum('bgrsn,nj->bsgj', p_cmp, jnp.asarray(overlap))
    cur = pos // SLC_BLOCK
    jb = np.arange(n_slc)
    forced = (jb[None] == 0) | (jb[None] == cur[:, None]) | (jb[None] == cur[:, None] - 1)
    future = jb[None] > cur[:, None]
    sel_score = jnp.where(future[None, :, None, :], -jnp.inf,
                          jnp.where(forced[None, :, None, :], FORCE_SCORE, imp))
    _, sel_idx = lax.top_k(sel_score, n_top)

    ks_b = k_slc.reshape(B, n_slc, SLC_BLOCK, G, Dh).transpose(0, 3, 1, 2, 4)
    vs_b = v_slc.reshape(B, n_slc, SLC_BLOCK, G, Dh).transpose(0, 3, 1, 2, 4)
    nqb = S // SLC_QBLOCK
    q_blocks = qg.reshape(B, nqb, SLC_QBLOCK, G, R, Dh).swapaxes(0, 1)
    i_blocks = sel_idx.reshape(B, nqb, SLC_QBLOCK, G, n_top).swapaxes(0, 1)
    p_blocks = jnp.asarray(pos.reshape(nqb, SLC_QBLOCK))
    b_ix = jnp.arange(B)[:, None, None, None]
    g_ix = jnp.arange(G)[None, None, :, None]

    def slc_block(args):
        qb, ib, pb = args
        kg = ks_b[b_ix, g_ix, ib]
        vg = vs_b[b_ix, g_ix, ib]
        s = jnp.einsum('bqgrd,bqgnld->bqgrnl', qb, kg).astype(jnp.float32) * scale
        key_pos = ib[..., None] * SLC_BLOCK + jnp.arange(SLC_BLOCK)
        ok = (key_pos <= pb[None, :, None, None, None])[:, :, :, None]
        s = jnp.where(ok, s, NEG_INF)
        p = jax.nn.softmax(s.reshape(B, SLC_QBLOCK, G, R, n_top * SLC_BLOCK), axis=-1).reshape(s.shape)
        return jnp.einsum('bqgrnl,bqgnld->bqgrd', p.astype(vg.dtype), vg)

    o_slc = lax.map(slc_block, (q_blocks, i_blocks, p_blocks)).swapaxes(0, 1).reshape(B, S, G, R, Dh)

    nwb = S // WIN_QBLOCK
    band = np.arange(nwb)[:, None] * WIN_QBLOCK + np.arange(WIN + WIN_QBLOCK)[None, :]
    key_pos_w = band - WIN
    q_pos_w = pos.reshape(nwb, WIN_QBLOCK)
    win_ok = ((key_pos_w[:, None, :] <= q_pos_w[:, :, None])
              & (key_pos_w[:, None, :] > q_pos_w[:, :, None] - WIN)
              & (key_pos_w[:, None, :] >= 0))
    pad = ((0, 0), (WIN, 0), (0, 0), (0, 0))
    kband = jnp.pad(k_win, pad)[:, band].swapaxes(0, 1)
    vband = jnp.pad(v_win, pad)[:, band].swapaxes(0, 1)
    qw = qg.reshape(B, nwb, WIN_QBLOCK, G, R, Dh).swapaxes(0, 1)

    def win_block(args):
        qb, kb, vb, mb = args
        s = jnp.einsum('bqgrd,bkgd->bgrqk', qb, kb).astype(jnp.float32) * scale
        p = _masked_softmax(s, mb[None, None, None])
        return jnp.einsum('bgrqk,bkgd->bqgrd', p.astype(vb.dtype), vb)

    o_win = lax.map(win_block, (qw, kband, vband, jnp.asarray(win_ok))).swapaxes(0, 1).reshape(B, S, G, R, Dh)

    gates = jax.nn.sigmoid(gate_logits.astype(jnp.float32)).reshape(B, S, G, R, 3).astype(q.dtype)
    o = gates[..., 0:1] * o_cmp + gates[..., 1:2] * o_slc + gates[..., 2:3] * o_win
    return o.reshape(B, S, NSA_WIDTH)

def _hgrn2(q, f_logits, i, g, lower_bound, norm_w):
    B, S = q.shape[0], q.shape[1]
    H, Dk, Dv, C = HG_HEADS, HG_DK, HG_DV, HG_CHUNK
    nc = S // C
    lb = lower_bound[None, None]
    f = lb + (1.0 - lb) * jax.nn.sigmoid(f_logits.astype(jnp.float32).reshape(B, S, H, Dk))
    k = 1.0 - f
    log_f = jnp.log(f)

    def chunks(a, d):
        return a.astype(jnp.float32).reshape(B, nc, C, H, d).transpose(1, 0, 3, 2, 4)

    causal = np.tril(np.ones((C, C), dtype=bool))[None, None, :, :, None]

    def step(state, inp):
        qc, kc, vc, gc = inp
        b = jnp.cumsum(gc, axis=2)
        decay = jnp.exp(jnp.where(causal, b[:, :, :, None, :] - b[:, :, None, :, :], -jnp.inf))
        attn = jnp.einsum('bhtd,bhsd,bhtsd->bhts', qc, kc, decay)
        o = jnp.einsum('bhts,bhse->bhte', attn, vc) + jnp.einsum('bhtd,bhde->bhte', qc * jnp.exp(b), state)
        b_last = b[:, :, -1:, :]
        new_state = (jnp.exp(b_last[:, :, 0, :])[..., None] * state
                     + jnp.einsum('bhsd,bhse->bhde', kc * jnp.exp(b_last - b), vc))
        return new_state, o

    state0 = jnp.zeros((B, H, Dk, Dv), jnp.float32)
    _, o = lax.scan(step, state0, (chunks(q, Dk), chunks(k, Dk), chunks(i, Dv), chunks(log_f, Dk)))
    o = o.transpose(1, 0, 3, 2, 4).reshape(B, S, H, Dv)
    o = o * lax.rsqrt(jnp.mean(jnp.square(o), axis=-1, keepdims=True) + LN_EPS) * norm_w.astype(jnp.float32)
    o = o * jax.nn.silu(g.astype(jnp.float32).reshape(B, S, H, Dv))
    return o.reshape(B, S, H * Dv).astype(q.dtype)

def _hybrid_mixer(x, w_in, cmp_pos, cmp_w1, cmp_w2, lower_bound, norm_w, w_out):
    B, S, _ = x.shape
    h = x @ w_in
    offs = [int(o) for o in np.cumsum(IN_SPLITS)[:-1]]
    q_a, kc, vc, ks, vs, kw, vw, gate_a, q_b, f_b, i_b, g_b = jnp.split(h, offs, axis=-1)

    def kv(a):
        return a.reshape(B, S, NSA_KV_GROUPS, NSA_HEAD_DIM)

    o_a = _nsa(q_a.reshape(B, S, NSA_HEADS, NSA_HEAD_DIM), kv(kc), kv(vc), kv(ks), kv(vs), kv(kw), kv(vw),
               gate_a, cmp_pos, cmp_w1, cmp_w2)
    o_b = _hgrn2(q_b, f_b, i_b, g_b, lower_bound, norm_w)
    return jnp.concatenate([o_a, o_b], axis=-1) @ w_out

def _memory_cross_attention(x, mem, wq, wkv, wo):
    B, S, _ = x.shape
    M = mem.shape[1]
    q = (x @ wq).reshape(B, S, XA_HEADS, XA_HEAD_DIM)
    kvm = (mem @ wkv).reshape(B, M, 2, XA_HEADS, XA_HEAD_DIM)
    k, v = kvm[:, :, 0], kvm[:, :, 1]
    s = jnp.einsum('bshd,bmhd->bhsm', q, k).astype(jnp.float32) * XA_HEAD_DIM ** -0.5
    p = jax.nn.softmax(s, axis=-1)
    o = jnp.einsum('bhsm,bmhd->bshd', p.astype(v.dtype), v).reshape(B, S, XA_HEADS * XA_HEAD_DIM)
    return o @ wo

def _peer(x, wq, sub_keys, down, up):
    B, S, D = x.shape
    T = B * S
    t = x.reshape(T, D)
    qry = (t @ wq).reshape(T, PEER_HEADS, 2, PEER_DKEY // 2)
    s = jnp.einsum('thcd,hcnd->thcn', qry, sub_keys).astype(jnp.float32)
    s1, i1 = lax.top_k(s[:, :, 0], PEER_TOPK)
    s2, i2 = lax.top_k(s[:, :, 1], PEER_TOPK)
    cand_s = (s1[..., :, None] + s2[..., None, :]).reshape(T, PEER_HEADS, PEER_TOPK * PEER_TOPK)
    cand_i = (i1[..., :, None] * PEER_NKEYS + i2[..., None, :]).reshape(T, PEER_HEADS, PEER_TOPK * PEER_TOPK)
    top_s, top_pos = lax.top_k(cand_s, PEER_TOPK)
    expert = jnp.take_along_axis(cand_i, top_pos, axis=-1)
    gate = jax.nn.softmax(top_s, axis=-1)
    nb = T // PEER_TOKEN_BLOCK
    E = PEER_HEADS * PEER_TOPK

    def block(args):
        tb, eb, gb = args
        a = jax.nn.gelu(jnp.einsum('ted,td->te', down[eb], tb).astype(jnp.float32), approximate=False)
        return jnp.einsum('te,ted->td', (a * gb).astype(up.dtype), up[eb])

    out = lax.map(block, (t.reshape(nb, PEER_TOKEN_BLOCK, D), expert.reshape(nb, PEER_TOKEN_BLOCK, E),
                          gate.reshape(nb, PEER_TOKEN_BLOCK, E)))
    return out.reshape(B, S, D)

def setup_inputs(seed: int = 0) -> dict:
    key = jax.random.key(seed)
    ks = jax.random.split(key, 18)

    def nrm(k, shape, scale):
        return jax.random.normal(k, shape, jnp.float32) * scale

    D = D_MODEL
    return {
        'x': nrm(ks[0], (BATCH, SEQ, D), 1.0),
        'mem': nrm(ks[1], (BATCH, MEM_LEN, D), 1.0),
        'w_in': nrm(ks[2], (DEPTH, D, IN_COLS), D ** -0.5),
        'cmp_pos': nrm(ks[3], (DEPTH, 2, CMP_BLOCK, NSA_HEAD_DIM), 0.1),
        'cmp_w1': nrm(ks[4], (DEPTH, 2, CMP_BLOCK * NSA_HEAD_DIM, CMP_HIDDEN), (CMP_BLOCK * NSA_HEAD_DIM) ** -0.5),
        'cmp_w2': nrm(ks[5], (DEPTH, 2, CMP_HIDDEN, NSA_HEAD_DIM), CMP_HIDDEN ** -0.5),
        'hgrn_lb_logits': nrm(ks[6], (DEPTH + 1, HG_HEADS, HG_DK), 0.5),
        'hgrn_norm_w': 1.0 + nrm(ks[7], (DEPTH, HG_HEADS, HG_DV), 0.02),
        'w_out': nrm(ks[8], (DEPTH, D, D), D ** -0.5 * DEEPNORM_BETA),
        'xa_wq': nrm(ks[9], (DEPTH, D, D), D ** -0.5),
        'xa_wkv': nrm(ks[10], (DEPTH, D, 2 * D), D ** -0.5),
        'xa_wo': nrm(ks[11], (DEPTH, D, D), D ** -0.5 * DEEPNORM_BETA),
        'peer_wq': nrm(ks[12], (DEPTH, D, PEER_HEADS * PEER_DKEY), D ** -0.5),
        'peer_subkeys': nrm(ks[13], (DEPTH, PEER_HEADS, 2, PEER_NKEYS, PEER_DKEY // 2), (PEER_DKEY // 2) ** -0.5),
        'peer_down': nrm(ks[14], (DEPTH, PEER_N_EXPERTS, D), D ** -0.5),
        'peer_up': nrm(ks[15], (DEPTH, PEER_N_EXPERTS, D), DEEPNORM_BETA),
        'ln_g': 1.0 + nrm(ks[16], (DEPTH, 3, D), 0.02),
        'ln_b': nrm(ks[17], (DEPTH, 3, D), 0.02),
    }

def reference(x, mem, w_in, cmp_pos, cmp_w1, cmp_w2, hgrn_lb_logits, hgrn_norm_w, w_out,
              xa_wq, xa_wkv, xa_wo, peer_wq, peer_subkeys, peer_down, peer_up, ln_g, ln_b):
    lower_bounds = jnp.cumsum(jax.nn.softmax(hgrn_lb_logits.astype(jnp.float32), axis=0), axis=0)
    for l in range(DEPTH):
        mix = _hybrid_mixer(x, w_in[l], cmp_pos[l], cmp_w1[l], cmp_w2[l], lower_bounds[l], hgrn_norm_w[l], w_out[l])
        x = _layer_norm(DEEPNORM_ALPHA * x + mix, ln_g[l, 0], ln_b[l, 0])
        xa = _memory_cross_attention(x, mem, xa_wq[l], xa_wkv[l], xa_wo[l])
        x = _layer_norm(DEEPNORM_ALPHA * x + xa, ln_g[l, 1], ln_b[l, 1])
        ff = _peer(x, peer_wq[l], peer_subkeys[l], peer_down[l], peer_up[l])
        x = _layer_norm(DEEPNORM_ALPHA * x + ff, ln_g[l, 2], ln_b[l, 2])
    return x


_drawn_inputs = setup_inputs


def setup_inputs(seed=0):
    import zlib

    import numpy as np

    out = dict(_drawn_inputs(seed))
    spreads = {}
    factors = {'hgrn_norm_w': 3.239}
    for name, (base, spread) in spreads.items():
        noise = np.random.default_rng([zlib.crc32(name.encode()), seed]).standard_normal(out[name].shape)
        drawn = base * np.exp(spread * noise) if base else spread * noise
        out[name] = jnp.asarray(drawn.astype(out[name].dtype))
    for name, factor in factors.items():
        out[name] = (out[name] * factor).astype(out[name].dtype)
    return out
```

```python
import numpy as np
import concourse.bass as bass
import concourse.mybir as mybir

FP32 = mybir.dt.float32
F32R = mybir.dt.float32r
BF16 = mybir.dt.bfloat16
U32 = mybir.dt.uint32
U16 = mybir.dt.uint16
ACT = mybir.ActivationFunctionType
ALU = mybir.AluOpType
AX = mybir.AxisListType

P = 128
D = 1024
S = 256
NT = S // P
KD = D // P
HD = 64
NH = 8
G = 2
REP = NH // G
CB, CS = 32, 16
NC = (S - CB) // CS + 1
HH = 4
XH = 4
PH = 8
TOPK = 16
NK = 128
E_TILES = NK * NK // P
ALPHA = 2.0 ** 0.25
EPS = 1e-5
VG = 2 * P + 3 * NH

RUNS = [("kc", "T", 1), ("vc", "T", 1), ("ks", "T", 1), ("kw", "T", 1), ("q", "T", 4), ("vg", "R", 1),
        ("hq", "T", HH), ("hf", "T", HH), ("hv", "R", 1), ("hg", "R", 1),
        ("mk", "T", KD), ("mv", "R", 2), ("wo", "R", 2), ("xq", "T", KD), ("xo", "R", 2), ("pq", "T", KD)]


def plan():
    tiles, at, use = [], {}, 0
    for name, kind, count in RUNS:
        at[name] = len(tiles)
        for i in range(count):
            if kind == "T":
                tiles.append((name, kind, i, 0, KD, P, True, True, use))
                use += 1
            else:
                cols = VG if name == "vg" else 512
                per = D // cols
                k = 0
                while k < KD:
                    m = min(per, KD - k)
                    tiles.append((name, kind, i, k, m, cols, k == 0, k + m == KD, use))
                    k += m
                use += NT
    return tiles, at, use


TILES, AT, USES = plan()
N1 = len(TILES)
DEPTH = 4
VECTOR_READS = ("wo", "xo")


def consumers():
    count, out = [0, 0], []
    for name, kind, i, k0, m, cols, first, last, use in TILES:
        if first:
            v = int(name in VECTOR_READS)
            for _ in range(1 if kind == "T" else NT):
                count[v] += 1
                out.append((v, count[v]))
    return out, count


TAKEN, TAKEN_ALL = consumers()

UNITS = [(b, g, t) for b in range(2) for g in range(G) for t in range(NT)]


def order():
    out = []
    n = 0

    def gemm(k):
        nonlocal n
        for _ in range(k):
            out.append(("gemm", n))
            n += 1
    gemm(4)
    out.append(("blocks", 0))
    gemm(AT["hq"] - 4)
    out.append(("hidden", 0))
    gemm(1)
    out.append(("gelu", 0))
    gemm(1)
    out.append(("compressed", 0))
    for u in range(len(UNITS)):
        out.append(("scores", u))
        gemm(2)
        out.append(("turn_probs", u))
        gemm(1)
        out.append(("values", u))
        if n >= AT["hv"] and ("decay", 0) not in out:
            out.append(("decay", 0))
    for u in range(len(UNITS), len(UNITS) + NT):
        out.append(("scores", u))
        gemm(1)
        out.append(("turn_probs", u))
        gemm(1)
        out.append(("values", u))
    for j in range(9):
        out.append(("level", j))
        gemm(min(1, AT["wo"] - n))
    out += [("read_out", 0), ("read_out", 1), ("rms", 0), ("turn", 0), ("turn", 1)]
    gemm(AT["xq"] - n)
    out += [("norm", (0, 0)), ("norm", (0, 1)), ("turn", 2), ("turn", 3)]
    gemm(AT["xo"] - n)
    out += [("scores", 10), ("scores", 11), ("turn_probs", 10), ("values", 10),
            ("turn_probs", 11), ("values", 11), ("turn", 4), ("turn", 5)]
    gemm(AT["pq"] - n)
    out += [("norm", (1, 0)), ("norm", (1, 1)), ("turn", 6), ("turn", 7)]
    gemm(N1 - n)
    return out


ORDER = order()


class Steps:

    def __init__(self, engine, semaphore):
        self.engine, self.semaphore, self.count = engine, semaphore, 0

    def __call__(self, instruction):
        instruction.then_inc(self.semaphore, 1)
        self.count += 1

    def wait(self):
        self.engine.wait_ge(self.semaphore, self.count)


def build(nc, a):
    from contextlib import ExitStack
    ctx = ExitStack()
    with ctx:
        base = -(-nc.sbuf_base // 32) * 32
        place = {"at": base}

        def sb(name, shape, dt=FP32, at=None):
            size = int(np.prod(shape[1:])) * {FP32: 4, F32R: 4, BF16: 2, U32: 4}[dt]
            size = -(-size // 32) * 32
            where = place["at"] if at is None else at
            if at is None:
                place["at"] += size
            return nc.alloc_sbuf_tensor_at(name, shape, dt, offset=where)

        def ps(name, shape, dt=FP32):
            return ctx.enter_context(nc.psum_tensor(name, shape, dt))

        def sem(name):
            return ctx.enter_context(nc.semaphore(name))

        ident = sb("ident", [P, P])
        identb = sb("identb", [P, P], BF16)
        iota = sb("iota", [P, P], BF16)
        x2 = sb("x2", [P, NT, D])
        B_at = place["at"]
        b_hi = sb("b_hi", [P, KD, S], F32R)
        b_lo = sb("b_lo", [P, KD, S], F32R)
        raw = [sb(f"raw{i}", [P, D]) for i in range(2)]
        hi = [sb(f"hi{i}", [P, D], F32R) for i in range(DEPTH)]
        lo = [sb(f"lo{i}", [P, D], F32R) for i in range(DEPTH)]
        R_at = place["at"]

        H = sb("H", [P, E_TILES, S])
        late_at = place["at"]
        score_at = R_at + (E_TILES - 14) * S * 4
        route_s = sb("route_s", [P, PH * NT, 2 * NK], at=score_at)
        place["at"] = late_at + 2 * 1024
        chosen = sb("chosen", [P, 2, PH * NT, TOPK])
        chosen_s = sb("chosen_s", [P, PH * NT, TOPK])
        i2T = sb("i2T", [P, S])
        igT = sb("igT", [P, S, 2])
        route_at = place["at"]
        unit_s = sb("unit_s", [P, 2, NK])
        unit_w = sb("unit_w", [P, 2, NK])
        unit_c = sb("unit_c", [P, 2, TOPK, TOPK])
        unit_m = sb("unit_m", [P, 2, TOPK])
        unit_i = sb("unit_i", [P, 2, TOPK], U32)
        unit_if = sb("unit_if", [P, 2, TOPK])
        unit_t = sb("unit_t", [P, TOPK])
        unit_p = sb("unit_p", [P, TOPK], U32)
        unit_ab = sb("unit_ab", [P, 2, TOPK], U32)
        unit_abf = sb("unit_abf", [P, 2, TOPK])
        iota16 = sb("iota16", [P, TOPK])
        gate_z = sb("gate_z", [P, PH * NT], at=route_at)
        hold_v = sb("hold_v", [P, 8])
        hold_p = sb("hold_p", [P, 8])
        ig_now = [sb(f"ig_now{i}", [P, 4, 2]) for i in range(2)]
        assert place["at"] <= nc.sbuf_usable_end, place["at"] - nc.sbuf_usable_end
        one2 = [sb(f"one2_{i}", [P, 4, NK], at=B_at + 2048 * i) for i in range(2)]
        one1 = [sb(f"one1_{i}", [P, 4, NK], at=B_at + 4096 + 2048 * i) for i in range(2)]
        ln_last = sb("ln_last", [P, 2, D], at=B_at)
        a_hi = [sb(f"act_hi{i}", [P, S], F32R, at=B_at + 8192 + 1024 * i) for i in range(4)]
        a_lo = [sb(f"act_lo{i}", [P, S], F32R, at=B_at + 12288 + 1024 * i) for i in range(4)]

        place["at"] = R_at
        raw += [sb(f"raw{i}", [P, D]) for i in (2, 3)]
        o_hi = sb("o_hi", [P, KD, S], F32R)
        o_lo = sb("o_lo", [P, KD, S], F32R)
        ln_gb = sb("ln_gb", [P, 2, D])
        xk_at = place["at"]
        xk = sb("xk", [P, KD, S])
        xT = sb("xT", [P, KD, S], at=xk_at)
        xq_at = place["at"]
        xq = sb("xq", [P, KD, S])
        memT = sb("memT", [P, KD, S], at=xq_at)
        xv_at = place["at"]
        xv = sb("xv", [P, NT, D])
        hg_t = sb("hg_t", [P, NT, 512], at=xv_at)
        qT = sb("qT", [P, REP, S])
        kT = [sb(f"kT{i}", [P, S]) for i in range(2)]
        vg = sb("vg", [P, NT, VG])
        gate = sb("gate", [P, NT, 3 * NH])
        kv_at = place["at"]
        kvc = sb("kvc", [P, 2, S])
        kcp = sb("kcp", [P, 2, G, S])
        blk = sb("blk", [P, 2, CB // 2, G * NC])
        place["at"] = max(place["at"], kv_at + 8192)
        x_tok = sb("x_tok", [P, NT, D], at=kv_at)
        w1_at = place["at"]
        w1 = sb("w1", [P, 2, CB // 2, P])
        x1 = sb("x1", [P, NT, D], at=w1_at)
        xo = sb("xo", [P, NT, D], at=w1_at + 8192)
        w2 = sb("w2", [P, 2, HD])
        pos = sb("pos", [P, 2, CB // 2])
        hx = sb("hx", [P, 2 * G * NC])
        hy = sb("hy", [P, 2 * G * NC])
        hz = sb("hz", [P, 2 * G * NC])
        kcmp = sb("kcmp", [P, NC])
        vcmp = sb("vcmp", [NC, P])
        probs = sb("probs", [P, 4 * S])
        probsT = sb("probsT", [P, 4 * S])
        neg_max = sb("neg_max", [P, 2, NH])
        row_max = sb("row_max", [P, NH])
        row_sum = sb("row_sum", [P, 2, NH])
        coef = sb("coef", [P, NH])
        cmp_s = sb("cmp_s", [P, NH, NC])
        o_acc = sb("o_acc", [P, NT, 512])
        o_tmp = sb("o_tmp", [P, 512])
        causal = sb("causal", [P, P], BF16)
        cmp_mask = sb("cmp_mask", [P, NT, NC])
        cmp_any = sb("cmp_any", [P, NT])
        hq_at = place["at"]
        hq = sb("hq", [P, HH, S])
        oh = sb("oh", [P, NT, 512], at=hq_at)
        QF = sb("QF", [P, HH, S])
        KB = sb("KB", [P, HH, S])
        Fa = sb("Fa", [P, HH * S])
        Fb = sb("Fb", [P, HH * S // 2])
        lb = sb("lb", [P, 8, HH])
        level_mask = sb("level_mask", [P, 8, P], BF16, at=w1_at + 8192)
        att = sb("att", [P, HH, NT, P])
        att_off = sb("att_off", [P, HH, P])
        hv = sb("hv", [P, NT, 512])
        hg = sb("hg", [P, NT, 512])
        norm_w = sb("norm_w", [P, 512])
        stats = sb("stats", [P, NT, 2, 6])
        mv = sb("mv", [P, NT, 2])
        std = sb("std", [P, NT, HH])
        rstd = sb("rstd", [P, NT, HH])
        assert place["at"] <= nc.sbuf_usable_end, place["at"] - nc.sbuf_usable_end
        qryT = sb("qryT", [P, PH, S], at=xk_at)
        subk = sb("subk", [P, PH, 2 * NK], at=kv_at)
        stats2 = sb("stats2", [P, NT, 2, 6], at=route_at)
        mv2 = sb("mv2", [P, NT, 2], at=route_at + 128)
        std2 = sb("std2", [P, NT, HH], at=route_at + 192)
        rstd2 = sb("rstd2", [P, NT, HH], at=route_at + 256)

        psG = [ps(f"psG{i}", [P, 512]) for i in range(2)]
        psS = ps("psS", [P, 1024])
        psT = ps("psT", [P, 1024])
        psO = ps("psO", [P, 1024])
        psM = psO[:, 512:1024]

        raw_in = [sem(f"raw_in{i}") for i in range(4)]
        table_in = [sem(f"table_in{i}") for i in range(2)]
        hi_done, lo_done, tile_used = sem("hi_done"), sem("lo_done"), sem("tile_used")
        x_in, mem_in, const_in, comp_in = sem("x_in"), sem("mem_in"), sem("const_in"), sem("comp_in")
        rec_in, xtok_in, subk_in, ln_in = sem("rec_in"), sem("xtok_in"), sem("subk_in"), sem("ln_in")
        shift_in, out_done, hold_ready = sem("shift_in"), sem("out_done"), sem("hold_ready")
        mask_in = sem("mask_in")
        split_hi, split_lo = sem("split_hi"), sem("split_lo")
        act_took, dve_took = sem("act_took"), sem("dve_took")
        took = (act_took, dve_took)
        blocks_ready, hidden_done, hidden_out, tanh_done, gelu_ready = (
            sem("blocks_ready"), sem("hidden_done"), sem("hidden_out"), sem("tanh_done"), sem("gelu_ready"))
        cmp_done, cmp_out = sem("cmp_done"), sem("cmp_out")
        s_done, max_done, exp_done, turned, probsT_ready, pv_done, combined = (
            sem("s_done"), sem("max_done"), sem("exp_done"), sem("turned"), sem("probsT_ready"),
            sem("pv_done"), sem("combined"))
        lb_exp, lb_max = sem("lb_exp"), sem("lb_max")
        att_zero, decay_ready, level_done, level_merged, factors_ready = (
            sem("att_zero"), sem("decay_ready"), sem("level_done"), sem("level_merged"), sem("factors_ready"))
        off_ready, read_done, read_out_ready, var_ready, std_ready, rec_ready = (
            sem("off_ready"), sem("read_done"), sem("read_out_ready"), sem("var_ready"), sem("std_ready"),
            sem("rec_ready"))
        turn_done, turn_hi, turn_lo = sem("turn_done"), sem("turn_hi"), sem("turn_lo")
        norm_ready = sem("norm_ready")
        score_done, score_out = sem("score_done"), sem("score_out")
        h_out, routed = sem("h_out"), sem("routed")
        shifted, gate_exp, gate_ready, index_done, index_out = (
            sem("shifted"), sem("gate_exp"), sem("gate_ready"), sem("index_done"), sem("index_out"))
        one2_ready, one1_ready, gates_done, gated = (
            sem("one2_ready"), sem("one1_ready"), sem("gates_done"), sem("gated"))
        act_hi, act_lo = sem("act_hi"), sem("act_lo")
        act_step, dve_step, pool_step = sem("act_step"), sem("dve_step"), sem("pool_step")
        block = ctx.enter_context(nc.Block())

        XU = len(UNITS) + NT

        def unit(u):
            if u < len(UNITS):
                b, g, t = UNITS[u]
                return b, g, t, REP, P * (t + 1)
            if u < XU:
                return 2, 0, u - len(UNITS), NH, NC
            return 3, 0, u - XU, XH, S

        @block.sync
        def _(sp):
            sp.dma_start(xT[:], a["xT"]).then_inc(x_in, 16)
            for n in range(N1):
                if n >= 4:
                    sp.wait_ge(lo_done, n - 3)
                sp.dma_start(raw[n % 4][:], a["w_stream"][n]).then_inc(raw_in[n % 4], 16)
                if n == 3:
                    sp.dma_start(memT[:], a["memT"]).then_inc(mem_in, 16)
            for j in range(2):
                sp.wait_ge(lo_done, N1 + j - 1)
                sp.dma_start(raw[j][:], a["down"][j]).then_inc(table_in[j], 16)
            with sp.Fori(1, E_TILES // 2) as it:
                for i in range(2):
                    sp.wait_ge(lo_done, it * 2 + (N1 + i - 1))
                    sp.dma_start(raw[i][:], a["down"][it * 2 + i]).then_inc(table_in[i], 16)
            with sp.Fori(0, E_TILES // 2) as it:
                for i in range(2):
                    sp.wait_ge(lo_done, it * 2 + (N1 + E_TILES + i - 1))
                    sp.dma_start(raw[i][:], a["up"][it * 2 + i]).then_inc(table_in[i], 16)
            for t in range(NT):
                sp.wait_ge(norm_ready, 2 * NT + t + 1)
                sp.dma_start(a["out"][t * P:(t + 1) * P, :], x2[:, t, :]).then_inc(out_done, 16)
            sp.wait_ge(out_done, 16 * NT)

        @block.gpsimd
        def _(pool):
            for dst, name in ((pos, "pos"), (w1, "w1"), (w2, "w2")):
                pool.dma_start(dst[:], a[name]).then_inc(comp_in, 16)
            for dst, name in ((ident, "ident"), (identb, "identb"), (iota, "iota"), (causal, "causal"),
                              (cmp_mask, "cmp_mask"), (cmp_any, "cmp_any")):
                pool.dma_start(dst[:], a[name]).then_inc(const_in, 16)
            pool.dma_start(lb[:, 0:2, :], a["lb"]).then_inc(rec_in, 16)
            pool.dma_start(norm_w[:], a["norm_w"].broadcast_to([P, 512])).then_inc(rec_in, 16)
            for i, name in enumerate(("ln_g", "ln_b")):
                pool.dma_start(ln_gb[:, i, :], a[name][0:1, :].broadcast_to([P, D])).then_inc(ln_in, 16)
            pool.memset(att[:], 0.0).then_inc(att_zero, 1)
            pool.wait_ge(act_took, 2)
            for g in range(G):
                for par in range(2):
                    pool.dma_start(kcp[par * HD:(par + 1) * HD, :, g, 0:S - par],
                                   kvc[g * HD:(g + 1) * HD, :, par:S]).then_inc(shift_in, 16)
            pool.wait_ge(hidden_done, 1)
            pool.dma_start(level_mask[:], a["level_mask"]).then_inc(mask_in, 16)
            pool.dma_start(x_tok[:], a["x_tok"]).then_inc(xtok_in, 16)
            pool.wait_ge(norm_ready, NT)
            for i, name in enumerate(("ln_g", "ln_b")):
                pool.dma_start(ln_gb[:, i, :], a[name][1:2, :].broadcast_to([P, D])).then_inc(ln_in, 16)
            pool.dma_start(subk[:], a["subk"]).then_inc(subk_in, 16)
            pool.dma_start(iota16[:], a["iota16"]).then_inc(subk_in, 16)
            pool.memset(hold_p[:], 0.0).then_inc(hold_ready, 1)
            pool.wait_ge(hold_ready, 1)
            pool.wait_ge(index_out, 3)
            step = Steps(pool, pool_step)

            def group(g, slot, first):
                pool.tensor_copy(ig_now[slot][:], igT[:, bass.ds(g * 4, 4), :]).then_inc(pool_step, 1)
                pool.wait_ge(pool_step, g + 1)
                if not first:
                    pool.wait_ge(gates_done, g - 1)
                pool.tensor_tensor(hold_p[:, 0:1], hold_p[:, 1:2], hold_p[:, 1:2], ALU.add)
                for i in range(4):
                    last = pool.tensor_scalar(one1[slot][:, i, :], iota[:], ig_now[slot][:, i, 0:1],
                                              ig_now[slot][:, i, 1:2], ALU.is_equal, ALU.mult)
                last.then_inc(one1_ready, 1)
            for i in range(2):
                group(i, i, True)
            with pool.Fori(1, S // 8) as it:
                for i in range(2):
                    group(it * 2 + i, i, False)
            pool.wait_ge(gates_done, S // 4)
            for i, name in enumerate(("ln_g", "ln_b")):
                pool.dma_start(ln_last[:, i, :], a[name][2:3, :].broadcast_to([P, D])).then_inc(ln_in, 16)

        @block.scalar
        def _(act):
            step = Steps(act, act_step)

            def split(n):
                act.wait_ge(raw_in[n % 4], 16 * (n // 4 + 1))
                if n >= DEPTH:
                    act.wait_ge(tile_used, n - DEPTH + 1)
                act.activation(hi[n % DEPTH][:], raw[n % 4][:], ACT.Copy).then_inc(hi_done, 1)

            def split_table(n, i, arrived):
                act.wait_ge(table_in[i % 2], arrived)
                act.wait_ge(tile_used, n - DEPTH + 1)
                act.activation(hi[(N1 + i) % DEPTH][:], raw[i % 2][:], ACT.Copy).then_inc(hi_done, 1)

            def take(n):
                name, kind, i, k0, m, cols, first, last, use = TILES[n]
                if not last or name in VECTOR_READS:
                    return
                act.wait_ge(tile_used, n + 1)
                if kind == "T":
                    src = psG[use % 2][:, 0:S]
                    if name == "hf":
                        act.activation(Fa[:, i * S:(i + 1) * S], src, ACT.Tanh, scale=0.5).then_inc(act_took, 1)
                        return
                    if name == "pq" and i == 0:
                        act.wait_ge(turned, XU + NT)
                    dst = {"kc": kvc[:, 0, :], "vc": kvc[:, 1, :], "ks": kT[0][:], "kw": kT[1][:],
                           "q": qT[:, i % REP, :], "hq": hq[:, i % HH, :], "mk": xk[:, i, :], "xq": xq[:, i, :],
                           "pq": qryT[:, i, :]}[name]
                    act.activation(dst, src, ACT.Copy).then_inc(act_took, 1)
                    return
                for t in range(NT):
                    src = psG[(use + t) % 2]
                    if name == "vg":
                        act.activation(vg[:, t, 0:2 * P], src[:, 0:2 * P], ACT.Copy)
                        act.activation(vg[:, t, 2 * P:VG], src[:, 2 * P:VG], ACT.Tanh, scale=0.5).then_inc(act_took, 1)
                    elif name == "hv":
                        act.activation(hv[:, t, :], src[:], ACT.Copy).then_inc(act_took, 1)
                    elif name == "hg":
                        act.activation(hg[:, t, :], src[:], ACT.Copy)
                        act.activation(hg_t[:, t, :], src[:], ACT.Tanh, scale=0.5).then_inc(act_took, 1)
                    else:
                        act.activation(xv[:, t, i * 512:(i + 1) * 512], src[:], ACT.Copy).then_inc(act_took, 1)

            def exp_unit(u):
                b, g, t, heads, keys = unit(u)
                act.wait_ge(max_done, u + 1)
                if u:
                    act.wait_ge(turned, u)
                if b == 2:
                    act.activation(probs[:, 0:NH * NC], cmp_s[:, :, :].rearrange("p h n -> p (h n)"), ACT.Exp)\
                        .then_inc(exp_done, 1)
                    return
                scale = HD ** -0.5 if b < 2 else (D // XH) ** -0.5
                for r in range(heads):
                    last = act.activation(probs[:, r * S:r * S + keys], psS[:, r * S:r * S + keys], ACT.Exp,
                                          bias=neg_max[:, u % 2, r:r + 1], scale=scale,
                                          accum_out=row_sum[:, u % 2, r:r + 1])
                last.then_inc(exp_done, 1)

            def take_probsT(u):
                b, g, t, heads, keys = unit(u)
                act.wait_ge(turned, u + 1)
                if u:
                    act.wait_ge(pv_done, u)
                if b == 2:
                    act.activation(probsT[0:NC, 0:NH * P], psT[0:NC, 0:NH * P], ACT.Copy).then_inc(probsT_ready, 1)
                else:
                    w = heads * P * (keys // P)
                    act.activation(probsT[:, 0:w], psT[:, 0:w], ACT.Copy).then_inc(probsT_ready, 1)

            act.wait_ge(x_in, 16)
            act.activation(o_hi[:], xT[:], ACT.Copy).then_inc(split_hi, 1)
            for n in range(DEPTH):
                split(n)
            act.wait_ge(lb_max, 1)
            act.activation(lb[:, 2:4, :], lb[:, 2:4, :], ACT.Exp).then_inc(lb_exp, 1)
            for what, i in ORDER:
                if what == "gemm":
                    if i + DEPTH < N1:
                        split(i + DEPTH)
                    else:
                        split_table(i + DEPTH, i + DEPTH - N1, 16 * ((i + DEPTH - N1) // 2 + 1))
                    take(i)
                    if i == AT["hq"]:
                        act.wait_ge(mem_in, 16)
                        act.activation(b_hi[:], memT[:], ACT.Copy).then_inc(split_hi, 1)
                elif what == "gelu":
                    act.wait_ge(hidden_done, 1)
                    act.activation(hx[:], psM[:, 0:2 * G * NC], ACT.Copy).then_inc(hidden_out, 1)
                    act.wait_ge(hidden_out, 2)
                    act.activation(hy[:], hy[:], ACT.Tanh, scale=(2 / np.pi) ** 0.5).then_inc(tanh_done, 1)
                elif what == "compressed":
                    act.wait_ge(cmp_done, 1)
                    act.activation(kcmp[:], psM[:, 128:128 + NC], ACT.Copy)
                    act.activation(vcmp[:], psM[0:NC, 256:256 + P], ACT.Copy).then_inc(cmp_out, 1)
                elif what == "scores":
                    exp_unit(i)
                elif what == "turn_probs":
                    take_probsT(i)
                elif what == "level" and i == 8:
                    act.wait_ge(level_done, 9)
                    act.activation(att_off[:], psS[:, 0:HH * P], ACT.Copy).then_inc(off_ready, 1)
                elif what == "read_out":
                    act.wait_ge(read_done, i + 1)
                    act.activation(oh[:, i, :], psO[:, i * 512:(i + 1) * 512], ACT.Copy).then_inc(read_out_ready, 1)
                elif what == "rms":
                    act.wait_ge(var_ready, 1)
                    act.activation(std[:], std[:], ACT.Sqrt).then_inc(std_ready, 1)
                elif what == "norm":
                    w, t = i
                    act.wait_ge(var_ready, 2 + w * NT + t)
                    act.activation(std[:, t, 0:1], mv[:, t, 1:2], ACT.Sqrt).then_inc(std_ready, 1)
                elif what == "turn":
                    t = i % 2
                    dst = o_hi if i // 2 % 2 == 0 else b_hi
                    act.wait_ge(turn_done, i + 1)
                    act.activation(dst[:, :, t * P:(t + 1) * P],
                                   (psS, psT)[t][:].rearrange("p (k c) -> p k c", c=P), ACT.Copy).then_inc(turn_hi, 1)
            for u in range(PH * NT):
                act.wait_ge(score_done, u + 1)
                act.activation(route_s[:, u, :], (psO, psS)[u % 4 // 2][:, u % 2 * 512:u % 2 * 512 + S], ACT.Copy).then_inc(score_out, 1)
            def activations(it):
                for i in range(8):
                    j = it * 8 + i
                    split_table(j + (N1 + DEPTH), i + DEPTH, it * 64 + 16 * ((i + DEPTH) // 2 + 1))
                    act.activation(H[:, bass.ds(j, 1), :].rearrange("p a t -> p (a t)"), psG[i % 2][:, 0:S],
                                   ACT.Gelu).then_inc(h_out, 1)
            with act.Fori(0, E_TILES // 8 - 2) as it:
                activations(it)
            with act.Fori(E_TILES // 8 - 2, E_TILES // 8) as it:
                act.wait_ge(routed, it)
                activations(it)
            act.wait_ge(shifted, 1)
            act.activation(chosen_s[:], chosen_s[:], ACT.Exp).then_inc(gate_exp, 1)
            for q in range(3):
                act.wait_ge(index_done, 3)
                dst = (igT[:, :, 0], i2T[:], igT[:, :, 1])[q]
                act.activation(dst, psO[:, q * S:(q + 1) * S], ACT.Copy).then_inc(index_out, 1)

            def round_act(j, slot, first=False):
                if not first:
                    act.wait_ge(tile_used, j + (N1 + E_TILES - 3))
                act.activation(a_hi[slot][:], H[:, bass.ds(j, 1), :].rearrange("p a t -> p (a t)"), ACT.Copy)\
                    .then_inc(act_hi, 1)
            act.wait_ge(gated, S // 4)
            for i in range(4):
                round_act(i, i, True)
            with act.Fori(0, E_TILES // 4 - 1) as it:
                for i in range(4):
                    round_act(it * 4 + (i + 4), i)
                    split_table(it * 4 + (N1 + E_TILES + 4 + i), i, it * 32 + 16 * (E_TILES // 2 + (i + 4) // 2 + 1))
            for t in range(NT):
                act.wait_ge(var_ready, 2 + 2 * NT + t)
                act.activation(std2[:, t, 0:1], mv2[:, t, 1:2], ACT.Sqrt).then_inc(std_ready, 1)

        @block.vector
        def _(dve):
            step = Steps(dve, dve_step)

            def rest(n):
                dve.wait_ge(hi_done, n + 1)
                if n >= DEPTH:
                    dve.wait_ge(tile_used, n - DEPTH + 1)
                src = raw[n % 4] if n < N1 else raw[(n - N1) % 2]
                dve.tensor_tensor(lo[n % DEPTH][:], src[:], hi[n % DEPTH][:].bitcast(FP32), ALU.subtract)\
                    .then_inc(lo_done, 1)

            def rest_table(n, i):
                dve.wait_ge(hi_done, n + 1)
                dve.wait_ge(tile_used, n - DEPTH + 1)
                s = (N1 + i) % DEPTH
                dve.tensor_tensor(lo[s][:], raw[i % 2][:], hi[s][:].bitcast(FP32), ALU.subtract)\
                    .then_inc(lo_done, 1)

            def add_residual(n):
                name, kind, i, k0, m, cols, first, last, use = TILES[n]
                if not last:
                    return
                src, dst = (x_tok, x1) if name == "wo" else (x1, x2)
                if name == "wo" and i == 0:
                    dve.wait_ge(xtok_in, 16)
                dve.wait_ge(tile_used, n + 1)
                for t in range(NT):
                    z = dst[:, t, i * 512:(i + 1) * 512]
                    dve.scalar_tensor_tensor(out=z, in0=src[:, t, i * 512:(i + 1) * 512], scalar=ALPHA,
                                             in1=psG[(use + t) % 2][:], op0=ALU.mult, op1=ALU.add)\
                        .then_inc(dve_took, 1)
                    dve.wait_ge(dve_took, TAKEN[use + t][1])
                    step(dve.bn_stats(stats[:, t, i, :], z))

            def variance(t, st, m):
                dve.bn_aggr(m[:, t, :], st[:, t, :, :].rearrange("p c s -> p (c s)")).then_inc(dve_step, 1)
                step.count += 1
                step.wait()
                dve.tensor_scalar(m[:, t, 1:2], m[:, t, 1:2], EPS, None, ALU.add).then_inc(var_ready, 1)

            def normalize(w, t, z, m, sd, rs, gb):
                dve.wait_ge(std_ready, 2 + w * NT + t)
                step(dve.reciprocal(rs[:, t, 0:1], sd[:, t, 0:1]))
                step.wait()
                step(dve.tensor_scalar(z, z, m[:, t, 0:1], rs[:, t, 0:1], ALU.subtract, ALU.mult))
                step.wait()
                dve.wait_ge(ln_in, 32 * (w + 1))
                step(dve.tensor_tensor(z, z, gb[:, 0, :], ALU.mult))
                step.wait()
                dve.tensor_tensor(z, z, gb[:, 1, :], ALU.add).then_inc(norm_ready, 1)

            def max_unit(u):
                b, g, t, heads, keys = unit(u)
                dve.wait_ge(s_done, u + 1)
                if b == 2:
                    for gg in range(G):
                        step(dve.scalar_tensor_tensor(
                            out=cmp_s[:, gg * REP:(gg + 1) * REP, :],
                            in0=psS[:, gg * 512:gg * 512 + REP * 16].rearrange("p (h n) -> p h n", n=16)[:, :, 0:NC],
                            scalar=HD ** -0.5, in1=cmp_mask[:, t, :].unsqueeze(1).broadcast_to([P, REP, NC]),
                            op0=ALU.mult, op1=ALU.add))
                    step.wait()
                    step(dve.tensor_reduce(row_max[:], cmp_s[:], AX.X, ALU.max))
                    step.wait()
                    dve.tensor_tensor(cmp_s[:], cmp_s[:], row_max[:].unsqueeze(2).broadcast_to([P, NH, NC]),
                                      ALU.subtract).then_inc(max_done, 1)
                    return
                scale = HD ** -0.5 if b < 2 else (D // XH) ** -0.5
                step(dve.tensor_reduce(row_max[:, 0:heads],
                                       psS[:].rearrange("p (h n) -> p h n", n=S)[:, :, 0:keys], AX.X, ALU.max))
                step.wait()
                dve.tensor_scalar(neg_max[:, u % 2, 0:heads], row_max[:, 0:heads], -scale, None, ALU.mult)\
                    .then_inc(max_done, 1)

            def combine(u):
                b, g, t, heads, keys = unit(u)
                dve.wait_ge(exp_done, u + 1)
                if u:
                    dve.wait_ge(combined, u)
                sums = row_sum[:, u % 2, 0:heads]
                if b == 2:
                    step(dve.tensor_reduce(sums, probs[:, 0:NH * NC].rearrange("p (h n) -> p h n", n=NC),
                                           AX.X, ALU.add))
                    step.wait()
                step(dve.reciprocal(coef[:, 0:heads], sums))
                step.wait()
                if b < 3:
                    col = {0: 1, 1: 2, 2: 0}[b]
                    gates = gate[:, t, :].rearrange("p (h c) -> p h c", c=3)[:, g * REP:g * REP + heads, col]
                    step(dve.tensor_tensor(coef[:, 0:heads], coef[:, 0:heads], gates, ALU.mult))
                    step.wait()
                if b == 2:
                    step(dve.tensor_scalar(coef[:], coef[:], cmp_any[:, t:t + 1], None, ALU.mult))
                    step.wait()
                dve.wait_ge(pv_done, u + 1)
                width = HD if b < 3 else D // XH
                src = psO[:, 0:heads * width].rearrange("p (h d) -> p h d", d=width)
                by = coef[:, 0:heads].unsqueeze(2).broadcast_to([P, heads, width])
                if b == 3:
                    dve.tensor_tensor(xo[:, t, :].rearrange("p (h d) -> p h d", d=width), src, by, ALU.mult)\
                        .then_inc(combined, 1)
                    return
                dst = o_acc[:, t, g * 256:g * 256 + heads * HD].rearrange("p (h d) -> p h d", d=HD)
                if b == 0:
                    dve.tensor_tensor(dst, src, by, ALU.mult).then_inc(combined, 1)
                    return
                tmp = o_tmp[:, 0:heads * HD].rearrange("p (h d) -> p h d", d=HD)
                step(dve.tensor_tensor(tmp, src, by, ALU.mult))
                step.wait()
                dve.tensor_tensor(dst, dst, tmp, ALU.add).then_inc(combined, 1)

            def lower_bound():
                dve.wait_ge(rec_in, 32)
                step(dve.tensor_tensor(lb[:, 4, :], lb[:, 0, :], lb[:, 1, :], ALU.max))
                step.wait()
                dve.tensor_tensor(lb[:, 2:4, :], lb[:, 0:2, :], lb[:, 4, :].unsqueeze(1).broadcast_to([P, 2, HH]),
                                  ALU.subtract).then_inc(lb_max, 1)
                dve.wait_ge(lb_exp, 1)
                step(dve.tensor_tensor(lb[:, 4, :], lb[:, 2, :], lb[:, 3, :], ALU.add))
                step.wait()
                step(dve.reciprocal(lb[:, 5, :], lb[:, 4, :]))
                step.wait()
                step(dve.tensor_tensor(lb[:, 6, :], lb[:, 2, :], lb[:, 5, :], ALU.mult))
                step.wait()
                step(dve.tensor_scalar(lb[:, 5, :], lb[:, 6, :], -0.5, 0.5, ALU.mult, ALU.add))
                step.wait()
                step(dve.tensor_tensor(lb[:, 7, :], lb[:, 6, :], lb[:, 5, :], ALU.add))
                step.wait()

            dve.wait_ge(split_hi, 1)
            dve.tensor_tensor(o_lo[:], xT[:], o_hi[:].bitcast(FP32), ALU.subtract).then_inc(split_lo, 1)
            for n in range(DEPTH):
                rest(n)
            lower_bound()
            for what, i in ORDER:
                if what == "gemm":
                    rest(i + DEPTH)
                    if TILES[i][0] in VECTOR_READS:
                        add_residual(i)
                    if i == AT["hq"]:
                        dve.wait_ge(split_hi, 2)
                        dve.tensor_tensor(b_lo[:], memT[:], b_hi[:].bitcast(FP32), ALU.subtract)\
                            .then_inc(split_lo, 1)
                        dve.wait_ge(act_took, TAKEN[TILES[AT["vg"]][8] + 1][1])
                        step(dve.tensor_scalar(gate[:], vg[:, :, 2 * P:VG], 1.0, 0.5, ALU.add, ALU.mult))
                    if i == AT["mk"]:
                        dve.wait_ge(act_took, TAKEN[TILES[AT["hg"]][8] + 1][1])
                        step(dve.tensor_scalar(hg_t[:], hg_t[:], 1.0, 0.5, ALU.add, ALU.mult))
                        step(dve.tensor_tensor(hg[:], hg[:], norm_w[:].unsqueeze(1).broadcast_to([P, NT, 512]),
                                               ALU.mult))
                        step.wait()
                        step(dve.tensor_tensor(hg[:], hg[:], hg_t[:], ALU.mult))
                elif what == "blocks":
                    dve.wait_ge(shift_in, 16 * 4)
                    dve.wait_ge(comp_in, 48)
                    for kv in range(2):
                        for g in range(G):
                            src = kcp[:, kv, g, :]
                            src = bass.AP(tensor=src.tensor, offset=src.offset,
                                          ap=[list(src.ap[0]), [2, CB // 2], [CS, NC]])
                            last = dve.tensor_tensor(blk[:, kv, :, g * NC:(g + 1) * NC], src,
                                                     pos[:, kv, :].unsqueeze(2).broadcast_to([P, CB // 2, NC]),
                                                     ALU.add)
                    last.then_inc(blocks_ready, 1)
                elif what == "gelu":
                    dve.wait_ge(hidden_out, 1)
                    step(dve.tensor_tensor(hy[:], hx[:], hx[:], ALU.mult))
                    step.wait()
                    step(dve.tensor_tensor(hy[:], hy[:], hx[:], ALU.mult))
                    step.wait()
                    dve.scalar_tensor_tensor(out=hy[:], in0=hy[:], scalar=0.044715, in1=hx[:],
                                             op0=ALU.mult, op1=ALU.add).then_inc(hidden_out, 1)
                    dve.wait_ge(tanh_done, 1)
                    step(dve.tensor_scalar(hz[:], hy[:], 1.0, 0.5, ALU.add, ALU.mult))
                    step.wait()
                    dve.tensor_tensor(hz[:], hz[:], hx[:], ALU.mult).then_inc(gelu_ready, 1)
                elif what == "scores":
                    max_unit(i)
                elif what == "values":
                    combine(i)
                elif what == "decay":
                    dve.wait_ge(act_took, TAKEN[TILES[AT["hf"] + HH - 1][8]][1])
                    for h in range(HH):
                        step(dve.tensor_scalar(Fa[:, h * S:(h + 1) * S], Fa[:, h * S:(h + 1) * S], lb[:, 5, h:h + 1],
                                               lb[:, 7, h:h + 1], ALU.mult, ALU.add))
                    step.wait()
                    step(dve.tensor_scalar(KB[:].rearrange("p h t -> p (h t)"), Fa[:], -1.0, 1.0, ALU.mult, ALU.add))
                    dve.tensor_tensor(QF[:].rearrange("p h t -> p (h t)"), Fa[:],
                                      hq[:].rearrange("p h t -> p (h t)"), ALU.mult).then_inc(decay_ready, 1)
                    step.wait()
                elif what == "level":
                    if 1 <= i <= 7:
                        L = 1 << (i - 1)
                        n = HH * S // (2 * L)
                        F, F2 = (Fa, Fb) if i % 2 else (Fb, Fa)
                        fe = F[:, 0:2 * n].rearrange("p (n b) -> p n b", b=2)
                        dve.wait_ge(level_done, i + 1)
                        if i == 1:
                            dve.wait_ge(decay_ready, 1)
                        q2 = QF[:].rearrange("p h t -> p (h t)").rearrange("p (n b l) -> p n b l", b=2, l=L)[:, :, 1, :]
                        k2 = KB[:].rearrange("p h t -> p (h t)").rearrange("p (n b l) -> p n b l", b=2, l=L)[:, :, 0, :]
                        dve.tensor_tensor(q2, q2, fe[:, :, 0].unsqueeze(2).broadcast_to([P, n, L]), ALU.mult)
                        dve.tensor_tensor(k2, k2, fe[:, :, 1].unsqueeze(2).broadcast_to([P, n, L]), ALU.mult)
                        dve.tensor_tensor(F2[:, 0:n], fe[:, :, 0], fe[:, :, 1], ALU.mult).then_inc(factors_ready, 1)
                    if i <= 7:
                        dve.wait_ge(level_done, i + 1)
                        if i == 0:
                            dve.wait_ge(att_zero, 1)
                            dve.wait_ge(mask_in, 16)
                        else:
                            dve.wait_ge(level_merged, i)
                        X = (psS, psT)[i % 2]
                        dve.copy_predicated(att[:].rearrange("p h b t -> p (h b) t"),
                                            level_mask[:, i, :].bitcast(U16).unsqueeze(1).broadcast_to([P, HH * NT, P]),
                                            X[:].rearrange("p (n t) -> p n t", t=P)).then_inc(level_merged, 1)
                        if 1 <= i <= 7:
                            dve.wait_ge(factors_ready, i)
                elif what == "rms":
                    dve.wait_ge(read_out_ready, NT)
                    t3 = probs[:].rearrange("p (n e) -> p n e", e=P)
                    o3 = oh[:].rearrange("p t (h e) -> p (t h) e", e=P)
                    step(dve.tensor_tensor(t3, o3, o3, ALU.mult))
                    step.wait()
                    sd = std[:].rearrange("p t h -> p (t h)")
                    step(dve.tensor_reduce(sd, t3, AX.X, ALU.add))
                    step.wait()
                    dve.tensor_scalar(sd, sd, 1.0 / P, EPS, ALU.mult, ALU.add).then_inc(var_ready, 1)
                    dve.wait_ge(std_ready, 1)
                    rs = rstd[:].rearrange("p t h -> p (t h)")
                    step(dve.reciprocal(rs, sd))
                    step.wait()
                    step(dve.tensor_tensor(o3, o3, rs.unsqueeze(2).broadcast_to([P, NT * HH, P]), ALU.mult))
                    step.wait()
                    dve.tensor_tensor(oh[:], oh[:], hg[:], ALU.mult).then_inc(rec_ready, 1)
                elif what == "turn":
                    t = i % 2
                    dst, rounded = (o_lo, o_hi) if i // 2 % 2 == 0 else (b_lo, b_hi)
                    dve.wait_ge(turn_hi, i + 1)
                    dve.tensor_tensor(dst[:, :, t * P:(t + 1) * P],
                                      (psS, psT)[t][:].rearrange("p (k c) -> p k c", c=P),
                                      rounded[:, :, t * P:(t + 1) * P].bitcast(FP32), ALU.subtract)\
                        .then_inc(turn_lo, 1)
                elif what == "norm":
                    w, t = i
                    step.wait()
                    variance(t, stats, mv)
                    normalize(w, t, (x1, x2)[w][:, t, :], mv, std, rstd, ln_gb)

            LOWEST = -3.0e38
            PER = 27
            dve.wait_ge(subk_in, 32)
            dve.wait_ge(score_out, PH * NT)
            step(dve.memset(hold_v[:], 0.0))
            step.wait()
            c0 = step.count
            with dve.Fori(0, E_TILES // 8) as it:
                mark = {"n": 0}

                def did(instruction):
                    instruction.then_inc(dve_step, 1)
                    mark["n"] += 1

                def mine():
                    dve.wait_ge(dve_step, it * PER + (c0 + mark["n"]))
                    dve.tensor_copy(hold_v[:, 0:1], hold_v[:, 1:2])

                def ahead(i):
                    rest_table(it * 8 + (N1 + DEPTH + i), i + DEPTH)

                def best(values, spare, out_v, out_i):
                    did(dve.max(out_v[:, 0:8], values))
                    mine()
                    did(dve.max_index(out_i[:, 0:8], out_v[:, 0:8], values))
                    did(dve.match_replace(spare, out_v[:, 0:8], values, LOWEST))
                    mine()
                    did(dve.max(out_v[:, 8:16], spare))
                    mine()
                    did(dve.max_index(out_i[:, 8:16], out_v[:, 8:16], spare))

                ahead(0)
                did(dve.tensor_copy(unit_s[:].rearrange("p c n -> p (c n)"),
                                    route_s[:, bass.ds(it, 1), :].rearrange("p a n -> p (a n)")))
                mine()
                best(unit_s[:, 0, :], unit_w[:, 0, :], unit_m[:, 0, :], unit_i[:, 0, :])
                ahead(1)
                best(unit_s[:, 1, :], unit_w[:, 1, :], unit_m[:, 1, :], unit_i[:, 1, :])
                mine()
                did(dve.tensor_copy(unit_if[:], unit_i[:]))
                ahead(2)
                cand = unit_c[:, 0, :, :]
                did(dve.tensor_tensor(cand, unit_m[:, 0, :].unsqueeze(2).broadcast_to([P, TOPK, TOPK]),
                                      unit_m[:, 1, :].unsqueeze(1).broadcast_to([P, TOPK, TOPK]), ALU.add))
                mine()
                best(cand.rearrange("p a b -> p (a b)"), unit_w[:].rearrange("p c n -> p (c n)"),
                     unit_t[:], unit_p[:])
                ahead(3)
                mine()
                did(dve.tensor_copy(chosen_s[:, bass.ds(it, 1), :].rearrange("p a k -> p (a k)"), unit_t[:]))
                did(dve.tensor_scalar(unit_ab[:, 0, :], unit_p[:], 4, None, ALU.logical_shift_right))
                did(dve.tensor_scalar(unit_ab[:, 1, :], unit_p[:], 15, None, ALU.bitwise_and))
                mine()
                did(dve.tensor_copy(unit_abf[:], unit_ab[:]))
                mine()
                ahead(4)
                did(dve.tensor_tensor(unit_c[:].rearrange("p c k a -> p (c k) a"),
                                      iota16[:].unsqueeze(1).broadcast_to([P, 2 * TOPK, TOPK]),
                                      unit_abf[:].rearrange("p c k -> p (c k)").unsqueeze(2)
                                      .broadcast_to([P, 2 * TOPK, TOPK]), ALU.is_equal))
                mine()
                ahead(5)
                for c in range(2):
                    did(dve.tensor_tensor(unit_c[:, c, :, :], unit_c[:, c, :, :],
                                          unit_if[:, c, :].unsqueeze(1).broadcast_to([P, TOPK, TOPK]), ALU.mult))
                mine()
                ahead(6)
                did(dve.tensor_reduce(chosen[:, 0, bass.ds(it, 1), :].rearrange("p a k -> p (a k)"),
                                      unit_c[:, 0, :, :], AX.X, ALU.add))
                did(dve.tensor_reduce(chosen[:, 1, bass.ds(it, 1), :].rearrange("p a k -> p (a k)"),
                                      unit_c[:, 1, :, :], AX.X, ALU.add))
                mine()
                assert mark["n"] == PER, mark
                dve.tensor_copy(unit_t[:, 0:1], unit_t[:, 1:2]).then_inc(routed, 1)
                ahead(7)
            step.count = c0 + PER * (E_TILES // 8)

            dve.wait_ge(routed, E_TILES // 8)
            step(dve.tensor_copy(gate_z[:], chosen_s[:, :, 0]))
            step.wait()
            dve.tensor_tensor(chosen_s[:], chosen_s[:], gate_z[:].unsqueeze(2).broadcast_to([P, PH * NT, TOPK]),
                              ALU.subtract).then_inc(shifted, 1)
            dve.wait_ge(gate_exp, 1)
            step(dve.tensor_reduce(gate_z[:], chosen_s[:], AX.X, ALU.add))
            step.wait()
            step(dve.reciprocal(gate_z[:], gate_z[:]))
            step.wait()
            dve.tensor_tensor(chosen_s[:], chosen_s[:], gate_z[:].unsqueeze(2).broadcast_to([P, PH * NT, TOPK]),
                              ALU.mult).then_inc(gate_ready, 1)

            def one_hot(g, slot, first):
                if not first:
                    dve.wait_ge(gates_done, g - 1)
                for i in range(4):
                    last = dve.tensor_scalar(one2[slot][:, i, :], iota[:], i2T[:, bass.ds(g * 4 + i, 1)], None,
                                             ALU.is_equal)
                last.then_inc(one2_ready, 1)

            def apply_gates(g, slot):
                dve.wait_ge(gates_done, g + 1)
                h = H[:, :, bass.ds(g * 4, 4)].rearrange("p j t -> p t j")
                dve.tensor_tensor(h, psG[slot][:].rearrange("p (t j) -> p t j", j=NK), h, ALU.mult)\
                    .then_inc(gated, 1)
            dve.wait_ge(index_out, 3)
            one_hot(0, 0, True)
            one_hot(1, 1, True)
            apply_gates(0, 0)
            with dve.Fori(0, S // 8 - 1) as it:
                for i in range(2):
                    one_hot(it * 2 + (2 + i), i, False)
                    apply_gates(it * 2 + (1 + i), 1 - i)
            apply_gates(S // 4 - 1, 1)

            def rest_act(j, slot, first=False):
                dve.wait_ge(act_hi, j + 1)
                if not first:
                    dve.wait_ge(tile_used, j + (N1 + E_TILES - 3))
                dve.tensor_tensor(a_lo[slot][:], H[:, bass.ds(j, 1), :].rearrange("p a t -> p (a t)"),
                                  a_hi[slot][:].bitcast(FP32), ALU.subtract).then_inc(act_lo, 1)
            for i in range(4):
                rest_act(i, i, True)
            with dve.Fori(0, E_TILES // 4 - 1) as it:
                for i in range(4):
                    rest_act(it * 4 + (i + 4), i)
                    rest_table(it * 4 + (N1 + E_TILES + 4 + i), i)
            dve.wait_ge(tile_used, N1 + 2 * E_TILES)
            for t in range(NT):
                for c in range(2):
                    z = x2[:, t, c * 512:(c + 1) * 512]
                    step(dve.scalar_tensor_tensor(out=z, in0=z, scalar=ALPHA,
                                                  in1=(psS, psT)[t][:, c * 512:(c + 1) * 512],
                                                  op0=ALU.mult, op1=ALU.add))
                    step.wait()
                    step(dve.bn_stats(stats2[:, t, c, :], z))
                step.wait()
                variance(t, stats2, mv2)
                normalize(2, t, x2[:, t, :], mv2, std2, rstd2, ln_last)

        @block.tensor
        def _(pe):
            def three(out, hi_l, lo_l, hi_r, lo_r, start, stop):
                pe.matmul(out, hi_l, hi_r, start=start, stop=False)
                pe.matmul(out, hi_l, lo_r, start=False, stop=False)
                return pe.matmul(out, lo_l, hi_r, start=False, stop=stop)

            def gemm(n):
                name, kind, i, k0, m, cols, first, last, use = TILES[n]
                act_hi_t, act_lo_t = (b_hi, b_lo) if name in ("mk", "mv", "xq", "pq") else (o_hi, o_lo)
                pe.wait_ge(lo_done, n + 1)
                if name == "mk" and i == 0:
                    pe.wait_ge(split_lo, 2)
                if name in ("wo", "xq", "xo", "pq") and i == 0 and k0 == 0:
                    pe.wait_ge(turn_lo, 2 * (1 + ("wo", "xq", "xo", "pq").index(name)))
                if first:
                    for u in range(use, use + (1 if kind == "T" else NT)):
                        if u >= 2:
                            v, count = TAKEN[u - 2]
                            pe.wait_ge(took[v], count)
                s = n % DEPTH
                if kind == "T":
                    wh = hi[s][:].rearrange("p (k c) -> p k c", c=P)
                    wl = lo[s][:].rearrange("p (k c) -> p k c", c=P)
                    for k in range(KD):
                        mm = three(psG[use % 2][:, 0:S], wh[:, k, :], wl[:, k, :], act_hi_t[:, k, :],
                                   act_lo_t[:, k, :], k == 0, k == KD - 1)
                else:
                    for t in range(NT):
                        for kk in range(m):
                            cut = slice(kk * cols, (kk + 1) * cols)
                            k = k0 + kk
                            mm = three(psG[(use + t) % 2][:, 0:cols], act_hi_t[:, k, t * P:(t + 1) * P],
                                       act_lo_t[:, k, t * P:(t + 1) * P], hi[s][:, cut], lo[s][:, cut],
                                       k == 0, k == KD - 1)
                mm.then_inc(tile_used, 1)

            def scores(u):
                b, g, t, heads, keys = unit(u)
                if u == 0:
                    pe.wait_ge(const_in, 16 * 6)
                    pe.wait_ge(act_took, TAKEN[TILES[AT["vg"]][8] + 1][1])
                if b == 2:
                    pe.wait_ge(cmp_out, 1)
                    pe.wait_ge(exp_done, u)
                    for h in range(NH):
                        at = h // REP * HD
                        col = h // REP * 512 + h % REP * 16
                        mm = pe.matmul(psS[:, col:col + NC], qT[at:at + HD, h % REP, t * P:(t + 1) * P],
                                       kcmp[at:at + HD, :], start=True, stop=True)
                    mm.then_inc(s_done, 1)
                    return
                if u:
                    pe.wait_ge(exp_done, u)
                if b == 3:
                    if u == XU:
                        pe.wait_ge(turn_lo, 4)
                        pe.wait_ge(act_took, TAKEN[TILES[AT["xq"] + KD - 1][8]][1])
                    for h in range(XH):
                        for kk in range(2):
                            mm = pe.matmul(psS[:, h * S:(h + 1) * S], xq[:, 2 * h + kk, t * P:(t + 1) * P],
                                           xk[:, 2 * h + kk, :], start=kk == 0, stop=kk == 1)
                    mm.then_inc(s_done, 1)
                    return
                for r in range(REP):
                    for kb in range(t + 1):
                        out = psS[:, r * S + kb * P:r * S + (kb + 1) * P]
                        diagonal = kb == t
                        mm = pe.matmul(out, qT[g * HD:(g + 1) * HD, r, t * P:(t + 1) * P],
                                       kT[b][g * HD:(g + 1) * HD, kb * P:(kb + 1) * P], start=True, stop=not diagonal)
                        if diagonal:
                            mm = pe.matmul(out, identb[:], causal[:], start=False, stop=True)
                mm.then_inc(s_done, 1)

            def turn_probs(u):
                b, g, t, heads, keys = unit(u)
                pe.wait_ge(exp_done, u + 1)
                if u:
                    pe.wait_ge(probsT_ready, u)
                if u == XU:
                    pe.wait_ge(turn_lo, 4)
                if b == 2:
                    for h in range(NH):
                        mm = pe.transpose(psT[0:NC, h * P:(h + 1) * P], probs[:, h * NC:(h + 1) * NC], ident[:])
                else:
                    kbs = keys // P
                    for r in range(heads):
                        for kb in range(kbs):
                            at = (r * kbs + kb) * P
                            mm = pe.transpose(psT[:, at:at + P], probs[:, r * S + kb * P:r * S + (kb + 1) * P],
                                              ident[:])
                mm.then_inc(turned, 1)

            def values(u):
                b, g, t, heads, keys = unit(u)
                pe.wait_ge(probsT_ready, u + 1)
                if u:
                    pe.wait_ge(combined, u)
                if u == XU:
                    pe.wait_ge(read_out_ready, NT)
                if b == 2:
                    for h in range(NH):
                        gg = h // REP
                        mm = pe.matmul(psO[:, h * HD:(h + 1) * HD], probsT[0:NC, h * P:(h + 1) * P],
                                       vcmp[:, gg * HD:(gg + 1) * HD], start=True, stop=True)
                elif b == 3:
                    for h in range(XH):
                        for kb in range(2):
                            mm = pe.matmul(psO[:, h * 256:(h + 1) * 256],
                                           probsT[:, (h * 2 + kb) * P:(h * 2 + kb + 1) * P],
                                           xv[:, kb, h * 256:(h + 1) * 256], start=kb == 0, stop=kb == 1)
                else:
                    for r in range(REP):
                        for kb in range(t + 1):
                            at = (r * (t + 1) + kb) * P
                            mm = pe.matmul(psO[:, r * HD:(r + 1) * HD], probsT[:, at:at + P],
                                           vg[:, kb, b * P + g * HD:b * P + (g + 1) * HD],
                                           start=kb == 0, stop=kb == t)
                mm.then_inc(pv_done, 1)

            pe.wait_ge(split_lo, 1)
            for what, i in ORDER:
                if what == "gemm":
                    gemm(i)
                elif what == "hidden":
                    pe.wait_ge(blocks_ready, 1)
                    for kv in range(2):
                        for m in range(CB // 2):
                            mm = pe.matmul(psM[:, kv * G * NC:(kv + 1) * G * NC], w1[:, kv, m, :], blk[:, kv, m, :],
                                           start=m == 0, stop=m == CB // 2 - 1)
                    mm.then_inc(hidden_done, 1)
                elif what == "compressed":
                    pe.wait_ge(gelu_ready, 1)
                    for g in range(G):
                        pe.matmul(psM[g * HD:(g + 1) * HD, 128:128 + NC], w2[:, 0, :],
                                  hz[:, g * NC:(g + 1) * NC], start=True, stop=True)
                    for g in range(G):
                        mm = pe.matmul(psM[0:NC, 256 + g * HD:256 + (g + 1) * HD],
                                       hz[:, (G + g) * NC:(G + g + 1) * NC], w2[:, 1, :], start=True, stop=True)
                    mm.then_inc(cmp_done, 1)
                elif what == "scores":
                    scores(i)
                elif what == "turn_probs":
                    turn_probs(i)
                elif what == "values":
                    values(i)
                elif what == "level":
                    if i == 0:
                        pe.wait_ge(decay_ready, 1)
                        pe.wait_ge(exp_done, XU)
                        pe.wait_ge(probsT_ready, XU)
                    if i >= 2:
                        pe.wait_ge(factors_ready, i - 1)
                        pe.wait_ge(level_merged, i - 1)
                    X = (psS, psT)[i % 2]
                    if i == 8:
                        for h in range(HH):
                            mm = pe.matmul(X[:, h * P:(h + 1) * P], KB[:, h, 0:P], QF[:, h, P:S], start=True, stop=True)
                    else:
                        q = hq if i == 0 else QF
                        for h in range(HH):
                            for t in range(NT):
                                at = (h * NT + t) * P
                                mm = pe.matmul(X[:, at:at + P], KB[:, h, t * P:(t + 1) * P],
                                               q[:, h, t * P:(t + 1) * P], start=True, stop=True)
                    mm.then_inc(level_done, 1)
                elif what == "read_out":
                    pe.wait_ge(level_merged, 8)
                    pe.wait_ge(off_ready, 1)
                    pe.wait_ge(combined, XU)
                    for h in range(HH):
                        out = psO[:, i * 512 + h * P:i * 512 + (h + 1) * P]
                        mm = pe.matmul(out, att[:, h, i, :], hv[:, i, h * P:(h + 1) * P], start=True, stop=i == 0)
                        if i == 1:
                            mm = pe.matmul(out, att_off[:, h, :], hv[:, 0, h * P:(h + 1) * P], start=False, stop=True)
                    mm.then_inc(read_done, 1)
                elif what == "turn":
                    t = i % 2
                    if i == 0:
                        pe.wait_ge(rec_ready, 1)
                    elif i in (2, 3):
                        pe.wait_ge(norm_ready, i - 1)
                        pe.wait_ge(turn_lo, i - 1)
                    elif i in (4, 5):
                        pe.wait_ge(combined, XU + i - 3)
                        pe.wait_ge(exp_done, XU + NT)
                        pe.wait_ge(probsT_ready, XU + NT)
                    elif i in (6, 7):
                        pe.wait_ge(norm_ready, i - 3)
                        pe.wait_ge(turn_lo, i - 1)
                    for k in range(KD):
                        if i < 2:
                            src = (o_acc if k < 4 else oh)[:, t, k % 4 * P:(k % 4 + 1) * P]
                        else:
                            src = (x1, xo, x2)[i // 2 - 1][:, t, k * P:(k + 1) * P]
                        mm = pe.transpose((psS, psT)[t][:, k * P:(k + 1) * P], src, ident[:])
                    mm.then_inc(turn_done, 1)
            pe.wait_ge(subk_in, 32)
            pe.wait_ge(act_took, TAKEN_ALL[0])
            pe.wait_ge(combined, XU + NT)
            for u in range(PH * NT):
                t, h = u // PH, u % PH
                if u >= 4:
                    pe.wait_ge(score_out, u - 3)
                mm = pe.matmul((psO, psS)[u % 4 // 2][:, u % 2 * 512:u % 2 * 512 + S], qryT[:, h, t * P:(t + 1) * P], subk[:, h, :],
                               start=True, stop=True)
                mm.then_inc(score_done, 1)

            def down(j, i, first):
                n = j + N1
                s = (N1 + i) % DEPTH
                pe.wait_ge(lo_done, n + 1)
                if not first:
                    pe.wait_ge(h_out, j - 1)
                wh = hi[s][:].rearrange("p (k c) -> p k c", c=P)
                wl = lo[s][:].rearrange("p (k c) -> p k c", c=P)
                for k in range(KD):
                    mm = three(psG[i % 2][:, 0:S], wh[:, k, :], wl[:, k, :], b_hi[:, k, :], b_lo[:, k, :],
                               k == 0, k == KD - 1)
                mm.then_inc(tile_used, 1)
            for j in range(4):
                down(j, j, j < 2)
            with pe.Fori(1, E_TILES // 4) as it:
                for i in range(4):
                    down(it * 4 + i, i, False)

            pe.wait_ge(gate_ready, 1)
            pe.wait_ge(score_out, PH * NT)
            for q in range(3):
                for t in range(NT):
                    src = (chosen[:, 0], chosen[:, 1], chosen_s[:])[q]
                    mm = pe.transpose(psO[:, q * S + t * P:q * S + (t + 1) * P],
                                      src[:, t * PH:(t + 1) * PH, :].rearrange("p h k -> p (h k)"), ident[:])
                mm.then_inc(index_done, 1)

            def gates(g, slot, first):
                pe.wait_ge(one2_ready, g + 1)
                pe.wait_ge(one1_ready, g + 1)
                if not first:
                    pe.wait_ge(gated, g - 1)
                for i in range(4):
                    mm = pe.matmul(psG[slot][:, i * NK:(i + 1) * NK], one2[slot][:, i, :], one1[slot][:, i, :],
                                   start=True, stop=True)
                mm.then_inc(gates_done, 1)
            pe.wait_ge(h_out, E_TILES)
            for i in range(2):
                gates(i, i, True)
            with pe.Fori(1, S // 8) as it:
                for i in range(2):
                    gates(it * 2 + i, i, False)

            def up(j, i, start, stop):
                pe.wait_ge(lo_done, j + (N1 + E_TILES + 1))
                pe.wait_ge(act_lo, j + 1)
                s = (N1 + i) % DEPTH
                for t in range(NT):
                    cut = slice(t * P, (t + 1) * P)
                    for left, right, st, sp in ((a_hi[i], hi[s], start, False), (a_hi[i], lo[s], False, False),
                                                (a_lo[i], hi[s], False, stop)):
                        for c in range(2):
                            mm = pe.matmul((psS, psT)[t][:, c * 512:(c + 1) * 512], left[:, cut],
                                           right[:, c * 512:(c + 1) * 512], start=st, stop=sp)
                mm.then_inc(tile_used, 1)
            for i in range(4):
                up(i, i, i == 0, False)
            with pe.Fori(1, E_TILES // 4 - 1) as it:
                for i in range(4):
                    up(it * 4 + i, i, False, False)
            for i in range(4):
                up(E_TILES - 4 + i, i, False, i == 3)


def tile_of(w):
    return w.reshape(KD, P, P).transpose(1, 0, 2).reshape(P, D)


def stream(w_in, w_out, xa_wq, xa_wkv, xa_wo, peer_wq):
    cuts = np.cumsum([512] + [P] * 6 + [24] + [512] * 4)
    qa, kc, vc, ks, vs, kw, vw, ga, qb, fb, ib, gb = np.split(w_in, cuts[:-1], axis=1)
    qa = qa.reshape(D, G, REP, HD).transpose(0, 2, 1, 3).reshape(D, 512)
    source = {"kc": kc, "vc": vc, "ks": ks, "kw": kw, "q": qa, "vg": np.concatenate([vs, vw, ga], axis=1),
              "hq": qb, "hf": fb, "hv": ib, "hg": gb, "mk": xa_wkv[:, :D], "mv": xa_wkv[:, D:], "wo": w_out,
              "xq": xa_wq, "xo": xa_wo, "pq": peer_wq}
    out = np.zeros((N1, P, D), np.float32)
    for n, (name, kind, i, k0, m, cols, first, last, use) in enumerate(TILES):
        w = source[name][:, i * cols:(i + 1) * cols]
        if kind == "T":
            out[n] = tile_of(w)
        else:
            out[n, :, :m * cols] = w[k0 * P:(k0 + m) * P].reshape(m, P, cols).transpose(1, 0, 2).reshape(P, m * cols)
    return out


def constants():
    bf = np.dtype("bfloat16")
    i = np.arange(P)
    s, t = i[:, None], i[None, :]
    masks = np.zeros((P, 8, P), np.float32)
    masks[:, 0] = s == t
    for j in range(1, 8):
        masks[:, j] = (((s ^ t) >> (j - 1)) == 1) & (t > s)
    tok = (np.arange(NT)[None, :] * P + i[:, None])
    valid = (np.arange(NC) * CS + CB - 1)[None, None, :] <= tok[:, :, None]
    return {"ident": np.eye(P, dtype=np.float32), "identb": np.eye(P).astype(bf),
            "iota": np.broadcast_to(i, (P, P)).astype(bf),
            "iota16": np.broadcast_to(np.arange(TOPK), (P, TOPK)).astype(np.float32),
            "causal": np.where(t > s, -1e30, 0.0).astype(bf),
            "cmp_mask": np.where(valid, 0.0, -1e30).astype(np.float32),
            "cmp_any": valid.any(-1).astype(np.float32),
            "level_mask": masks.astype(bf)}


def kernel(x, mem, w_in, cmp_pos, cmp_w1, cmp_w2, hgrn_lb_logits, hgrn_norm_w, w_out,
           xa_wq, xa_wkv, xa_wo, peer_wq, peer_subkeys, peer_down, peer_up, ln_g, ln_b):
    import concourse.bacc as bacc
    from concourse.bass_utils import run_bass_kernel_spmd

    f = lambda v: np.asarray(v)
    x, mem = f(x)[0], f(mem)[0]
    sub = f(peer_subkeys)[0]
    subk = np.zeros((P, PH, 2 * NK), np.float32)
    for c in range(2):
        subk[c * 64:(c + 1) * 64, :, c * NK:(c + 1) * NK] = sub[:, c].transpose(2, 0, 1)
    arrays = {
        "xT": x.T.reshape(KD, P, S).transpose(1, 0, 2),
        "memT": mem.T.reshape(KD, P, S).transpose(1, 0, 2),
        "x_tok": x.reshape(NT, P, D).transpose(1, 0, 2),
        "w_stream": stream(f(w_in)[0], f(w_out)[0], f(xa_wq)[0], f(xa_wkv)[0], f(xa_wo)[0], f(peer_wq)[0]),
        "down": f(peer_down)[0].reshape(E_TILES, P, KD, P).transpose(0, 3, 2, 1).reshape(E_TILES, P, D),
        "up": f(peer_up)[0].reshape(E_TILES, P, D),
        "w1": f(cmp_w1)[0].reshape(2, CB // 2, P, P).transpose(2, 0, 1, 3),
        "w2": f(cmp_w2)[0].transpose(1, 0, 2),
        "pos": f(cmp_pos)[0].reshape(2, CB // 2, P).transpose(2, 0, 1),
        "lb": f(hgrn_lb_logits).transpose(2, 0, 1),
        "norm_w": f(hgrn_norm_w)[0].reshape(1, 512),
        "subk": subk,
        "ln_g": f(ln_g)[0], "ln_b": f(ln_b)[0],
        **constants(),
    }
    arrays = {k: np.ascontiguousarray(v) for k, v in arrays.items()}
    nc = bacc.Bacc("TRN2", target_bir_lowering=False, num_devices=1)
    aps = {k: nc.dram_tensor(f"in_{k}", v.shape, mybir.dt.from_np(v.dtype), kind="ExternalInput").ap()
           for k, v in arrays.items()}
    aps["out"] = nc.dram_tensor("out_x", (S, D), FP32, kind="ExternalOutput").ap()
    build(nc, aps)
    r = run_bass_kernel_spmd(nc, [{f"in_{k}": v for k, v in arrays.items()}], core_ids=[0])
    return r.results[0]["out_x"].reshape(1, S, D)
```

```python
import numpy as np
import concourse.bass as bass
import concourse.mybir as mybir

FP32 = mybir.dt.float32
F32R = mybir.dt.float32r
BF16 = mybir.dt.bfloat16
U32 = mybir.dt.uint32
U16 = mybir.dt.uint16
ACT = mybir.ActivationFunctionType
ALU = mybir.AluOpType
AX = mybir.AxisListType

P = 128
D = 1024
S = 256
NT = S // P
KD = D // P
HD = 64
NH = 8
G = 2
REP = NH // G
CB, CS = 32, 16
NC = (S - CB) // CS + 1
HH = 4
XH = 4
PH = 8
TOPK = 16
NK = 128
E_TILES = NK * NK // P
ALPHA = 2.0 ** 0.25
EPS = 1e-5
VG = 2 * P + 3 * NH

RUNS = [("kc", "T", 1), ("vc", "T", 1), ("ks", "T", 1), ("kw", "T", 1), ("q", "T", 4), ("vg", "R", 1),
        ("hq", "T", HH), ("hf", "T", HH), ("hv", "R", 1), ("hg", "R", 1),
        ("mk", "T", KD), ("mv", "R", 2), ("wo", "R", 2), ("xq", "T", KD), ("xo", "R", 2), ("pq", "T", KD)]


def plan():
    tiles, at, use = [], {}, 0
    for name, kind, count in RUNS:
        at[name] = len(tiles)
        for i in range(count):
            if kind == "T":
                tiles.append((name, kind, i, 0, KD, P, True, True, use))
                use += 1
            else:
                cols = VG if name == "vg" else 512
                per = D // cols
                k = 0
                while k < KD:
                    m = min(per, KD - k)
                    tiles.append((name, kind, i, k, m, cols, k == 0, k + m == KD, use))
                    k += m
                use += NT
    return tiles, at, use


TILES, AT, USES = plan()
N1 = len(TILES)
DEPTH = 4
EARLY = 8
AHEAD = 3
HALF = E_TILES // 2
VECTOR_READS = ("wo", "xo")


def consumers():
    count, out = [0, 0], []
    for name, kind, i, k0, m, cols, first, last, use in TILES:
        if first:
            v = int(name in VECTOR_READS)
            for _ in range(1 if kind == "T" else NT):
                count[v] += 1
                out.append((v, count[v]))
    return out, count


TAKEN, TAKEN_ALL = consumers()

UNITS = [(b, g, t) for b in range(2) for g in range(G) for t in range(NT)]


def order():
    out = []
    n = 0

    def gemm(k):
        nonlocal n
        for _ in range(k):
            out.append(("gemm", n))
            n += 1
    gemm(4)
    out.append(("blocks", 0))
    gemm(AT["hq"] - 4)
    out.append(("hidden", 0))
    gemm(1)
    out.append(("gelu", 0))
    gemm(1)
    out.append(("compressed", 0))
    for u in range(len(UNITS)):
        out.append(("scores", u))
        gemm(2)
        out.append(("turn_probs", u))
        gemm(1)
        out.append(("values", u))
        if n >= AT["hv"] and ("decay", 0) not in out:
            out.append(("decay", 0))
    for u in range(len(UNITS), len(UNITS) + NT):
        out.append(("scores", u))
        gemm(1)
        out.append(("turn_probs", u))
        gemm(1)
        out.append(("values", u))
    for j in range(9):
        out.append(("level", j))
        gemm(min(1, AT["wo"] - n))
    out += [("read_out", 0), ("read_out", 1), ("rms", 0), ("turn", 0), ("turn", 1)]
    gemm(AT["xq"] - n)
    out += [("norm", (0, 0)), ("norm", (0, 1)), ("turn", 2), ("turn", 3)]
    gemm(AT["xo"] - n)
    out += [("scores", 10), ("scores", 11), ("turn_probs", 10), ("values", 10),
            ("turn_probs", 11), ("values", 11), ("turn", 4), ("turn", 5)]
    gemm(AT["pq"] - n)
    out += [("norm", (1, 0)), ("norm", (1, 1)), ("turn", 6), ("turn", 7)]
    gemm(N1 - n)
    return out


ORDER = order()


class Steps:

    def __init__(self, engine, semaphore):
        self.engine, self.semaphore, self.count = engine, semaphore, 0

    def __call__(self, instruction):
        instruction.then_inc(self.semaphore, 1)
        self.count += 1

    def wait(self):
        self.engine.wait_ge(self.semaphore, self.count)


def build(nc, a):
    from contextlib import ExitStack
    ctx = ExitStack()
    with ctx:
        base = -(-nc.sbuf_base // 32) * 32
        place = {"at": base}

        def sb(name, shape, dt=FP32, at=None):
            size = int(np.prod(shape[1:])) * {FP32: 4, F32R: 4, BF16: 2, U32: 4}[dt]
            size = -(-size // 32) * 32
            where = place["at"] if at is None else at
            if at is None:
                place["at"] += size
            return nc.alloc_sbuf_tensor_at(name, shape, dt, offset=where)

        def ps(name, shape, dt=FP32):
            return ctx.enter_context(nc.psum_tensor(name, shape, dt))

        def sem(name):
            return ctx.enter_context(nc.semaphore(name))

        ident = sb("ident", [P, P])
        identb = sb("identb", [P, P], BF16)
        iota = sb("iota", [P, P])
        x2 = sb("x2", [P, NT, D])
        B_at = place["at"]
        b_hi = sb("b_hi", [P, KD, S], F32R)
        b_lo = sb("b_lo", [P, KD, S], F32R)
        hi = [sb(f"hi{i}", [P, D], F32R) for i in range(DEPTH)]
        raw, lo = [], []

        def raw_slot(i):
            at = place["at"]
            raw.append(sb(f"raw{i}", [P, D]))
            lo.append(sb(f"lo{i}", [P, D], F32R, at=at))
        for i in range(DEPTH):
            raw_slot(i)
        R_at = place["at"]

        H = sb("H", [P, E_TILES, S])
        late_at = place["at"]
        score_at = R_at + (E_TILES - 14) * S * 4
        route_s = sb("route_s", [P, PH * NT, 2 * NK], at=score_at)
        place["at"] = late_at + 2 * 1024
        chosen = sb("chosen", [P, 2, PH * NT, TOPK])
        chosen_s = sb("chosen_s", [P, PH * NT, TOPK])
        i1T = sb("i1T", [P, S])
        i2T = sb("i2T", [P, S])
        gT = sb("gT", [P, S])
        route_at = place["at"]
        unit_s = sb("unit_s", [P, 2, NK])
        unit_w = sb("unit_w", [P, 2, NK])
        unit_c = sb("unit_c", [P, 2, TOPK, TOPK])
        unit_m = sb("unit_m", [P, 2, TOPK])
        unit_i = sb("unit_i", [P, 2, TOPK], U32)
        unit_if = sb("unit_if", [P, 2, TOPK])
        unit_t = sb("unit_t", [P, TOPK])
        unit_p = sb("unit_p", [P, TOPK], U32)
        unit_ab = sb("unit_ab", [P, 2, TOPK], U32)
        unit_abf = sb("unit_abf", [P, 2, TOPK])
        iota16 = sb("iota16", [P, TOPK])
        gate_z = sb("gate_z", [P, PH * NT], at=route_at)
        hold_v = sb("hold_v", [P, 8])
        one2 = [sb(f"one2_{i}", [P, 4, NK]) for i in range(2)]
        same1 = [sb(f"same1_{i}", [P, 4, HALF]) for i in range(2)]
        one1 = [sb(f"one1_{i}", [P, 4, HALF]) for i in range(2)]
        assert place["at"] <= nc.sbuf_usable_end, place["at"] - nc.sbuf_usable_end
        ln_last = sb("ln_last", [P, 2, D], at=B_at)
        a_hi = [sb(f"act_hi{i}", [P, S], F32R, at=B_at + 8192 + 1024 * i) for i in range(4)]
        a_lo = [sb(f"act_lo{i}", [P, S], F32R, at=B_at + 12288 + 1024 * i) for i in range(4)]

        place["at"] = R_at
        for i in range(DEPTH, EARLY):
            raw_slot(i)
        o_hi = sb("o_hi", [P, KD, S], F32R)
        o_lo = sb("o_lo", [P, KD, S], F32R)
        ln_gb = sb("ln_gb", [P, 2, D])
        xk_at = place["at"]
        xk = sb("xk", [P, KD, S])
        xT = sb("xT", [P, KD, S], at=xk_at)
        xq_at = place["at"]
        xq = sb("xq", [P, KD, S])
        memT = sb("memT", [P, KD, S], at=xq_at)
        xv_at = place["at"]
        xv = sb("xv", [P, NT, D])
        hg_t = sb("hg_t", [P, NT, 512], at=xv_at)
        qT = sb("qT", [P, REP, S])
        kT = [sb(f"kT{i}", [P, S]) for i in range(2)]
        vg = sb("vg", [P, NT, VG])
        gate = sb("gate", [P, NT, 3 * NH])
        kv_at = place["at"]
        kvc = sb("kvc", [P, 2, S])
        kcp = sb("kcp", [P, 2, G, S])
        blk = sb("blk", [P, 2, CB // 2, G * NC])
        place["at"] = max(place["at"], kv_at + 8192)
        x_tok = sb("x_tok", [P, NT, D], at=kv_at)
        w1_at = place["at"]
        w1 = sb("w1", [P, 2, CB // 2, P])
        x1 = sb("x1", [P, NT, D], at=w1_at)
        xo = sb("xo", [P, NT, D], at=w1_at + 8192)
        w2 = sb("w2", [P, 2, HD])
        pos = sb("pos", [P, 2, CB // 2])
        hx = sb("hx", [P, 2 * G * NC])
        hy = sb("hy", [P, 2 * G * NC])
        hz = sb("hz", [P, 2 * G * NC])
        kcmp = sb("kcmp", [P, NC])
        vcmp = sb("vcmp", [NC, P])
        probs = sb("probs", [P, 4 * S])
        probsT = sb("probsT", [P, 4 * S])
        neg_max = sb("neg_max", [P, 2, NH])
        row_max = sb("row_max", [P, NH])
        row_sum = sb("row_sum", [P, 2, NH])
        coef = sb("coef", [P, NH])
        cmp_s = sb("cmp_s", [P, NH, NC])
        o_acc = sb("o_acc", [P, NT, 512])
        o_tmp = sb("o_tmp", [P, 512])
        causal = sb("causal", [P, P], BF16)
        cmp_mask = sb("cmp_mask", [P, NT, NC])
        cmp_any = sb("cmp_any", [P, NT])
        hq_at = place["at"]
        hq = sb("hq", [P, HH, S])
        oh = sb("oh", [P, NT, 512], at=hq_at)
        QF = sb("QF", [P, HH, S])
        KB = sb("KB", [P, HH, S])
        Fa = sb("Fa", [P, HH * S])
        Fb = sb("Fb", [P, HH * S // 2])
        lb = sb("lb", [P, 8, HH])
        level_mask = sb("level_mask", [P, 8, P], BF16, at=w1_at + 8192)
        att = sb("att", [P, HH, NT, P])
        att_off = sb("att_off", [P, HH, P])
        hv = sb("hv", [P, NT, 512])
        hg = sb("hg", [P, NT, 512])
        norm_w = sb("norm_w", [P, 512])
        stats = sb("stats", [P, NT, 2, 6])
        mv = sb("mv", [P, NT, 2])
        std = sb("std", [P, NT, HH])
        rstd = sb("rstd", [P, NT, HH])
        assert place["at"] <= nc.sbuf_usable_end, place["at"] - nc.sbuf_usable_end
        qryT = sb("qryT", [P, PH, S], at=xk_at)
        subk = sb("subk", [P, PH, 2 * NK], at=kv_at)
        stats2 = sb("stats2", [P, NT, 2, 6], at=route_at)
        mv2 = sb("mv2", [P, NT, 2], at=route_at + 128)
        std2 = sb("std2", [P, NT, HH], at=route_at + 192)
        rstd2 = sb("rstd2", [P, NT, HH], at=route_at + 256)

        psG = [ps(f"psG{i}", [P, 512]) for i in range(2)]
        psS = ps("psS", [P, 1024])
        psT = ps("psT", [P, 1024])
        psO = ps("psO", [P, 1024])
        psM = psO[:, 512:1024]

        raw_in = [sem(f"raw_in{i}") for i in range(EARLY)]
        table_in = [sem(f"table_in{i}") for i in range(DEPTH)]
        hi_done, lo_done, tile_used = sem("hi_done"), sem("lo_done"), sem("tile_used")
        x_in, mem_in, const_in, comp_in = sem("x_in"), sem("mem_in"), sem("const_in"), sem("comp_in")
        rec_in, xtok_in, subk_in, ln_in = sem("rec_in"), sem("xtok_in"), sem("subk_in"), sem("ln_in")
        shift_in, out_done = sem("shift_in"), sem("out_done")
        mask_in = sem("mask_in")
        split_hi, split_lo = sem("split_hi"), sem("split_lo")
        act_took, dve_took = sem("act_took"), sem("dve_took")
        took = (act_took, dve_took)
        blocks_ready, hidden_done, hidden_out, tanh_done, gelu_ready = (
            sem("blocks_ready"), sem("hidden_done"), sem("hidden_out"), sem("tanh_done"), sem("gelu_ready"))
        cmp_done, cmp_out = sem("cmp_done"), sem("cmp_out")
        s_done, max_done, exp_done, turned, probsT_ready, pv_done, combined = (
            sem("s_done"), sem("max_done"), sem("exp_done"), sem("turned"), sem("probsT_ready"),
            sem("pv_done"), sem("combined"))
        lb_exp, lb_max = sem("lb_exp"), sem("lb_max")
        att_zero, decay_ready, level_done, level_merged, factors_ready = (
            sem("att_zero"), sem("decay_ready"), sem("level_done"), sem("level_merged"), sem("factors_ready"))
        off_ready, read_done, read_out_ready, var_ready, std_ready, rec_ready = (
            sem("off_ready"), sem("read_done"), sem("read_out_ready"), sem("var_ready"), sem("std_ready"),
            sem("rec_ready"))
        turn_done, turn_hi, turn_lo = sem("turn_done"), sem("turn_hi"), sem("turn_lo")
        norm_ready = sem("norm_ready")
        score_done, score_out = sem("score_done"), sem("score_out")
        h_out, routed = sem("h_out"), sem("routed")
        shifted, gate_exp, gate_ready, index_done, index_out = (
            sem("shifted"), sem("gate_exp"), sem("gate_ready"), sem("index_done"), sem("index_out"))
        same_ready, one_ready, gates_done, gated = (
            sem("same_ready"), sem("one_ready"), sem("gates_done"), sem("gated"))
        act_hi, act_lo = sem("act_hi"), sem("act_lo")
        dve_step = sem("dve_step")
        block = ctx.enter_context(nc.Block())

        XU = len(UNITS) + NT

        def unit(u):
            if u < len(UNITS):
                b, g, t = UNITS[u]
                return b, g, t, REP, P * (t + 1)
            if u < XU:
                return 2, 0, u - len(UNITS), NH, NC
            return 3, 0, u - XU, XH, S

        @block.sync
        def _(sp):
            sp.dma_start(xT[:], a["xT"]).then_inc(x_in, 16)
            for n in range(N1):
                if n >= EARLY:
                    sp.wait_ge(tile_used, n - EARLY + 1)
                sp.dma_start(raw[n % EARLY][:], a["w_stream"][n]).then_inc(raw_in[n % EARLY], 16)
                if n == 3:
                    sp.dma_start(memT[:], a["memT"]).then_inc(mem_in, 16)

            def table(name, j, i, used):
                sp.wait_ge(tile_used, used)
                sp.dma_start(raw[(N1 + i) % DEPTH][:], a[name][j]).then_inc(table_in[i], 16)
            with sp.Fori(0, E_TILES // DEPTH) as it:
                for i in range(DEPTH):
                    table("down", it * DEPTH + i, i, it * DEPTH + (N1 + i - DEPTH + 1))
            with sp.Fori(0, E_TILES // DEPTH) as it:
                for i in range(DEPTH):
                    table("up", it * DEPTH + i, i, it * DEPTH + (N1 + E_TILES + i - DEPTH + 1))
            for t in range(NT):
                sp.wait_ge(norm_ready, 2 * NT + t + 1)
                sp.dma_start(a["out"][t * P:(t + 1) * P, :], x2[:, t, :]).then_inc(out_done, 16)
            sp.wait_ge(out_done, 16 * NT)

        @block.gpsimd
        def _(pool):
            for dst, name in ((pos, "pos"), (w1, "w1"), (w2, "w2")):
                pool.dma_start(dst[:], a[name]).then_inc(comp_in, 16)
            for dst, name in ((ident, "ident"), (identb, "identb"), (iota, "iota"), (causal, "causal"),
                              (cmp_mask, "cmp_mask"), (cmp_any, "cmp_any")):
                pool.dma_start(dst[:], a[name]).then_inc(const_in, 16)
            pool.dma_start(lb[:, 0:2, :], a["lb"]).then_inc(rec_in, 16)
            pool.dma_start(norm_w[:], a["norm_w"].broadcast_to([P, 512])).then_inc(rec_in, 16)
            for i, name in enumerate(("ln_g", "ln_b")):
                pool.dma_start(ln_gb[:, i, :], a[name][0:1, :].broadcast_to([P, D])).then_inc(ln_in, 16)
            pool.memset(att[:], 0.0).then_inc(att_zero, 1)
            pool.wait_ge(act_took, 2)
            for g in range(G):
                for par in range(2):
                    pool.dma_start(kcp[par * HD:(par + 1) * HD, :, g, 0:S - par],
                                   kvc[g * HD:(g + 1) * HD, :, par:S]).then_inc(shift_in, 16)
            pool.wait_ge(hidden_done, 1)
            pool.dma_start(level_mask[:], a["level_mask"]).then_inc(mask_in, 16)
            pool.dma_start(x_tok[:], a["x_tok"]).then_inc(xtok_in, 16)
            pool.wait_ge(norm_ready, NT)
            for i, name in enumerate(("ln_g", "ln_b")):
                pool.dma_start(ln_gb[:, i, :], a[name][1:2, :].broadcast_to([P, D])).then_inc(ln_in, 16)
            pool.dma_start(subk[:], a["subk"]).then_inc(subk_in, 16)
            pool.dma_start(iota16[:], a["iota16"]).then_inc(subk_in, 16)
            pool.wait_ge(h_out, E_TILES)
            for i, name in enumerate(("ln_g", "ln_b")):
                pool.dma_start(ln_last[:, i, :], a[name][2:3, :].broadcast_to([P, D])).then_inc(ln_in, 16)

        @block.scalar
        def _(act):
            def split(n):
                act.wait_ge(raw_in[n % EARLY], 16 * (n // EARLY + 1))
                if n >= DEPTH:
                    act.wait_ge(tile_used, n - DEPTH + 1)
                act.activation(hi[n % DEPTH][:], raw[n % EARLY][:], ACT.Copy).then_inc(hi_done, 1)

            def split_table(n, i, arrived):
                s = (N1 + i) % DEPTH
                act.wait_ge(table_in[i % DEPTH], arrived)
                act.wait_ge(tile_used, n - DEPTH + 1)
                act.activation(hi[s][:], raw[s][:], ACT.Copy).then_inc(hi_done, 1)

            def take(n):
                name, kind, i, k0, m, cols, first, last, use = TILES[n]
                if not last or name in VECTOR_READS:
                    return
                act.wait_ge(tile_used, n + 1)
                if kind == "T":
                    src = psG[use % 2][:, 0:S]
                    if name == "hf":
                        act.activation(Fa[:, i * S:(i + 1) * S], src, ACT.Tanh, scale=0.5).then_inc(act_took, 1)
                        return
                    if name == "pq" and i == 0:
                        act.wait_ge(turned, XU + NT)
                    dst = {"kc": kvc[:, 0, :], "vc": kvc[:, 1, :], "ks": kT[0][:], "kw": kT[1][:],
                           "q": qT[:, i % REP, :], "hq": hq[:, i % HH, :], "mk": xk[:, i, :], "xq": xq[:, i, :],
                           "pq": qryT[:, i, :]}[name]
                    act.activation(dst, src, ACT.Copy).then_inc(act_took, 1)
                    return
                for t in range(NT):
                    src = psG[(use + t) % 2]
                    if name == "vg":
                        act.activation(vg[:, t, 0:2 * P], src[:, 0:2 * P], ACT.Copy)
                        act.activation(vg[:, t, 2 * P:VG], src[:, 2 * P:VG], ACT.Tanh, scale=0.5).then_inc(act_took, 1)
                    elif name == "hv":
                        act.activation(hv[:, t, :], src[:], ACT.Copy).then_inc(act_took, 1)
                    elif name == "hg":
                        act.activation(hg[:, t, :], src[:], ACT.Copy)
                        act.activation(hg_t[:, t, :], src[:], ACT.Tanh, scale=0.5).then_inc(act_took, 1)
                    else:
                        act.activation(xv[:, t, i * 512:(i + 1) * 512], src[:], ACT.Copy).then_inc(act_took, 1)

            def exp_unit(u):
                b, g, t, heads, keys = unit(u)
                act.wait_ge(max_done, u + 1)
                if u:
                    act.wait_ge(turned, u)
                if b == 2:
                    act.activation(probs[:, 0:NH * NC], cmp_s[:, :, :].rearrange("p h n -> p (h n)"), ACT.Exp)\
                        .then_inc(exp_done, 1)
                    return
                scale = HD ** -0.5 if b < 2 else (D // XH) ** -0.5
                for r in range(heads):
                    last = act.activation(probs[:, r * S:r * S + keys], psS[:, r * S:r * S + keys], ACT.Exp,
                                          bias=neg_max[:, u % 2, r:r + 1], scale=scale,
                                          accum_out=row_sum[:, u % 2, r:r + 1])
                last.then_inc(exp_done, 1)

            def take_probsT(u):
                b, g, t, heads, keys = unit(u)
                act.wait_ge(turned, u + 1)
                if u:
                    act.wait_ge(pv_done, u)
                if b == 2:
                    act.activation(probsT[0:NC, 0:NH * P], psT[0:NC, 0:NH * P], ACT.Copy).then_inc(probsT_ready, 1)
                else:
                    w = heads * P * (keys // P)
                    act.activation(probsT[:, 0:w], psT[:, 0:w], ACT.Copy).then_inc(probsT_ready, 1)

            act.wait_ge(x_in, 16)
            act.activation(o_hi[:], xT[:], ACT.Copy).then_inc(split_hi, 1)
            for n in range(DEPTH):
                split(n)
            act.wait_ge(lb_max, 1)
            act.activation(lb[:, 2:4, :], lb[:, 2:4, :], ACT.Exp).then_inc(lb_exp, 1)
            for what, i in ORDER:
                if what == "gemm":
                    if i + DEPTH < N1:
                        split(i + DEPTH)
                    elif i + DEPTH < N1 + AHEAD:
                        split_table(i + DEPTH, i + DEPTH - N1, 16 * ((i + DEPTH - N1) // DEPTH + 1))
                    take(i)
                    if i == AT["hq"]:
                        act.wait_ge(mem_in, 16)
                        act.activation(b_hi[:], memT[:], ACT.Copy).then_inc(split_hi, 1)
                elif what == "gelu":
                    act.wait_ge(hidden_done, 1)
                    act.activation(hx[:], psM[:, 0:2 * G * NC], ACT.Copy).then_inc(hidden_out, 1)
                    act.wait_ge(hidden_out, 2)
                    act.activation(hy[:], hy[:], ACT.Tanh, scale=(2 / np.pi) ** 0.5).then_inc(tanh_done, 1)
                elif what == "compressed":
                    act.wait_ge(cmp_done, 1)
                    act.activation(kcmp[:], psM[:, 128:128 + NC], ACT.Copy)
                    act.activation(vcmp[:], psM[0:NC, 256:256 + P], ACT.Copy).then_inc(cmp_out, 1)
                elif what == "scores":
                    exp_unit(i)
                elif what == "turn_probs":
                    take_probsT(i)
                elif what == "level" and i == 8:
                    act.wait_ge(level_done, 9)
                    act.activation(att_off[:], psS[:, 0:HH * P], ACT.Copy).then_inc(off_ready, 1)
                elif what == "read_out":
                    act.wait_ge(read_done, i + 1)
                    act.activation(oh[:, i, :], psO[:, i * 512:(i + 1) * 512], ACT.Copy).then_inc(read_out_ready, 1)
                elif what == "rms":
                    act.wait_ge(var_ready, 1)
                    act.activation(std[:], std[:], ACT.Sqrt).then_inc(std_ready, 1)
                elif what == "norm":
                    w, t = i
                    act.wait_ge(var_ready, 2 + w * NT + t)
                    act.activation(std[:, t, 0:1], mv[:, t, 1:2], ACT.Sqrt).then_inc(std_ready, 1)
                elif what == "turn":
                    t = i % 2
                    dst = o_hi if i // 2 % 2 == 0 else b_hi
                    act.wait_ge(turn_done, i + 1)
                    act.activation(dst[:, :, t * P:(t + 1) * P],
                                   (psS, psT)[t][:].rearrange("p (k c) -> p k c", c=P), ACT.Copy).then_inc(turn_hi, 1)
            for u in range(PH * NT):
                act.wait_ge(score_done, u + 1)
                act.activation(route_s[:, u, :], (psO, psS)[u % 4 // 2][:, u % 2 * 512:u % 2 * 512 + S], ACT.Copy).then_inc(score_out, 1)
            def activations(j, i):
                act.wait_ge(tile_used, j + (N1 + 1))
                act.activation(H[:, bass.ds(j, 1), :].rearrange("p a t -> p (a t)"), psG[i % 2][:, 0:S],
                               ACT.Gelu).then_inc(h_out, 1)

            def ahead(j, i):
                k = (i + AHEAD) % DEPTH
                split_table(j + (N1 + AHEAD), i + AHEAD, (j + (AHEAD - k)) * (16 // DEPTH) + 16)

            def scale_gates(g, slot, half):
                act.wait_ge(same_ready, g + 1)
                for i in range(4):
                    last = act.activation(one1[slot][:, i, :], same1[slot][:, i, :], ACT.Copy,
                                          scale=gT[:, bass.ds(g * 4 + (i - half * S), 1)])
                last.then_inc(one_ready, 1)
            with act.Fori(0, HALF // 8) as it:
                for i in range(8):
                    activations(it * 8 + i, i % DEPTH)
                    ahead(it * 8 + i, i % DEPTH)
            act.wait_ge(shifted, 1)
            act.activation(chosen_s[:], chosen_s[:], ACT.Exp).then_inc(gate_exp, 1)
            for i in range(2):
                activations(HALF + i, i)
                ahead(HALF + i, i)
            act.wait_ge(index_done, 3)
            for q in range(3):
                act.activation((i1T, i2T, gT)[q][:], psO[:, q * S:(q + 1) * S], ACT.Copy).then_inc(index_out, 1)
            for i in range(2, 4):
                activations(HALF + i, i)
                ahead(HALF + i, i)
            scale_gates(0, 0, 0)
            with act.Fori(HALF // 4 + 1, E_TILES // 4) as it:
                for i in range(4):
                    activations(it * 4 + i, i)
                    ahead(it * 4 + i, i)
                    scale_gates(it * 4 + (i + 1 - HALF - 4), (i + 1) % 2, 0)
            for g in range(S // 4 - 3, S // 4 + 1):
                scale_gates(g, g % 2, int(g == S // 4))

            def round_act(j, slot, first=False):
                if not first:
                    act.wait_ge(tile_used, j + (N1 + E_TILES - 3))
                act.activation(a_hi[slot][:], H[:, bass.ds(j, 1), :].rearrange("p a t -> p (a t)"), ACT.Copy)\
                    .then_inc(act_hi, 1)

            def next_tile(j, i):
                round_act(j, i)
                ahead(j + (E_TILES - 4), i)
            act.wait_ge(gated, S // 4)
            for i in range(4):
                round_act(i, i, True)
            with act.Fori(1, HALF // 4) as it:
                for i in range(4):
                    next_tile(it * 4 + i, i)
                    scale_gates(it * 4 + (HALF - 3 + i), (i + 1) % 2, 1)
            for g in range(S // 2 - 3, S // 2):
                scale_gates(g, g % 2, 1)
            act.wait_ge(gated, S // 2)
            with act.Fori(HALF // 4, E_TILES // 4) as it:
                for i in range(4):
                    next_tile(it * 4 + i, i)
            ahead(2 * E_TILES - 4, 0)
            for t in range(NT):
                act.wait_ge(var_ready, 2 + 2 * NT + t)
                act.activation(std2[:, t, 0:1], mv2[:, t, 1:2], ACT.Sqrt).then_inc(std_ready, 1)

        @block.vector
        def _(dve):
            step = Steps(dve, dve_step)

            def rest(n):
                dve.wait_ge(hi_done, n + 1)
                if n >= DEPTH:
                    dve.wait_ge(tile_used, n - DEPTH + 1)
                s = n % (EARLY if n < N1 else DEPTH)
                dve.tensor_tensor(lo[s][:], raw[s][:], hi[n % DEPTH][:].bitcast(FP32), ALU.subtract)\
                    .then_inc(lo_done, 1)

            def rest_table(n, i):
                dve.wait_ge(hi_done, n + 1)
                s = (N1 + i) % DEPTH
                dve.tensor_tensor(lo[s][:], raw[s][:], hi[s][:].bitcast(FP32), ALU.subtract)\
                    .then_inc(lo_done, 1)

            def add_residual(n):
                name, kind, i, k0, m, cols, first, last, use = TILES[n]
                if not last:
                    return
                src, dst = (x_tok, x1) if name == "wo" else (x1, x2)
                if name == "wo" and i == 0:
                    dve.wait_ge(xtok_in, 16)
                dve.wait_ge(tile_used, n + 1)
                for t in range(NT):
                    z = dst[:, t, i * 512:(i + 1) * 512]
                    dve.scalar_tensor_tensor(out=z, in0=src[:, t, i * 512:(i + 1) * 512], scalar=ALPHA,
                                             in1=psG[(use + t) % 2][:], op0=ALU.mult, op1=ALU.add)\
                        .then_inc(dve_took, 1)
                    dve.wait_ge(dve_took, TAKEN[use + t][1])
                    step(dve.bn_stats(stats[:, t, i, :], z))

            def variance(t, st, m):
                dve.bn_aggr(m[:, t, :], st[:, t, :, :].rearrange("p c s -> p (c s)")).then_inc(dve_step, 1)
                step.count += 1
                step.wait()
                dve.tensor_scalar(m[:, t, 1:2], m[:, t, 1:2], EPS, None, ALU.add).then_inc(var_ready, 1)

            def normalize(w, t, z, m, sd, rs, gb):
                dve.wait_ge(std_ready, 2 + w * NT + t)
                step(dve.reciprocal(rs[:, t, 0:1], sd[:, t, 0:1]))
                step.wait()
                step(dve.tensor_scalar(z, z, m[:, t, 0:1], rs[:, t, 0:1], ALU.subtract, ALU.mult))
                step.wait()
                dve.wait_ge(ln_in, 32 * (w + 1))
                step(dve.tensor_tensor(z, z, gb[:, 0, :], ALU.mult))
                step.wait()
                dve.tensor_tensor(z, z, gb[:, 1, :], ALU.add).then_inc(norm_ready, 1)

            def max_unit(u):
                b, g, t, heads, keys = unit(u)
                dve.wait_ge(s_done, u + 1)
                if b == 2:
                    for gg in range(G):
                        step(dve.scalar_tensor_tensor(
                            out=cmp_s[:, gg * REP:(gg + 1) * REP, :],
                            in0=psS[:, gg * 512:gg * 512 + REP * 16].rearrange("p (h n) -> p h n", n=16)[:, :, 0:NC],
                            scalar=HD ** -0.5, in1=cmp_mask[:, t, :].unsqueeze(1).broadcast_to([P, REP, NC]),
                            op0=ALU.mult, op1=ALU.add))
                    step.wait()
                    step(dve.tensor_reduce(row_max[:], cmp_s[:], AX.X, ALU.max))
                    step.wait()
                    dve.tensor_tensor(cmp_s[:], cmp_s[:], row_max[:].unsqueeze(2).broadcast_to([P, NH, NC]),
                                      ALU.subtract).then_inc(max_done, 1)
                    return
                scale = HD ** -0.5 if b < 2 else (D // XH) ** -0.5
                step(dve.tensor_reduce(row_max[:, 0:heads],
                                       psS[:].rearrange("p (h n) -> p h n", n=S)[:, :, 0:keys], AX.X, ALU.max))
                step.wait()
                dve.tensor_scalar(neg_max[:, u % 2, 0:heads], row_max[:, 0:heads], -scale, None, ALU.mult)\
                    .then_inc(max_done, 1)

            def combine(u):
                b, g, t, heads, keys = unit(u)
                dve.wait_ge(exp_done, u + 1)
                if u:
                    dve.wait_ge(combined, u)
                sums = row_sum[:, u % 2, 0:heads]
                if b == 2:
                    step(dve.tensor_reduce(sums, probs[:, 0:NH * NC].rearrange("p (h n) -> p h n", n=NC),
                                           AX.X, ALU.add))
                    step.wait()
                step(dve.reciprocal(coef[:, 0:heads], sums))
                step.wait()
                if b < 3:
                    col = {0: 1, 1: 2, 2: 0}[b]
                    gates = gate[:, t, :].rearrange("p (h c) -> p h c", c=3)[:, g * REP:g * REP + heads, col]
                    step(dve.tensor_tensor(coef[:, 0:heads], coef[:, 0:heads], gates, ALU.mult))
                    step.wait()
                if b == 2:
                    step(dve.tensor_scalar(coef[:], coef[:], cmp_any[:, t:t + 1], None, ALU.mult))
                    step.wait()
                dve.wait_ge(pv_done, u + 1)
                width = HD if b < 3 else D // XH
                src = psO[:, 0:heads * width].rearrange("p (h d) -> p h d", d=width)
                by = coef[:, 0:heads].unsqueeze(2).broadcast_to([P, heads, width])
                if b == 3:
                    dve.tensor_tensor(xo[:, t, :].rearrange("p (h d) -> p h d", d=width), src, by, ALU.mult)\
                        .then_inc(combined, 1)
                    return
                dst = o_acc[:, t, g * 256:g * 256 + heads * HD].rearrange("p (h d) -> p h d", d=HD)
                if b == 0:
                    dve.tensor_tensor(dst, src, by, ALU.mult).then_inc(combined, 1)
                    return
                tmp = o_tmp[:, 0:heads * HD].rearrange("p (h d) -> p h d", d=HD)
                step(dve.tensor_tensor(tmp, src, by, ALU.mult))
                step.wait()
                dve.tensor_tensor(dst, dst, tmp, ALU.add).then_inc(combined, 1)

            def lower_bound():
                dve.wait_ge(rec_in, 32)
                step(dve.tensor_tensor(lb[:, 4, :], lb[:, 0, :], lb[:, 1, :], ALU.max))
                step.wait()
                dve.tensor_tensor(lb[:, 2:4, :], lb[:, 0:2, :], lb[:, 4, :].unsqueeze(1).broadcast_to([P, 2, HH]),
                                  ALU.subtract).then_inc(lb_max, 1)
                dve.wait_ge(lb_exp, 1)
                step(dve.tensor_tensor(lb[:, 4, :], lb[:, 2, :], lb[:, 3, :], ALU.add))
                step.wait()
                step(dve.reciprocal(lb[:, 5, :], lb[:, 4, :]))
                step.wait()
                step(dve.tensor_tensor(lb[:, 6, :], lb[:, 2, :], lb[:, 5, :], ALU.mult))
                step.wait()
                step(dve.tensor_scalar(lb[:, 5, :], lb[:, 6, :], -0.5, 0.5, ALU.mult, ALU.add))
                step.wait()
                step(dve.tensor_tensor(lb[:, 7, :], lb[:, 6, :], lb[:, 5, :], ALU.add))
                step.wait()

            dve.wait_ge(split_hi, 1)
            dve.tensor_tensor(o_lo[:], xT[:], o_hi[:].bitcast(FP32), ALU.subtract).then_inc(split_lo, 1)
            for n in range(DEPTH):
                rest(n)
            lower_bound()
            for what, i in ORDER:
                if what == "gemm":
                    if i + DEPTH < N1 + AHEAD:
                        rest(i + DEPTH)
                    if TILES[i][0] in VECTOR_READS:
                        add_residual(i)
                    if i == AT["hq"]:
                        dve.wait_ge(split_hi, 2)
                        dve.tensor_tensor(b_lo[:], memT[:], b_hi[:].bitcast(FP32), ALU.subtract)\
                            .then_inc(split_lo, 1)
                        dve.wait_ge(act_took, TAKEN[TILES[AT["vg"]][8] + 1][1])
                        step(dve.tensor_scalar(gate[:], vg[:, :, 2 * P:VG], 1.0, 0.5, ALU.add, ALU.mult))
                    if i == AT["mk"]:
                        dve.wait_ge(act_took, TAKEN[TILES[AT["hg"]][8] + 1][1])
                        step(dve.tensor_scalar(hg_t[:], hg_t[:], 1.0, 0.5, ALU.add, ALU.mult))
                        step(dve.tensor_tensor(hg[:], hg[:], norm_w[:].unsqueeze(1).broadcast_to([P, NT, 512]),
                                               ALU.mult))
                        step.wait()
                        step(dve.tensor_tensor(hg[:], hg[:], hg_t[:], ALU.mult))
                elif what == "blocks":
                    dve.wait_ge(shift_in, 16 * 4)
                    dve.wait_ge(comp_in, 48)
                    for kv in range(2):
                        for g in range(G):
                            src = kcp[:, kv, g, :]
                            src = bass.AP(tensor=src.tensor, offset=src.offset,
                                          ap=[list(src.ap[0]), [2, CB // 2], [CS, NC]])
                            last = dve.tensor_tensor(blk[:, kv, :, g * NC:(g + 1) * NC], src,
                                                     pos[:, kv, :].unsqueeze(2).broadcast_to([P, CB // 2, NC]),
                                                     ALU.add)
                    last.then_inc(blocks_ready, 1)
                elif what == "gelu":
                    dve.wait_ge(hidden_out, 1)
                    step(dve.tensor_tensor(hy[:], hx[:], hx[:], ALU.mult))
                    step.wait()
                    step(dve.tensor_tensor(hy[:], hy[:], hx[:], ALU.mult))
                    step.wait()
                    dve.scalar_tensor_tensor(out=hy[:], in0=hy[:], scalar=0.044715, in1=hx[:],
                                             op0=ALU.mult, op1=ALU.add).then_inc(hidden_out, 1)
                    dve.wait_ge(tanh_done, 1)
                    step(dve.tensor_scalar(hz[:], hy[:], 1.0, 0.5, ALU.add, ALU.mult))
                    step.wait()
                    dve.tensor_tensor(hz[:], hz[:], hx[:], ALU.mult).then_inc(gelu_ready, 1)
                elif what == "scores":
                    max_unit(i)
                elif what == "values":
                    combine(i)
                elif what == "decay":
                    dve.wait_ge(act_took, TAKEN[TILES[AT["hf"] + HH - 1][8]][1])
                    for h in range(HH):
                        step(dve.tensor_scalar(Fa[:, h * S:(h + 1) * S], Fa[:, h * S:(h + 1) * S], lb[:, 5, h:h + 1],
                                               lb[:, 7, h:h + 1], ALU.mult, ALU.add))
                    step.wait()
                    step(dve.tensor_scalar(KB[:].rearrange("p h t -> p (h t)"), Fa[:], -1.0, 1.0, ALU.mult, ALU.add))
                    dve.tensor_tensor(QF[:].rearrange("p h t -> p (h t)"), Fa[:],
                                      hq[:].rearrange("p h t -> p (h t)"), ALU.mult).then_inc(decay_ready, 1)
                    step.wait()
                elif what == "level":
                    if 1 <= i <= 7:
                        L = 1 << (i - 1)
                        n = HH * S // (2 * L)
                        F, F2 = (Fa, Fb) if i % 2 else (Fb, Fa)
                        fe = F[:, 0:2 * n].rearrange("p (n b) -> p n b", b=2)
                        dve.wait_ge(level_done, i + 1)
                        if i == 1:
                            dve.wait_ge(decay_ready, 1)
                        q2 = QF[:].rearrange("p h t -> p (h t)").rearrange("p (n b l) -> p n b l", b=2, l=L)[:, :, 1, :]
                        k2 = KB[:].rearrange("p h t -> p (h t)").rearrange("p (n b l) -> p n b l", b=2, l=L)[:, :, 0, :]
                        dve.tensor_tensor(q2, q2, fe[:, :, 0].unsqueeze(2).broadcast_to([P, n, L]), ALU.mult)
                        dve.tensor_tensor(k2, k2, fe[:, :, 1].unsqueeze(2).broadcast_to([P, n, L]), ALU.mult)
                        dve.tensor_tensor(F2[:, 0:n], fe[:, :, 0], fe[:, :, 1], ALU.mult).then_inc(factors_ready, 1)
                    if i <= 7:
                        dve.wait_ge(level_done, i + 1)
                        if i == 0:
                            dve.wait_ge(att_zero, 1)
                            dve.wait_ge(mask_in, 16)
                        else:
                            dve.wait_ge(level_merged, i)
                        X = (psS, psT)[i % 2]
                        dve.copy_predicated(att[:].rearrange("p h b t -> p (h b) t"),
                                            level_mask[:, i, :].bitcast(U16).unsqueeze(1).broadcast_to([P, HH * NT, P]),
                                            X[:].rearrange("p (n t) -> p n t", t=P)).then_inc(level_merged, 1)
                        if 1 <= i <= 7:
                            dve.wait_ge(factors_ready, i)
                elif what == "rms":
                    dve.wait_ge(read_out_ready, NT)
                    t3 = probs[:].rearrange("p (n e) -> p n e", e=P)
                    o3 = oh[:].rearrange("p t (h e) -> p (t h) e", e=P)
                    step(dve.tensor_tensor(t3, o3, o3, ALU.mult))
                    step.wait()
                    sd = std[:].rearrange("p t h -> p (t h)")
                    step(dve.tensor_reduce(sd, t3, AX.X, ALU.add))
                    step.wait()
                    dve.tensor_scalar(sd, sd, 1.0 / P, EPS, ALU.mult, ALU.add).then_inc(var_ready, 1)
                    dve.wait_ge(std_ready, 1)
                    rs = rstd[:].rearrange("p t h -> p (t h)")
                    step(dve.reciprocal(rs, sd))
                    step.wait()
                    step(dve.tensor_tensor(o3, o3, rs.unsqueeze(2).broadcast_to([P, NT * HH, P]), ALU.mult))
                    step.wait()
                    dve.tensor_tensor(oh[:], oh[:], hg[:], ALU.mult).then_inc(rec_ready, 1)
                elif what == "turn":
                    t = i % 2
                    dst, rounded = (o_lo, o_hi) if i // 2 % 2 == 0 else (b_lo, b_hi)
                    dve.wait_ge(turn_hi, i + 1)
                    dve.tensor_tensor(dst[:, :, t * P:(t + 1) * P],
                                      (psS, psT)[t][:].rearrange("p (k c) -> p k c", c=P),
                                      rounded[:, :, t * P:(t + 1) * P].bitcast(FP32), ALU.subtract)\
                        .then_inc(turn_lo, 1)
                elif what == "norm":
                    w, t = i
                    step.wait()
                    variance(t, stats, mv)
                    normalize(w, t, (x1, x2)[w][:, t, :], mv, std, rstd, ln_gb)

            LOWEST = -3.0e38
            PER = 27
            dve.wait_ge(subk_in, 32)
            dve.wait_ge(score_out, PH * NT)
            step(dve.memset(hold_v[:], 0.0))
            step.wait()
            c0 = step.count
            with dve.Fori(0, HALF // 8) as it:
                mark = {"n": 0}

                def did(instruction):
                    instruction.then_inc(dve_step, 1)
                    mark["n"] += 1

                def mine():
                    dve.wait_ge(dve_step, it * (2 * PER) + (c0 + mark["n"]))
                    dve.tensor_copy(hold_v[:, 0:1], hold_v[:, 1:2])

                def ahead(i):
                    rest_table(it * 8 + (N1 + AHEAD + i), i + AHEAD)

                def best(values, spare, out_v, out_i):
                    did(dve.max(out_v[:, 0:8], values))
                    mine()
                    did(dve.max_index(out_i[:, 0:8], out_v[:, 0:8], values))
                    did(dve.match_replace(spare, out_v[:, 0:8], values, LOWEST))
                    mine()
                    did(dve.max(out_v[:, 8:16], spare))
                    mine()
                    did(dve.max_index(out_i[:, 8:16], out_v[:, 8:16], spare))

                def route(r):
                    u = it * 2 + r
                    ahead(4 * r)
                    did(dve.tensor_copy(unit_s[:].rearrange("p c n -> p (c n)"),
                                        route_s[:, bass.ds(u, 1), :].rearrange("p a n -> p (a n)")))
                    mine()
                    best(unit_s[:, 0, :], unit_w[:, 0, :], unit_m[:, 0, :], unit_i[:, 0, :])
                    best(unit_s[:, 1, :], unit_w[:, 1, :], unit_m[:, 1, :], unit_i[:, 1, :])
                    ahead(4 * r + 1)
                    mine()
                    did(dve.tensor_copy(unit_if[:], unit_i[:]))
                    cand = unit_c[:, 0, :, :]
                    did(dve.tensor_tensor(cand, unit_m[:, 0, :].unsqueeze(2).broadcast_to([P, TOPK, TOPK]),
                                          unit_m[:, 1, :].unsqueeze(1).broadcast_to([P, TOPK, TOPK]), ALU.add))
                    mine()
                    best(cand.rearrange("p a b -> p (a b)"), unit_w[:].rearrange("p c n -> p (c n)"),
                         unit_t[:], unit_p[:])
                    ahead(4 * r + 2)
                    mine()
                    did(dve.tensor_copy(chosen_s[:, bass.ds(u, 1), :].rearrange("p a k -> p (a k)"), unit_t[:]))
                    did(dve.tensor_scalar(unit_ab[:, 0, :], unit_p[:], 4, None, ALU.logical_shift_right))
                    did(dve.tensor_scalar(unit_ab[:, 1, :], unit_p[:], 15, None, ALU.bitwise_and))
                    mine()
                    did(dve.tensor_copy(unit_abf[:], unit_ab[:]))
                    mine()
                    did(dve.tensor_tensor(unit_c[:].rearrange("p c k a -> p (c k) a"),
                                          iota16[:].unsqueeze(1).broadcast_to([P, 2 * TOPK, TOPK]),
                                          unit_abf[:].rearrange("p c k -> p (c k)").unsqueeze(2)
                                          .broadcast_to([P, 2 * TOPK, TOPK]), ALU.is_equal))
                    mine()
                    ahead(4 * r + 3)
                    for c in range(2):
                        did(dve.tensor_tensor(unit_c[:, c, :, :], unit_c[:, c, :, :],
                                              unit_if[:, c, :].unsqueeze(1).broadcast_to([P, TOPK, TOPK]), ALU.mult))
                    mine()
                    did(dve.tensor_reduce(chosen[:, 0, bass.ds(u, 1), :].rearrange("p a k -> p (a k)"),
                                          unit_c[:, 0, :, :], AX.X, ALU.add))
                    did(dve.tensor_reduce(chosen[:, 1, bass.ds(u, 1), :].rearrange("p a k -> p (a k)"),
                                          unit_c[:, 1, :, :], AX.X, ALU.add))
                    mine()
                route(0)
                route(1)
                assert mark["n"] == 2 * PER, mark
            step.count = c0 + PER * PH * NT

            step.wait()
            step(dve.tensor_copy(gate_z[:], chosen_s[:, :, 0]))
            step.wait()
            dve.tensor_tensor(chosen_s[:], chosen_s[:], gate_z[:].unsqueeze(2).broadcast_to([P, PH * NT, TOPK]),
                              ALU.subtract).then_inc(shifted, 1)
            rest_table(N1 + HALF + AHEAD, AHEAD)
            dve.wait_ge(gate_exp, 1)
            step(dve.tensor_reduce(gate_z[:], chosen_s[:], AX.X, ALU.add))
            step.wait()
            step(dve.reciprocal(gate_z[:], gate_z[:]))
            step.wait()
            dve.tensor_tensor(chosen_s[:], chosen_s[:], gate_z[:].unsqueeze(2).broadcast_to([P, PH * NT, TOPK]),
                              ALU.mult).then_inc(gate_ready, 1)
            for i in range(1, 4):
                rest_table(N1 + HALF + AHEAD + i, i + AHEAD)

            def one_hot(g, slot, half, first=False):
                if not first:
                    dve.wait_ge(gates_done, g - 1)
                t = g * 4 - half * S
                dve.tensor_tensor(one2[slot][:], iota[:].unsqueeze(1).broadcast_to([P, 4, NK]),
                                  i2T[:, bass.ds(t, 4)].unsqueeze(2).broadcast_to([P, 4, NK]), ALU.is_equal)
                dve.tensor_tensor(same1[slot][:],
                                  iota[:, half * HALF:(half + 1) * HALF].unsqueeze(1).broadcast_to([P, 4, HALF]),
                                  i1T[:, bass.ds(t, 4)].unsqueeze(2).broadcast_to([P, 4, HALF]), ALU.is_equal)\
                    .then_inc(same_ready, 1)

            def apply_gates(g, slot, half):
                dve.wait_ge(gates_done, g + 1)
                h = H[:, half * HALF:(half + 1) * HALF, bass.ds(g * 4 - half * S, 4)].rearrange("p j t -> p t j")
                dve.tensor_tensor(h, psO[:, slot * 512:slot * 512 + 4 * HALF].rearrange("p (t j) -> p t j", j=HALF),
                                  h, ALU.mult).then_inc(gated, 1)
            dve.wait_ge(index_out, 3)
            one_hot(0, 0, 0, True)
            for i in range(4):
                one_hot(i + 1, (i + 1) % 2, 0, i == 0)
                if i == 0:
                    dve.wait_ge(h_out, HALF)
                apply_gates(i, i % 2, 0)
                rest_table(N1 + HALF + DEPTH + AHEAD + i, i + AHEAD)
            with dve.Fori(1, HALF // 4 - 1) as it:
                for i in range(4):
                    one_hot(it * 4 + (i + 1), (i + 1) % 2, 0)
                    apply_gates(it * 4 + i, i % 2, 0)
                    rest_table(it * 4 + (N1 + HALF + DEPTH + AHEAD + i), i + AHEAD)
            for g in range(S // 4 - 4, S // 4):
                one_hot(g + 1, (g + 1) % 2, int(g + 1 == S // 4))
                apply_gates(g, g % 2, 0)

            def rest_act(j, slot, first=False):
                dve.wait_ge(act_hi, j + 1)
                if not first:
                    dve.wait_ge(tile_used, j + (N1 + E_TILES - 3))
                dve.tensor_tensor(a_lo[slot][:], H[:, bass.ds(j, 1), :].rearrange("p a t -> p (a t)"),
                                  a_hi[slot][:].bitcast(FP32), ALU.subtract).then_inc(act_lo, 1)
            for i in range(4):
                rest_act(i, i, True)
            dve.wait_ge(h_out, E_TILES)
            with dve.Fori(1, HALF // 4) as it:
                for i in range(4):
                    j = it * 4 + i
                    one_hot(j + (HALF - 3), (i + 1) % 2, 1)
                    apply_gates(j + (HALF - 4), i % 2, 1)
                    rest_act(j, i)
                    rest_table(j + (N1 + E_TILES - 1), i + AHEAD)
            for g in range(S // 2 - 4, S // 2):
                if g + 1 < S // 2:
                    one_hot(g + 1, (g + 1) % 2, 1)
                apply_gates(g, g % 2, 1)
            with dve.Fori(HALF // 4, E_TILES // 4) as it:
                for i in range(4):
                    j = it * 4 + i
                    rest_act(j, i)
                    rest_table(j + (N1 + E_TILES - 1), i + AHEAD)
            rest_table(N1 + 2 * E_TILES - 1, AHEAD)
            dve.wait_ge(tile_used, N1 + 2 * E_TILES)
            for t in range(NT):
                for c in range(2):
                    z = x2[:, t, c * 512:(c + 1) * 512]
                    step(dve.scalar_tensor_tensor(out=z, in0=z, scalar=ALPHA,
                                                  in1=(psS, psT)[t][:, c * 512:(c + 1) * 512],
                                                  op0=ALU.mult, op1=ALU.add))
                    step.wait()
                    step(dve.bn_stats(stats2[:, t, c, :], z))
                step.wait()
                variance(t, stats2, mv2)
                normalize(2, t, x2[:, t, :], mv2, std2, rstd2, ln_last)

        @block.tensor
        def _(pe):
            def three(out, hi_l, lo_l, hi_r, lo_r, start, stop):
                pe.matmul(out, hi_l, hi_r, start=start, stop=False)
                pe.matmul(out, hi_l, lo_r, start=False, stop=False)
                return pe.matmul(out, lo_l, hi_r, start=False, stop=stop)

            def gemm(n):
                name, kind, i, k0, m, cols, first, last, use = TILES[n]
                act_hi_t, act_lo_t = (b_hi, b_lo) if name in ("mk", "mv", "xq", "pq") else (o_hi, o_lo)
                pe.wait_ge(lo_done, n + 1)
                if name == "mk" and i == 0:
                    pe.wait_ge(split_lo, 2)
                if name in ("wo", "xq", "xo", "pq") and i == 0 and k0 == 0:
                    pe.wait_ge(turn_lo, 2 * (1 + ("wo", "xq", "xo", "pq").index(name)))
                if first:
                    for u in range(use, use + (1 if kind == "T" else NT)):
                        if u >= 2:
                            v, count = TAKEN[u - 2]
                            pe.wait_ge(took[v], count)
                s = n % DEPTH
                if kind == "T":
                    wh = hi[s][:].rearrange("p (k c) -> p k c", c=P)
                    wl = lo[n % EARLY][:].rearrange("p (k c) -> p k c", c=P)
                    for k in range(KD):
                        mm = three(psG[use % 2][:, 0:S], wh[:, k, :], wl[:, k, :], act_hi_t[:, k, :],
                                   act_lo_t[:, k, :], k == 0, k == KD - 1)
                else:
                    for t in range(NT):
                        for kk in range(m):
                            cut = slice(kk * cols, (kk + 1) * cols)
                            k = k0 + kk
                            mm = three(psG[(use + t) % 2][:, 0:cols], act_hi_t[:, k, t * P:(t + 1) * P],
                                       act_lo_t[:, k, t * P:(t + 1) * P], hi[s][:, cut], lo[n % EARLY][:, cut],
                                       k == 0, k == KD - 1)
                mm.then_inc(tile_used, 1)

            def scores(u):
                b, g, t, heads, keys = unit(u)
                if u == 0:
                    pe.wait_ge(const_in, 16 * 6)
                    pe.wait_ge(act_took, TAKEN[TILES[AT["vg"]][8] + 1][1])
                if b == 2:
                    pe.wait_ge(cmp_out, 1)
                    pe.wait_ge(exp_done, u)
                    for h in range(NH):
                        at = h // REP * HD
                        col = h // REP * 512 + h % REP * 16
                        mm = pe.matmul(psS[:, col:col + NC], qT[at:at + HD, h % REP, t * P:(t + 1) * P],
                                       kcmp[at:at + HD, :], start=True, stop=True)
                    mm.then_inc(s_done, 1)
                    return
                if u:
                    pe.wait_ge(exp_done, u)
                if b == 3:
                    if u == XU:
                        pe.wait_ge(turn_lo, 4)
                        pe.wait_ge(act_took, TAKEN[TILES[AT["xq"] + KD - 1][8]][1])
                    for h in range(XH):
                        for kk in range(2):
                            mm = pe.matmul(psS[:, h * S:(h + 1) * S], xq[:, 2 * h + kk, t * P:(t + 1) * P],
                                           xk[:, 2 * h + kk, :], start=kk == 0, stop=kk == 1)
                    mm.then_inc(s_done, 1)
                    return
                for r in range(REP):
                    for kb in range(t + 1):
                        out = psS[:, r * S + kb * P:r * S + (kb + 1) * P]
                        diagonal = kb == t
                        mm = pe.matmul(out, qT[g * HD:(g + 1) * HD, r, t * P:(t + 1) * P],
                                       kT[b][g * HD:(g + 1) * HD, kb * P:(kb + 1) * P], start=True, stop=not diagonal)
                        if diagonal:
                            mm = pe.matmul(out, identb[:], causal[:], start=False, stop=True)
                mm.then_inc(s_done, 1)

            def turn_probs(u):
                b, g, t, heads, keys = unit(u)
                pe.wait_ge(exp_done, u + 1)
                if u:
                    pe.wait_ge(probsT_ready, u)
                if u == XU:
                    pe.wait_ge(turn_lo, 4)
                if b == 2:
                    for h in range(NH):
                        mm = pe.transpose(psT[0:NC, h * P:(h + 1) * P], probs[:, h * NC:(h + 1) * NC], ident[:])
                else:
                    kbs = keys // P
                    for r in range(heads):
                        for kb in range(kbs):
                            at = (r * kbs + kb) * P
                            mm = pe.transpose(psT[:, at:at + P], probs[:, r * S + kb * P:r * S + (kb + 1) * P],
                                              ident[:])
                mm.then_inc(turned, 1)

            def values(u):
                b, g, t, heads, keys = unit(u)
                pe.wait_ge(probsT_ready, u + 1)
                if u:
                    pe.wait_ge(combined, u)
                if u == XU:
                    pe.wait_ge(read_out_ready, NT)
                if b == 2:
                    for h in range(NH):
                        gg = h // REP
                        mm = pe.matmul(psO[:, h * HD:(h + 1) * HD], probsT[0:NC, h * P:(h + 1) * P],
                                       vcmp[:, gg * HD:(gg + 1) * HD], start=True, stop=True)
                elif b == 3:
                    for h in range(XH):
                        for kb in range(2):
                            mm = pe.matmul(psO[:, h * 256:(h + 1) * 256],
                                           probsT[:, (h * 2 + kb) * P:(h * 2 + kb + 1) * P],
                                           xv[:, kb, h * 256:(h + 1) * 256], start=kb == 0, stop=kb == 1)
                else:
                    for r in range(REP):
                        for kb in range(t + 1):
                            at = (r * (t + 1) + kb) * P
                            mm = pe.matmul(psO[:, r * HD:(r + 1) * HD], probsT[:, at:at + P],
                                           vg[:, kb, b * P + g * HD:b * P + (g + 1) * HD],
                                           start=kb == 0, stop=kb == t)
                mm.then_inc(pv_done, 1)

            pe.wait_ge(split_lo, 1)
            for what, i in ORDER:
                if what == "gemm":
                    gemm(i)
                elif what == "hidden":
                    pe.wait_ge(blocks_ready, 1)
                    for kv in range(2):
                        for m in range(CB // 2):
                            mm = pe.matmul(psM[:, kv * G * NC:(kv + 1) * G * NC], w1[:, kv, m, :], blk[:, kv, m, :],
                                           start=m == 0, stop=m == CB // 2 - 1)
                    mm.then_inc(hidden_done, 1)
                elif what == "compressed":
                    pe.wait_ge(gelu_ready, 1)
                    for g in range(G):
                        pe.matmul(psM[g * HD:(g + 1) * HD, 128:128 + NC], w2[:, 0, :],
                                  hz[:, g * NC:(g + 1) * NC], start=True, stop=True)
                    for g in range(G):
                        mm = pe.matmul(psM[0:NC, 256 + g * HD:256 + (g + 1) * HD],
                                       hz[:, (G + g) * NC:(G + g + 1) * NC], w2[:, 1, :], start=True, stop=True)
                    mm.then_inc(cmp_done, 1)
                elif what == "scores":
                    scores(i)
                elif what == "turn_probs":
                    turn_probs(i)
                elif what == "values":
                    values(i)
                elif what == "level":
                    if i == 0:
                        pe.wait_ge(decay_ready, 1)
                        pe.wait_ge(exp_done, XU)
                        pe.wait_ge(probsT_ready, XU)
                    if i >= 2:
                        pe.wait_ge(factors_ready, i - 1)
                        pe.wait_ge(level_merged, i - 1)
                    X = (psS, psT)[i % 2]
                    if i == 8:
                        for h in range(HH):
                            mm = pe.matmul(X[:, h * P:(h + 1) * P], KB[:, h, 0:P], QF[:, h, P:S], start=True, stop=True)
                    else:
                        q = hq if i == 0 else QF
                        for h in range(HH):
                            for t in range(NT):
                                at = (h * NT + t) * P
                                mm = pe.matmul(X[:, at:at + P], KB[:, h, t * P:(t + 1) * P],
                                               q[:, h, t * P:(t + 1) * P], start=True, stop=True)
                    mm.then_inc(level_done, 1)
                elif what == "read_out":
                    pe.wait_ge(level_merged, 8)
                    pe.wait_ge(off_ready, 1)
                    pe.wait_ge(combined, XU)
                    for h in range(HH):
                        out = psO[:, i * 512 + h * P:i * 512 + (h + 1) * P]
                        mm = pe.matmul(out, att[:, h, i, :], hv[:, i, h * P:(h + 1) * P], start=True, stop=i == 0)
                        if i == 1:
                            mm = pe.matmul(out, att_off[:, h, :], hv[:, 0, h * P:(h + 1) * P], start=False, stop=True)
                    mm.then_inc(read_done, 1)
                elif what == "turn":
                    t = i % 2
                    if i == 0:
                        pe.wait_ge(rec_ready, 1)
                    elif i in (2, 3):
                        pe.wait_ge(norm_ready, i - 1)
                        pe.wait_ge(turn_lo, i - 1)
                    elif i in (4, 5):
                        pe.wait_ge(combined, XU + i - 3)
                        pe.wait_ge(exp_done, XU + NT)
                        pe.wait_ge(probsT_ready, XU + NT)
                    elif i in (6, 7):
                        pe.wait_ge(norm_ready, i - 3)
                        pe.wait_ge(turn_lo, i - 1)
                    for k in range(KD):
                        if i < 2:
                            src = (o_acc if k < 4 else oh)[:, t, k % 4 * P:(k % 4 + 1) * P]
                        else:
                            src = (x1, xo, x2)[i // 2 - 1][:, t, k * P:(k + 1) * P]
                        mm = pe.transpose((psS, psT)[t][:, k * P:(k + 1) * P], src, ident[:])
                    mm.then_inc(turn_done, 1)
            pe.wait_ge(subk_in, 32)
            pe.wait_ge(act_took, TAKEN_ALL[0])
            pe.wait_ge(combined, XU + NT)
            for u in range(PH * NT):
                t, h = u // PH, u % PH
                if u >= 4:
                    pe.wait_ge(score_out, u - 3)
                mm = pe.matmul((psO, psS)[u % 4 // 2][:, u % 2 * 512:u % 2 * 512 + S], qryT[:, h, t * P:(t + 1) * P], subk[:, h, :],
                               start=True, stop=True)
                mm.then_inc(score_done, 1)

            def down(j, i, first):
                n = j + N1
                s = (N1 + i) % DEPTH
                pe.wait_ge(lo_done, n + 1)
                if not first:
                    pe.wait_ge(h_out, j - 1)
                wh = hi[s][:].rearrange("p (k c) -> p k c", c=P)
                wl = lo[s][:].rearrange("p (k c) -> p k c", c=P)
                for k in range(KD):
                    mm = three(psG[i % 2][:, 0:S], wh[:, k, :], wl[:, k, :], b_hi[:, k, :], b_lo[:, k, :],
                               k == 0, k == KD - 1)
                mm.then_inc(tile_used, 1)
            def gates(g, slot, first=False):
                pe.wait_ge(one_ready, g + 1)
                if not first:
                    pe.wait_ge(gated, g - 1)
                for i in range(4):
                    mm = pe.matmul(psO[:, slot * 512 + i * HALF:slot * 512 + (i + 1) * HALF], one2[slot][:, i, :],
                                   one1[slot][:, i, :], start=True, stop=True)
                mm.then_inc(gates_done, 1)
            for j in range(4):
                down(j, j, j < 2)
            with pe.Fori(1, HALF // 4) as it:
                for i in range(4):
                    down(it * 4 + i, i, False)
            for i in range(4):
                down(HALF + i, i, False)
                if i == 1:
                    pe.wait_ge(gate_ready, 1)
                    pe.wait_ge(score_out, PH * NT)
                    for q in range(3):
                        for t in range(NT):
                            src = (chosen[:, 0], chosen[:, 1], chosen_s[:])[q]
                            mm = pe.transpose(psO[:, q * S + t * P:q * S + (t + 1) * P],
                                              src[:, t * PH:(t + 1) * PH, :].rearrange("p h k -> p (h k)"), ident[:])
                        mm.then_inc(index_done, 1)
            for i in range(4):
                down(HALF + 4 + i, i, False)
                if i == 0:
                    pe.wait_ge(index_out, 3)
                gates(i, i % 2, i < 2)
            with pe.Fori(1, HALF // 4 - 1) as it:
                for i in range(4):
                    down(it * 4 + (HALF + 4 + i), i, False)
                    gates(it * 4 + i, i % 2)
            for g in range(S // 4 - 4, S // 4):
                gates(g, g % 2)

            def up(j, i, start, stop):
                pe.wait_ge(lo_done, j + (N1 + E_TILES + 1))
                pe.wait_ge(act_lo, j + 1)
                s = (N1 + i) % DEPTH
                for t in range(NT):
                    cut = slice(t * P, (t + 1) * P)
                    for left, right, st, sp in ((a_hi[i], hi[s], start, False), (a_hi[i], lo[s], False, False),
                                                (a_lo[i], hi[s], False, stop)):
                        for c in range(2):
                            mm = pe.matmul((psS, psT)[t][:, c * 512:(c + 1) * 512], left[:, cut],
                                           right[:, c * 512:(c + 1) * 512], start=st, stop=sp)
                mm.then_inc(tile_used, 1)
            def round_of(it):
                for i in range(4):
                    up(it * 4 + i, i, False, False)
                    gates(it * 4 + (HALF + i), i % 2)
            for i in range(4):
                up(i, i, i == 0, False)
                gates(HALF + i, i % 2)
            with pe.Fori(1, HALF // 4 - 1) as it:
                round_of(it)
            for i in range(4):
                if i < 2:
                    gates(S // 2 - 4 + 2 * i, 0)
                    gates(S // 2 - 3 + 2 * i, 1)
                up(HALF - 4 + i, i, False, False)
            with pe.Fori(HALF // 4, E_TILES // 4 - 1) as it:
                for i in range(4):
                    up(it * 4 + i, i, False, False)
            for i in range(4):
                up(E_TILES - 4 + i, i, False, i == 3)


def tile_of(w):
    return w.reshape(KD, P, P).transpose(1, 0, 2).reshape(P, D)


def stream(w_in, w_out, xa_wq, xa_wkv, xa_wo, peer_wq):
    cuts = np.cumsum([512] + [P] * 6 + [24] + [512] * 4)
    qa, kc, vc, ks, vs, kw, vw, ga, qb, fb, ib, gb = np.split(w_in, cuts[:-1], axis=1)
    qa = qa.reshape(D, G, REP, HD).transpose(0, 2, 1, 3).reshape(D, 512)
    source = {"kc": kc, "vc": vc, "ks": ks, "kw": kw, "q": qa, "vg": np.concatenate([vs, vw, ga], axis=1),
              "hq": qb, "hf": fb, "hv": ib, "hg": gb, "mk": xa_wkv[:, :D], "mv": xa_wkv[:, D:], "wo": w_out,
              "xq": xa_wq, "xo": xa_wo, "pq": peer_wq}
    out = np.zeros((N1, P, D), np.float32)
    for n, (name, kind, i, k0, m, cols, first, last, use) in enumerate(TILES):
        w = source[name][:, i * cols:(i + 1) * cols]
        if kind == "T":
            out[n] = tile_of(w)
        else:
            out[n, :, :m * cols] = w[k0 * P:(k0 + m) * P].reshape(m, P, cols).transpose(1, 0, 2).reshape(P, m * cols)
    return out


def constants():
    bf = np.dtype("bfloat16")
    i = np.arange(P)
    s, t = i[:, None], i[None, :]
    masks = np.zeros((P, 8, P), np.float32)
    masks[:, 0] = s == t
    for j in range(1, 8):
        masks[:, j] = (((s ^ t) >> (j - 1)) == 1) & (t > s)
    tok = (np.arange(NT)[None, :] * P + i[:, None])
    valid = (np.arange(NC) * CS + CB - 1)[None, None, :] <= tok[:, :, None]
    return {"ident": np.eye(P, dtype=np.float32), "identb": np.eye(P).astype(bf),
            "iota": np.broadcast_to(i, (P, P)).astype(np.float32),
            "iota16": np.broadcast_to(np.arange(TOPK), (P, TOPK)).astype(np.float32),
            "causal": np.where(t > s, -1e30, 0.0).astype(bf),
            "cmp_mask": np.where(valid, 0.0, -1e30).astype(np.float32),
            "cmp_any": valid.any(-1).astype(np.float32),
            "level_mask": masks.astype(bf)}


def kernel(x, mem, w_in, cmp_pos, cmp_w1, cmp_w2, hgrn_lb_logits, hgrn_norm_w, w_out,
           xa_wq, xa_wkv, xa_wo, peer_wq, peer_subkeys, peer_down, peer_up, ln_g, ln_b):
    import concourse.bacc as bacc
    from concourse.bass_utils import run_bass_kernel_spmd

    f = lambda v: np.asarray(v)
    x, mem = f(x)[0], f(mem)[0]
    sub = f(peer_subkeys)[0]
    subk = np.zeros((P, PH, 2 * NK), np.float32)
    for c in range(2):
        subk[c * 64:(c + 1) * 64, :, c * NK:(c + 1) * NK] = sub[:, c].transpose(2, 0, 1)
    arrays = {
        "xT": x.T.reshape(KD, P, S).transpose(1, 0, 2),
        "memT": mem.T.reshape(KD, P, S).transpose(1, 0, 2),
        "x_tok": x.reshape(NT, P, D).transpose(1, 0, 2),
        "w_stream": stream(f(w_in)[0], f(w_out)[0], f(xa_wq)[0], f(xa_wkv)[0], f(xa_wo)[0], f(peer_wq)[0]),
        "down": f(peer_down)[0].reshape(E_TILES, P, KD, P).transpose(0, 3, 2, 1).reshape(E_TILES, P, D),
        "up": f(peer_up)[0].reshape(E_TILES, P, D),
        "w1": f(cmp_w1)[0].reshape(2, CB // 2, P, P).transpose(2, 0, 1, 3),
        "w2": f(cmp_w2)[0].transpose(1, 0, 2),
        "pos": f(cmp_pos)[0].reshape(2, CB // 2, P).transpose(2, 0, 1),
        "lb": f(hgrn_lb_logits).transpose(2, 0, 1),
        "norm_w": f(hgrn_norm_w)[0].reshape(1, 512),
        "subk": subk,
        "ln_g": f(ln_g)[0], "ln_b": f(ln_b)[0],
        **constants(),
    }
    arrays = {k: np.ascontiguousarray(v) for k, v in arrays.items()}
    nc = bacc.Bacc("TRN2", target_bir_lowering=False, num_devices=1)
    aps = {k: nc.dram_tensor(f"in_{k}", v.shape, mybir.dt.from_np(v.dtype), kind="ExternalInput").ap()
           for k, v in arrays.items()}
    aps["out"] = nc.dram_tensor("out_x", (S, D), FP32, kind="ExternalOutput").ap()
    build(nc, aps)
    r = run_bass_kernel_spmd(nc, [{f"in_{k}": v for k, v in arrays.items()}], core_ids=[0])
    return r.results[0]["out_x"].reshape(1, S, D)
```

```python
import numpy as np
import concourse.bass as bass
import concourse.mybir as mybir

FP32 = mybir.dt.float32
F32R = mybir.dt.float32r
BF16 = mybir.dt.bfloat16
F16 = mybir.dt.float16
U32 = mybir.dt.uint32
U16 = mybir.dt.uint16
ACT = mybir.ActivationFunctionType
ALU = mybir.AluOpType
AX = mybir.AxisListType

P = 128
D = 1024
S = 256
NT = S // P
KD = D // P
HD = 64
NH = 8
G = 2
REP = NH // G
CB, CS = 32, 16
NC = (S - CB) // CS + 1
HH = 4
XH = 4
PH = 8
TOPK = 16
NK = 128
E_TILES = NK * NK // P
ALPHA = 2.0 ** 0.25
EPS = 1e-5
VG = 2 * P + 3 * NH

RUNS = [("kc", "T", 0, 1), ("vc", "T", 0, 1), ("ks", "T", 0, 1), ("kw", "T", 0, 1), ("q", "T", 0, 4),
        ("vg", "R", 0, 1), ("hq", "T", 0, HH), ("hf", "T", 0, HH), ("hv", "R", 0, 1), ("hg", "R", 0, 1),
        ("mk", "T", 0, KD), ("mv", "R", 0, 1), ("wo", "R", 0, 2), ("mv", "R", 1, 1), ("xq", "T", 0, KD),
        ("xo", "R", 0, 2), ("pq", "T", 0, KD)]


def plan():
    tiles, at, use = [], {}, 0
    for name, kind, i0, count in RUNS:
        at.setdefault(name, len(tiles))
        for i in range(i0, i0 + count):
            if kind == "T":
                tiles.append((name, kind, i, 0, KD, P, True, True, use))
                use += 1
            else:
                cols = VG if name == "vg" else 512
                per = D // cols
                k = 0
                while k < KD:
                    m = min(per, KD - k)
                    tiles.append((name, kind, i, k, m, cols, k == 0, k + m == KD, use))
                    k += m
                use += NT
    return tiles, at, use


TILES, AT, USES = plan()
N1 = len(TILES)
DEPTH = 4
EARLY = 8
AHEAD = 3
GATE_SCALE = 2.0 ** 15
HALF = E_TILES // 2
EVEN = HALF - 12
VECTOR_READS = ("wo", "xo")


def consumers():
    count, out = [0, 0], []
    for name, kind, i, k0, m, cols, first, last, use in TILES:
        if first:
            v = int(name in VECTOR_READS)
            for _ in range(1 if kind == "T" else NT):
                count[v] += 1
                out.append((v, count[v]))
    return out, count


TAKEN, TAKEN_ALL = consumers()


def banks():
    where = []
    for name, kind, i, k0, m, cols, first, last, use in TILES:
        if first:
            for t in range(1 if kind == "T" else NT):
                where.append(2 + t if name in VECTOR_READS and i == 1 else (use + t) % 2)
    before = [max((v for v in range(u) if where[v] == where[u]), default=None) for u in range(len(where))]
    return where, before


BANK, BEFORE = banks()
FIRST_HALVES = [n for n, (name, *_, last, use) in enumerate(TILES) if name in VECTOR_READS and last]

UNITS = [(b, g, t) for b in range(2) for g in range(G) for t in range(NT)]


def order():
    out = []
    n = 0

    def gemm(k):
        nonlocal n
        for _ in range(k):
            out.append(("gemm", n))
            n += 1
    gemm(4)
    out.append(("blocks", 0))
    gemm(AT["hq"] - 4)
    out.append(("hidden", 0))
    gemm(1)
    out.append(("gelu", 0))
    gemm(1)
    out.append(("compressed", 0))
    last = len(UNITS) + NT - 1
    out.append(("scores", 0))
    for u in range(last + 1):
        gemm(2 if u < 2 else 1)
        if u >= 2:
            out.append(("level", (u - 2, 0)))
        out.append(("turn_probs", u))
        if u + 1 < last:
            out.append(("scores", u + 1))
        gemm(1)
        if u == 1:
            assert n == AT["hv"]
            out.append(("decay", 0))
        if u >= 2:
            out.append(("level", (u - 2, 1)))
        out.append(("values", u))
        if u + 1 == last:
            out.append(("scores", last))
    gemm(1)
    out += [("level", (8, 0)), ("read_out", 0), ("read_out", 1), ("rms", 0)]
    gemm(2)
    out += [("turn", 0), ("turn", 1)]
    gemm(AT["wo"] - n)
    gemm(2 * KD // 2)
    out += [("norm", (0, 0)), ("norm", (0, 1))]
    gemm(2)
    out.append(("turn", 2))
    gemm(1)
    out.append(("turn", 3))
    gemm(AT["xq"] - n)
    gemm(AT["xo"] - n)
    out += [("scores", 10), ("turn_probs", 10), ("scores", 11), ("values", 10),
            ("turn_probs", 11), ("values", 11), ("turn", 4), ("turn", 5)]
    gemm(AT["pq"] - n)
    out += [("norm", (1, 0)), ("norm", (1, 1)), ("turn", 6), ("turn", 7)]
    gemm(1)
    for h in range(PH):
        gemm(min(1, N1 - n))
        out.append(("route", h))
    return out


ORDER = order()


class Steps:

    def __init__(self, engine, semaphore):
        self.engine, self.semaphore, self.count = engine, semaphore, 0

    def __call__(self, instruction):
        instruction.then_inc(self.semaphore, 1)
        self.count += 1

    def wait(self):
        self.engine.wait_ge(self.semaphore, self.count)


def build(nc, a):
    from contextlib import ExitStack
    ctx = ExitStack()
    with ctx:
        base = -(-nc.sbuf_base // 32) * 32
        place = {"at": base}

        def sb(name, shape, dt=FP32, at=None):
            size = int(np.prod(shape[1:])) * {FP32: 4, F32R: 4, BF16: 2, F16: 2, U32: 4}[dt]
            size = -(-size // 32) * 32
            where = place["at"] if at is None else at
            if at is None:
                place["at"] += size
            return nc.alloc_sbuf_tensor_at(name, shape, dt, offset=where)

        def ps(name, shape, dt=FP32):
            return ctx.enter_context(nc.psum_tensor(name, shape, dt))

        def sem(name):
            return ctx.enter_context(nc.semaphore(name))

        ident = sb("ident", [P, P])
        identb = sb("identb", [P, P], BF16)
        iota = sb("iota", [P, P], F16)
        x2 = sb("x2", [P, NT, D])
        B_at = place["at"]
        b_hi = sb("b_hi", [P, KD, S], F32R)
        b_lo = sb("b_lo", [P, KD, S], F32R)
        hi = [sb(f"hi{i}", [P, D], F32R) for i in range(DEPTH)]
        raw, lo = [], []

        def raw_slot(i):
            at = place["at"]
            raw.append(sb(f"raw{i}", [P, D]))
            lo.append(sb(f"lo{i}", [P, D], F32R, at=at))
        for i in range(DEPTH):
            raw_slot(i)
        R_at = place["at"]

        H = sb("H", [P, E_TILES, S])
        late_at = place["at"]
        score_at = R_at + (E_TILES - 14) * S * 4
        route_s = sb("route_s", [P, PH * NT, 2 * NK], at=score_at)
        place["at"] = late_at + 2 * 1024
        chosen = sb("chosen", [P, 2, PH * NT, TOPK])
        chosen_s = sb("chosen_s", [P, PH * NT, TOPK])
        i1T = sb("i1T", [P, S], F16)
        i2T = sb("i2T", [P, S], F16)
        gT = sb("gT", [P, S])
        g_hi = sb("g_hi", [P, S], F16)
        g_lo = sb("g_lo", [P, S], F16)
        route_at = place["at"]
        unit_s = sb("unit_s", [P, 2, NK])
        unit_w = sb("unit_w", [P, 2, NK])
        unit_c = sb("unit_c", [P, 2, TOPK, TOPK])
        unit_m = sb("unit_m", [P, 2, TOPK])
        unit_i = sb("unit_i", [P, 2, TOPK], U32)
        unit_if = sb("unit_if", [P, 2, TOPK])
        unit_t = sb("unit_t", [P, TOPK])
        unit_p = sb("unit_p", [P, TOPK], U32)
        unit_ab = sb("unit_ab", [P, 2, TOPK], U32)
        unit_abf = sb("unit_abf", [P, 2, TOPK])
        iota16 = sb("iota16", [P, TOPK])
        gate_z = sb("gate_z", [P, PH * NT], at=route_at)
        hold_v = sb("hold_v", [P, 8])
        warm = sb("warm", [P, 8])
        one2 = [sb(f"one2_{i}", [P, 4, NK], F16) for i in range(2)]
        same1 = [sb(f"same1_{i}", [P, 4, HALF], F16) for i in range(2)]
        one1_hi = [sb(f"one1_hi{i}", [P, 4, HALF], F16) for i in range(2)]
        one1_lo = [sb(f"one1_lo{i}", [P, 4, HALF], F16) for i in range(2)]
        assert place["at"] <= nc.sbuf_usable_end, place["at"] - nc.sbuf_usable_end
        ln_last = sb("ln_last", [P, 2, D], at=B_at)
        a_hi = [sb(f"act_hi{i}", [P, S], F32R, at=B_at + 8192 + 1024 * i) for i in range(4)]
        a_lo = [sb(f"act_lo{i}", [P, S], F32R, at=B_at + 12288 + 1024 * i) for i in range(4)]

        place["at"] = R_at
        for i in range(DEPTH, EARLY):
            raw_slot(i)
        o_hi = sb("o_hi", [P, KD, S], F32R)
        o_lo = sb("o_lo", [P, KD, S], F32R)
        ln_gb = sb("ln_gb", [P, 2, D])
        xk_at = place["at"]
        xk = sb("xk", [P, KD, S])
        xT = sb("xT", [P, KD, S], at=xk_at)
        xq_at = place["at"]
        xq = sb("xq", [P, KD, S])
        memT = sb("memT", [P, KD, S], at=xq_at)
        xv_at = place["at"]
        xv = sb("xv", [P, NT, D])
        hg_t = sb("hg_t", [P, NT, 512], at=xv_at)
        qT = sb("qT", [P, REP, S])
        kT = [sb(f"kT{i}", [P, S]) for i in range(2)]
        vg = sb("vg", [P, NT, VG])
        gate = sb("gate", [P, NT, 3 * NH])
        kv_at = place["at"]
        kvc = sb("kvc", [P, 2, S])
        kcp = sb("kcp", [P, 2, G, S])
        blk = sb("blk", [P, 2, CB // 2, G * NC])
        place["at"] = max(place["at"], kv_at + 8192)
        x_tok = sb("x_tok", [P, NT, D], at=kv_at)
        w1_at = place["at"]
        w1 = sb("w1", [P, 2, CB // 2, P])
        x1 = sb("x1", [P, NT, D], at=w1_at)
        xo = sb("xo", [P, NT, D], at=w1_at + 8192)
        w2 = sb("w2", [P, 2, HD])
        pos = sb("pos", [P, 2, CB // 2])
        hx = sb("hx", [P, 2 * G * NC])
        hy = sb("hy", [P, 2 * G * NC])
        hz = sb("hz", [P, 2 * G * NC])
        kcmp = sb("kcmp", [P, NC])
        vcmp = sb("vcmp", [NC, P])
        probs = sb("probs", [P, 4 * S])
        probsT = sb("probsT", [P, 4 * S])
        neg_max = sb("neg_max", [P, 2, NH])
        row_max = sb("row_max", [P, NH])
        row_sum = sb("row_sum", [P, 2, NH])
        coef = sb("coef", [P, NH])
        cmp_s = sb("cmp_s", [P, NH, NC])
        o_acc = sb("o_acc", [P, NT, 512])
        o_tmp = sb("o_tmp", [P, 512])
        causal = sb("causal", [P, P], BF16)
        cmp_mask = sb("cmp_mask", [P, NT, NC])
        cmp_any = sb("cmp_any", [P, NT])
        hq_at = place["at"]
        hq = sb("hq", [P, HH, S])
        oh = sb("oh", [P, NT, 512], at=hq_at)
        QF = sb("QF", [P, HH, S])
        KB = sb("KB", [P, HH, S])
        Fa = sb("Fa", [P, HH * S])
        Fb = sb("Fb", [P, HH * S // 2])
        lb = sb("lb", [P, 8, HH])
        level_mask = sb("level_mask", [P, 8, P], BF16, at=w1_at + 8192)
        att = sb("att", [P, HH, NT, P])
        att_off = sb("att_off", [P, HH, P])
        hv = sb("hv", [P, NT, 512])
        hg = sb("hg", [P, NT, 512])
        norm_w = sb("norm_w", [P, 512])
        stats = sb("stats", [P, NT, 2, 6])
        mv = sb("mv", [P, NT, 2])
        std = sb("std", [P, NT, HH])
        rstd = sb("rstd", [P, NT, HH])
        assert place["at"] <= nc.sbuf_usable_end, place["at"] - nc.sbuf_usable_end
        qryT = sb("qryT", [P, PH, S], at=xk_at)
        subk = sb("subk", [P, PH, 2 * NK], at=kv_at)
        stats2 = sb("stats2", [P, NT, 2, 6], at=route_at)
        mv2 = sb("mv2", [P, NT, 2], at=route_at + 128)
        std2 = sb("std2", [P, NT, HH], at=route_at + 192)
        rstd2 = sb("rstd2", [P, NT, HH], at=route_at + 256)

        psG = [ps(f"psG{i}", [P, 512]) for i in range(2)]
        psS = ps("psS", [P, 1024])
        psT = ps("psT", [P, 1024])
        psO = ps("psO", [P, 1024])
        psM = psO[:, 512:1024]
        bank = (psG[0][:], psG[1][:], psO[:, 0:512], psO[:, 512:1024])

        raw_in = [sem(f"raw_in{i}") for i in range(EARLY)]
        table_in = [sem(f"table_in{i}") for i in range(DEPTH)]
        table_lo = [sem(f"table_lo{i}") for i in range(DEPTH)]
        hi_done, lo_done, tile_used = sem("hi_done"), sem("lo_done"), sem("tile_used")
        x_in = [sem(f"x_in{i}") for i in range(2)]
        mem_in, const_in, comp_in = sem("mem_in"), sem("const_in"), sem("comp_in")
        rec_in, xtok_in, subk_in, ln_in = sem("rec_in"), sem("xtok_in"), sem("subk_in"), sem("ln_in")
        shift_in, out_done = sem("shift_in"), sem("out_done")
        mask_in = sem("mask_in")
        split_hi, split_lo = sem("split_hi"), sem("split_lo")
        act_took, dve_took = sem("act_took"), sem("dve_took")
        took = (act_took, dve_took)
        blocks_ready, hidden_done, hidden_out, tanh_done, gelu_ready = (
            sem("blocks_ready"), sem("hidden_done"), sem("hidden_out"), sem("tanh_done"), sem("gelu_ready"))
        cmp_done, cmp_out = sem("cmp_done"), sem("cmp_out")
        s_done, max_done, exp_done, turned, probsT_ready, pv_done, combined = (
            sem("s_done"), sem("max_done"), sem("exp_done"), sem("turned"), sem("probsT_ready"),
            sem("pv_done"), sem("combined"))
        lb_exp, lb_max = sem("lb_exp"), sem("lb_max")
        att_zero, decay_ready, level_done, level_merged, factors_ready = (
            sem("att_zero"), sem("decay_ready"), sem("level_done"), sem("level_merged"), sem("factors_ready"))
        off_ready, read_done, read_out_ready, var_ready, std_ready, rec_ready = (
            sem("off_ready"), sem("read_done"), sem("read_out_ready"), sem("var_ready"), sem("std_ready"),
            sem("rec_ready"))
        turn_done, turn_hi, turn_lo = sem("turn_done"), sem("turn_hi"), sem("turn_lo")
        norm_ready = sem("norm_ready")
        score_done, score_out = sem("score_done"), sem("score_out")
        h_out, routed = sem("h_out"), sem("routed")
        shifted, gate_exp, gate_ready, index_done, index_out = (
            sem("shifted"), sem("gate_exp"), sem("gate_ready"), sem("index_done"), sem("index_out"))
        same_ready, one_ready, gates_done, gated = (
            sem("same_ready"), sem("one_ready"), sem("gates_done"), sem("gated"))
        act_hi, act_lo = sem("act_hi"), sem("act_lo")
        dve_step, pool_step, silu_ready = sem("dve_step"), sem("pool_step"), sem("silu_ready")
        first_half = sem("first_half")
        block = ctx.enter_context(nc.Block())

        XU = len(UNITS) + NT

        def unit(u):
            if u < len(UNITS):
                b, g, t = UNITS[u]
                return b, g, t, REP, P * (t + 1)
            if u < XU:
                return 2, 0, u - len(UNITS), NH, NC
            return 3, 0, u - XU, XH, S

        @block.sync
        def _(sp):
            for i in range(2):
                half = slice(i * KD // 2, (i + 1) * KD // 2)
                sp.dma_start(xT[:, half, :], a["xT"][:, half, :]).then_inc(x_in[i], 16)
            for n in range(N1):
                if n >= EARLY:
                    sp.wait_ge(tile_used, n - EARLY + 1)
                sp.dma_start(raw[n % EARLY][:], a["w_stream"][n]).then_inc(raw_in[n % EARLY], 16)
                if n == 16:
                    sp.dma_start(memT[:], a["memT"]).then_inc(mem_in, 16)

            def table(name, j, i, used):
                sp.wait_ge(tile_used, used)
                sp.dma_start(raw[(N1 + i) % DEPTH][:], a[name][j]).then_inc(table_in[i], 16)
            with sp.Fori(0, E_TILES // DEPTH) as it:
                for i in range(DEPTH):
                    table("down", it * DEPTH + i, i, it * DEPTH + (N1 + i - DEPTH + 1))
            with sp.Fori(0, E_TILES // DEPTH) as it:
                for i in range(DEPTH):
                    table("up", it * DEPTH + i, i, it * DEPTH + (N1 + E_TILES + i - DEPTH + 1))
            for t in range(NT):
                sp.wait_ge(norm_ready, 2 * NT + t + 1)
                sp.dma_start(a["out"][t * P:(t + 1) * P, :], x2[:, t, :]).then_inc(out_done, 16)
            sp.wait_ge(out_done, 16 * NT)

        @block.gpsimd
        def _(pool):
            for dst, name in ((ident, "ident"), (identb, "identb"), (iota, "iota"), (causal, "causal"),
                              (cmp_mask, "cmp_mask"), (cmp_any, "cmp_any")):
                pool.dma_start(dst[:], a[name]).then_inc(const_in, 16)
            pool.dma_start(lb[:, 0:2, :], a["lb"]).then_inc(rec_in, 16)
            pool.dma_start(norm_w[:], a["norm_w"].broadcast_to([P, 512])).then_inc(rec_in, 16)
            pool.memset(att[:], 0.0).then_inc(att_zero, 1)
            pool.wait_ge(lo_done, 3)
            for dst, name in ((pos, "pos"), (w1, "w1"), (w2, "w2")):
                pool.dma_start(dst[:], a[name]).then_inc(comp_in, 16)
            pool.wait_ge(act_took, 2)
            for g in range(G):
                for par in range(2):
                    pool.dma_start(kcp[par * HD:(par + 1) * HD, :, g, 0:S - par],
                                   kvc[g * HD:(g + 1) * HD, :, par:S]).then_inc(shift_in, 16)
            pool.wait_ge(hidden_done, 1)
            pool.dma_start(level_mask[:], a["level_mask"]).then_inc(mask_in, 16)
            pool.dma_start(x_tok[:], a["x_tok"]).then_inc(xtok_in, 16)
            for i, name in enumerate(("ln_g", "ln_b")):
                pool.dma_start(ln_gb[:, i, :], a[name][0:1, :].broadcast_to([P, D])).then_inc(ln_in, 16)
            pool.wait_ge(act_took, TAKEN[TILES[AT["hg"]][8] + 1][1])
            pool.wait_ge(rec_in, 32)
            pool.tensor_scalar(hg_t[:], hg_t[:], 1.0, 0.5, ALU.add, ALU.mult).then_inc(pool_step, 1)
            pool.tensor_tensor(hg[:], hg[:], norm_w[:].unsqueeze(1).broadcast_to([P, NT, 512]), ALU.mult)\
                .then_inc(pool_step, 1)
            pool.wait_ge(pool_step, 2)
            pool.tensor_tensor(hg[:], hg[:], hg_t[:], ALU.mult).then_inc(silu_ready, 1)
            pool.wait_ge(norm_ready, NT)
            for i, name in enumerate(("ln_g", "ln_b")):
                pool.dma_start(ln_gb[:, i, :], a[name][1:2, :].broadcast_to([P, D])).then_inc(ln_in, 16)
            pool.dma_start(subk[:], a["subk"]).then_inc(subk_in, 16)
            pool.dma_start(iota16[:], a["iota16"]).then_inc(subk_in, 16)

            def rest_table(q, i):
                s = (N1 + i) % DEPTH
                pool.wait_ge(hi_done, q + (N1 + 1))
                pool.tensor_tensor(lo[s][:], raw[s][:], hi[s][:].bitcast(FP32), ALU.subtract)\
                    .then_inc(table_lo[i], DEPTH)
            with pool.Fori(0, HALF // DEPTH) as it:
                for i in (0, 2, 3):
                    rest_table(it * DEPTH + i, i)
            with pool.Fori(HALF // DEPTH, E_TILES // DEPTH + 1) as it:
                for i in range(0, DEPTH, 2):
                    rest_table(it * DEPTH + i, i)
            def rest_act(j, slot, first=False):
                pool.wait_ge(act_hi, j + 1)
                if not first:
                    pool.wait_ge(tile_used, j + (N1 + E_TILES - 3))
                pool.tensor_tensor(a_lo[slot][:], H[:, bass.ds(j, 1), :].rearrange("p a t -> p (a t)"),
                                  a_hi[slot][:].bitcast(FP32), ALU.subtract).then_inc(act_lo, 1)
            for i in range(4):
                rest_act(i, i, True)
            pool.wait_ge(h_out, E_TILES)
            for i, name in enumerate(("ln_g", "ln_b")):
                pool.dma_start(ln_last[:, i, :], a[name][2:3, :].broadcast_to([P, D])).then_inc(ln_in, 16)
            with pool.Fori(1, E_TILES // DEPTH) as it:
                for i in range(DEPTH):
                    rest_act(it * DEPTH + i, i)
                    if i % 2:
                        rest_table(it * DEPTH + (E_TILES + i - 1), i - 1)

        @block.scalar
        def _(act):
            def split(n):
                act.wait_ge(raw_in[n % EARLY], 16 * (n // EARLY + 1))
                if n >= DEPTH:
                    act.wait_ge(tile_used, n - DEPTH + 1)
                act.activation(hi[n % DEPTH][:], raw[n % EARLY][:], ACT.Copy).then_inc(hi_done, 1)

            def split_table(n, i, arrived):
                s = (N1 + i) % DEPTH
                act.wait_ge(table_in[i % DEPTH], arrived)
                act.wait_ge(tile_used, n - DEPTH + 1)
                act.activation(hi[s][:], raw[s][:], ACT.Copy).then_inc(hi_done, 1)

            def take(n):
                name, kind, i, k0, m, cols, first, last, use = TILES[n]
                if not last or name in VECTOR_READS:
                    return
                act.wait_ge(tile_used, n + 1)
                if kind == "T":
                    src = psG[use % 2][:, 0:S]
                    if name == "hf":
                        act.activation(Fa[:, i * S:(i + 1) * S], src, ACT.Tanh, scale=0.5).then_inc(act_took, 1)
                        return
                    if name == "pq" and i == 0:
                        act.wait_ge(turned, XU + NT)
                    dst = {"kc": kvc[:, 0, :], "vc": kvc[:, 1, :], "ks": kT[0][:], "kw": kT[1][:],
                           "q": qT[:, i % REP, :], "hq": hq[:, i % HH, :], "mk": xk[:, i, :], "xq": xq[:, i, :],
                           "pq": qryT[:, i, :]}[name]
                    act.activation(dst, src, ACT.Copy).then_inc(act_took, 1)
                    return
                for t in range(NT):
                    src = bank[BANK[use + t]]
                    if name == "mv" and i == 0 and t == 0:
                        act.wait_ge(silu_ready, 1)
                    if name == "vg":
                        act.activation(vg[:, t, 0:2 * P], src[:, 0:2 * P], ACT.Copy)
                        act.activation(vg[:, t, 2 * P:VG], src[:, 2 * P:VG], ACT.Tanh, scale=0.5).then_inc(act_took, 1)
                    elif name == "hv":
                        act.activation(hv[:, t, :], src, ACT.Copy).then_inc(act_took, 1)
                    elif name == "hg":
                        act.activation(hg[:, t, :], src, ACT.Copy)
                        act.activation(hg_t[:, t, :], src, ACT.Tanh, scale=0.5).then_inc(act_took, 1)
                    else:
                        act.activation(xv[:, t, i * 512:(i + 1) * 512], src, ACT.Copy).then_inc(act_took, 1)

            def exp_unit(u):
                b, g, t, heads, keys = unit(u)
                act.wait_ge(max_done, u + 1)
                if u:
                    act.wait_ge(turned, u)
                if b == 2:
                    act.activation(probs[:, 0:NH * NC], cmp_s[:, :, :].rearrange("p h n -> p (h n)"), ACT.Exp)\
                        .then_inc(exp_done, 1)
                    return
                scale = HD ** -0.5 if b < 2 else (D // XH) ** -0.5
                for r in range(heads):
                    last = act.activation(probs[:, r * S:r * S + keys], psS[:, r * S:r * S + keys], ACT.Exp,
                                          bias=neg_max[:, u % 2, r:r + 1], scale=scale,
                                          accum_out=row_sum[:, u % 2, r:r + 1])
                last.then_inc(exp_done, 1)

            def take_probsT(u):
                b, g, t, heads, keys = unit(u)
                act.wait_ge(turned, u + 1)
                if u:
                    act.wait_ge(pv_done, u)
                if b == 2:
                    act.activation(probsT[0:NC, 0:NH * P], psT[0:NC, 0:NH * P], ACT.Copy).then_inc(probsT_ready, 1)
                else:
                    w = heads * P * (keys // P)
                    act.activation(probsT[:, 0:w], psT[:, 0:w], ACT.Copy).then_inc(probsT_ready, 1)

            for i in range(2):
                half = slice(i * KD // 2, (i + 1) * KD // 2)
                act.wait_ge(x_in[i], 16)
                act.activation(o_hi[:, half, :], xT[:, half, :], ACT.Copy).then_inc(split_hi, 1)
            for n in range(DEPTH):
                split(n)
            for what, i in ORDER:
                if what == "gemm":
                    take(i)
                    if i + DEPTH < N1:
                        split(i + DEPTH)
                    elif i + DEPTH < N1 + AHEAD:
                        split_table(i + DEPTH, i + DEPTH - N1, 16 * ((i + DEPTH - N1) // DEPTH + 1))
                    if i == AT["hv"]:
                        act.wait_ge(mem_in, 16)
                        act.activation(b_hi[:], memT[:], ACT.Copy).then_inc(split_hi, 1)
                elif what == "blocks":
                    act.wait_ge(lb_max, 1)
                    act.activation(lb[:, 2:4, :], lb[:, 2:4, :], ACT.Exp).then_inc(lb_exp, 1)
                elif what == "gelu":
                    act.wait_ge(hidden_done, 1)
                    act.activation(hx[:], psM[:, 0:2 * G * NC], ACT.Copy).then_inc(hidden_out, 1)
                    act.wait_ge(hidden_out, 2)
                    act.activation(hy[:], hy[:], ACT.Tanh, scale=(2 / np.pi) ** 0.5).then_inc(tanh_done, 1)
                elif what == "compressed":
                    act.wait_ge(cmp_done, 1)
                    act.activation(kcmp[:], psM[:, 128:128 + NC], ACT.Copy)
                    act.activation(vcmp[:], psM[0:NC, 256:256 + P], ACT.Copy).then_inc(cmp_out, 1)
                elif what == "scores":
                    exp_unit(i)
                elif what == "turn_probs":
                    take_probsT(i)
                elif what == "level" and i[0] == 8:
                    act.wait_ge(level_done, 17)
                    act.activation(att_off[:], psM, ACT.Copy).then_inc(off_ready, 1)
                elif what == "read_out":
                    act.wait_ge(read_done, i + 1)
                    act.activation(oh[:, i, :], psO[:, i * 512:(i + 1) * 512], ACT.Copy).then_inc(read_out_ready, 1)
                elif what == "route":
                    for u in range(i * NT, (i + 1) * NT):
                        act.wait_ge(score_done, u + 1)
                        act.activation(route_s[:, u % NT * PH + i, :],
                                       (psO, psS)[u % 4 // 2][:, u % 2 * 512:u % 2 * 512 + S], ACT.Copy)\
                            .then_inc(score_out, 1)
                elif what == "rms":
                    act.wait_ge(var_ready, 1)
                    act.activation(std[:], std[:], ACT.Sqrt).then_inc(std_ready, 1)
                elif what == "norm":
                    w, t = i
                    act.wait_ge(var_ready, 2 + w * NT + t)
                    act.activation(std[:, t, 0:1], mv[:, t, 1:2], ACT.Sqrt).then_inc(std_ready, 1)
                elif what == "turn":
                    t = i % 2
                    dst = o_hi if i < 4 else b_hi
                    for b in range(2):
                        act.wait_ge(turn_done, 2 * i + b + 1)
                        act.activation(dst[:, 4 * b:4 * b + 4, t * P:(t + 1) * P],
                                       (psS, psT)[t][:, b * 512:(b + 1) * 512].rearrange("p (k c) -> p k c", c=P),
                                       ACT.Copy).then_inc(turn_hi, 1)
            def activations(j, i):
                act.wait_ge(tile_used, j + (N1 + 1))
                act.activation(H[:, bass.ds(j, 1), :].rearrange("p a t -> p (a t)"), psG[i % 2][:, 0:S],
                               ACT.Gelu).then_inc(h_out, 1)

            def ahead(j, i):
                k = (i + AHEAD) % DEPTH
                split_table(j + (N1 + AHEAD), i + AHEAD, (j + (AHEAD - k)) * (16 // DEPTH) + 16)

            act.wait_ge(const_in, 16 * 6)
            act.activation(warm[:], ident[:, 0:8], ACT.Gelu)
            with act.Fori(0, HALF // 8) as it:
                for i in range(8):
                    activations(it * 8 + i, i % DEPTH)
                    ahead(it * 8 + i, i % DEPTH)
            for i in range(4):
                activations(HALF + i, i)
                ahead(HALF + i, i)
                if i == 0:
                    act.wait_ge(shifted, 1)
                    act.activation(chosen_s[:], chosen_s[:], ACT.Exp).then_inc(gate_exp, 1)
            act.wait_ge(index_done, 3)
            act.activation(g_hi[:], psO[:, 2 * S:3 * S], ACT.Copy, scale=GATE_SCALE).then_inc(index_out, 1)
            for q in range(3):
                act.activation((i1T, i2T, gT)[q][:], psO[:, q * S:(q + 1) * S], ACT.Copy,
                               scale=(1.0, 1.0, GATE_SCALE)[q]).then_inc(index_out, 1)
            with act.Fori(HALF // 4 + 1, E_TILES // 4) as it:
                for i in range(4):
                    activations(it * 4 + i, i)
                    ahead(it * 4 + i, i)

            def round_act(j, slot, first=False):
                if not first:
                    act.wait_ge(tile_used, j + (N1 + E_TILES - 3))
                act.activation(a_hi[slot][:], H[:, bass.ds(j, 1), :].rearrange("p a t -> p (a t)"), ACT.Copy)\
                    .then_inc(act_hi, 1)

            def next_tile(j, i):
                round_act(j, i)
                ahead(j + (E_TILES - 4), i)
            act.wait_ge(gated, S // 4)
            for i in range(4):
                round_act(i, i, True)
            with act.Fori(1, HALF // 4) as it:
                for i in range(4):
                    next_tile(it * 4 + i, i)
            act.wait_ge(gated, S // 2)
            with act.Fori(HALF // 4, E_TILES // 4) as it:
                for i in range(4):
                    next_tile(it * 4 + i, i)
            ahead(2 * E_TILES - 4, 0)
            for t in range(NT):
                act.wait_ge(var_ready, 2 + 2 * NT + t)
                act.activation(std2[:, t, 0:1], mv2[:, t, 1:2], ACT.Sqrt).then_inc(std_ready, 1)

        @block.vector
        def _(dve):
            step = Steps(dve, dve_step)

            def rest(n):
                dve.wait_ge(hi_done, n + 1)
                if n >= DEPTH:
                    dve.wait_ge(tile_used, n - DEPTH + 1)
                s = n % (EARLY if n < N1 else DEPTH)
                done, by = (lo_done, 1) if n < N1 else (table_lo[n - N1], DEPTH)
                dve.tensor_tensor(lo[s][:], raw[s][:], hi[n % DEPTH][:].bitcast(FP32), ALU.subtract)\
                    .then_inc(done, by)

            def rest_table(n, i, mine=(1, 3)):
                if i % DEPTH not in mine:
                    return
                dve.wait_ge(hi_done, n + 1)
                s = (N1 + i) % DEPTH
                dve.tensor_tensor(lo[s][:], raw[s][:], hi[s][:].bitcast(FP32), ALU.subtract)\
                    .then_inc(table_lo[i % DEPTH], DEPTH)

            def add_residual(n, tokens=range(NT)):
                name, kind, i, k0, m, cols, first, last, use = TILES[n]
                if not last:
                    return
                src, dst = (x_tok, x1) if name == "wo" else (x1, x2)
                if name == "wo" and i == 0:
                    dve.wait_ge(xtok_in, 16)
                for t in tokens:
                    if t == 0:
                        dve.wait_ge(first_half, FIRST_HALVES.index(n) + 1)
                    else:
                        dve.wait_ge(tile_used, n + 1)
                    z = dst[:, t, i * 512:(i + 1) * 512]
                    dve.scalar_tensor_tensor(out=z, in0=src[:, t, i * 512:(i + 1) * 512], scalar=ALPHA,
                                             in1=bank[BANK[use + t]], op0=ALU.mult, op1=ALU.add)\
                        .then_inc(dve_took, 1)
                    dve.wait_ge(dve_took, TAKEN[use + t][1])
                    step(dve.bn_stats(stats[:, t, i, :], z))

            def variance(t, st, m, eps=EPS):
                dve.bn_aggr(m[:, t, :], st[:, t, :, :].rearrange("p c s -> p (c s)")).then_inc(dve_step, 1)
                step.count += 1
                step.wait()
                dve.tensor_scalar(m[:, t, 1:2], m[:, t, 1:2], eps, None, ALU.add).then_inc(var_ready, 1)

            def normalize(w, t, z, m, sd, rs, gb):
                dve.wait_ge(ln_in, 32 * (w + 1))
                step(dve.scalar_tensor_tensor(out=z, in0=z, scalar=m[:, t, 0:1], in1=gb[:, 0, :],
                                              op0=ALU.subtract, op1=ALU.mult))
                dve.wait_ge(std_ready, 2 + w * NT + t)
                step(dve.reciprocal(rs[:, t, 0:1], sd[:, t, 0:1]))
                step.wait()
                dve.scalar_tensor_tensor(out=z, in0=z, scalar=rs[:, t, 0:1], in1=gb[:, 1, :],
                                         op0=ALU.mult, op1=ALU.add).then_inc(norm_ready, 1)

            def max_unit(u):
                b, g, t, heads, keys = unit(u)
                dve.wait_ge(s_done, u + 1)
                if b == 2:
                    for gg in range(G):
                        step(dve.scalar_tensor_tensor(
                            out=cmp_s[:, gg * REP:(gg + 1) * REP, :],
                            in0=psS[:, gg * 512:gg * 512 + REP * 16].rearrange("p (h n) -> p h n", n=16)[:, :, 0:NC],
                            scalar=HD ** -0.5, in1=cmp_mask[:, t, :].unsqueeze(1).broadcast_to([P, REP, NC]),
                            op0=ALU.mult, op1=ALU.add))
                    step.wait()
                    step(dve.tensor_reduce(row_max[:], cmp_s[:], AX.X, ALU.max))
                    step.wait()
                    dve.tensor_tensor(cmp_s[:], cmp_s[:], row_max[:].unsqueeze(2).broadcast_to([P, NH, NC]),
                                      ALU.subtract).then_inc(max_done, 1)
                    return
                scale = HD ** -0.5 if b < 2 else (D // XH) ** -0.5
                step(dve.tensor_reduce(row_max[:, 0:heads],
                                       psS[:].rearrange("p (h n) -> p h n", n=S)[:, :, 0:keys], AX.X, ALU.max))
                step.wait()
                dve.tensor_scalar(neg_max[:, u % 2, 0:heads], row_max[:, 0:heads], -scale, None, ALU.mult)\
                    .then_inc(max_done, 1)

            def combine(u):
                b, g, t, heads, keys = unit(u)
                dve.wait_ge(exp_done, u + 1)
                if u:
                    dve.wait_ge(combined, u)
                sums = row_sum[:, u % 2, 0:heads]
                if b == 2:
                    step(dve.tensor_reduce(sums, probs[:, 0:NH * NC].rearrange("p (h n) -> p h n", n=NC),
                                           AX.X, ALU.add))
                    step.wait()
                step(dve.reciprocal(coef[:, 0:heads], sums))
                step.wait()
                if b < 3:
                    col = {0: 1, 1: 2, 2: 0}[b]
                    gates = gate[:, t, :].rearrange("p (h c) -> p h c", c=3)[:, g * REP:g * REP + heads, col]
                    step(dve.tensor_tensor(coef[:, 0:heads], coef[:, 0:heads], gates, ALU.mult))
                    step.wait()
                if b == 2:
                    step(dve.tensor_scalar(coef[:], coef[:], cmp_any[:, t:t + 1], None, ALU.mult))
                    step.wait()
                dve.wait_ge(pv_done, u + 1)
                width = HD if b < 3 else D // XH
                src = psO[:, 0:heads * width].rearrange("p (h d) -> p h d", d=width)
                by = coef[:, 0:heads].unsqueeze(2).broadcast_to([P, heads, width])
                if b == 3:
                    dve.tensor_tensor(xo[:, t, :].rearrange("p (h d) -> p h d", d=width), src, by, ALU.mult)\
                        .then_inc(combined, 1)
                    return
                dst = o_acc[:, t, g * 256:g * 256 + heads * HD].rearrange("p (h d) -> p h d", d=HD)
                if b == 0:
                    dve.tensor_tensor(dst, src, by, ALU.mult).then_inc(combined, 1)
                    return
                tmp = o_tmp[:, 0:heads * HD].rearrange("p (h d) -> p h d", d=HD)
                step(dve.tensor_tensor(tmp, src, by, ALU.mult))
                step.wait()
                dve.tensor_tensor(dst, dst, tmp, ALU.add).then_inc(combined, 1)

            def lower_bound():
                dve.wait_ge(rec_in, 32)
                step(dve.tensor_tensor(lb[:, 4, :], lb[:, 0, :], lb[:, 1, :], ALU.max))
                step.wait()
                dve.tensor_tensor(lb[:, 2:4, :], lb[:, 0:2, :], lb[:, 4, :].unsqueeze(1).broadcast_to([P, 2, HH]),
                                  ALU.subtract).then_inc(lb_max, 1)
                dve.wait_ge(lb_exp, 1)
                step(dve.tensor_tensor(lb[:, 4, :], lb[:, 2, :], lb[:, 3, :], ALU.add))
                step.wait()
                step(dve.reciprocal(lb[:, 5, :], lb[:, 4, :]))
                step.wait()
                step(dve.tensor_tensor(lb[:, 6, :], lb[:, 2, :], lb[:, 5, :], ALU.mult))
                step.wait()
                step(dve.tensor_scalar(lb[:, 5, :], lb[:, 6, :], -0.5, 0.5, ALU.mult, ALU.add))
                step.wait()
                step(dve.tensor_tensor(lb[:, 7, :], lb[:, 6, :], lb[:, 5, :], ALU.add))
                step.wait()

            for i in range(2):
                half = slice(i * KD // 2, (i + 1) * KD // 2)
                dve.wait_ge(split_hi, i + 1)
                dve.tensor_tensor(o_lo[:, half, :], xT[:, half, :], o_hi[:, half, :].bitcast(FP32), ALU.subtract)\
                    .then_inc(split_lo, 1)
            for n in range(DEPTH):
                rest(n)
            late = []
            for what, i in ORDER:
                if what == "gemm":
                    if late:
                        rest(late.pop())
                    before_norm = i + 1 in (AT["wo"] + KD, AT["pq"])
                    if TILES[i][0] in VECTOR_READS:
                        add_residual(i, range(1 if before_norm else NT))
                    if before_norm:
                        late.append(i + DEPTH)
                    elif i + DEPTH < N1 or i + DEPTH - N1 in range(1, AHEAD, 2):
                        rest(i + DEPTH)
                    if i == AT["hv"]:
                        dve.wait_ge(split_hi, 3)
                        dve.tensor_tensor(b_lo[:], memT[:], b_hi[:].bitcast(FP32), ALU.subtract)\
                            .then_inc(split_lo, 1)
                    if i == AT["hq"]:
                        dve.wait_ge(act_took, TAKEN[TILES[AT["vg"]][8] + 1][1])
                        step(dve.tensor_scalar(gate[:], vg[:, :, 2 * P:VG], 1.0, 0.5, ALU.add, ALU.mult))
                elif what == "blocks":
                    lower_bound()
                    dve.wait_ge(shift_in, 16 * 4)
                    dve.wait_ge(comp_in, 48)
                    for kv in range(2):
                        for g in range(G):
                            src = kcp[:, kv, g, :]
                            src = bass.AP(tensor=src.tensor, offset=src.offset,
                                          ap=[list(src.ap[0]), [2, CB // 2], [CS, NC]])
                            last = dve.tensor_tensor(blk[:, kv, :, g * NC:(g + 1) * NC], src,
                                                     pos[:, kv, :].unsqueeze(2).broadcast_to([P, CB // 2, NC]),
                                                     ALU.add)
                    last.then_inc(blocks_ready, 1)
                elif what == "gelu":
                    dve.wait_ge(hidden_out, 1)
                    step(dve.tensor_tensor(hy[:], hx[:], hx[:], ALU.mult))
                    step.wait()
                    step(dve.tensor_tensor(hy[:], hy[:], hx[:], ALU.mult))
                    step.wait()
                    dve.scalar_tensor_tensor(out=hy[:], in0=hy[:], scalar=0.044715, in1=hx[:],
                                             op0=ALU.mult, op1=ALU.add).then_inc(hidden_out, 1)
                    dve.wait_ge(tanh_done, 1)
                    step(dve.tensor_scalar(hz[:], hy[:], 1.0, 0.5, ALU.add, ALU.mult))
                    step.wait()
                    dve.tensor_tensor(hz[:], hz[:], hx[:], ALU.mult).then_inc(gelu_ready, 1)
                elif what == "scores":
                    max_unit(i)
                elif what == "values":
                    combine(i)
                elif what == "decay":
                    dve.wait_ge(act_took, TAKEN[TILES[AT["hf"] + HH - 1][8]][1])
                    for h in range(HH):
                        step(dve.tensor_scalar(Fa[:, h * S:(h + 1) * S], Fa[:, h * S:(h + 1) * S], lb[:, 5, h:h + 1],
                                               lb[:, 7, h:h + 1], ALU.mult, ALU.add))
                    step.wait()
                    step(dve.tensor_scalar(KB[:].rearrange("p h t -> p (h t)"), Fa[:], -1.0, 1.0, ALU.mult, ALU.add))
                    dve.tensor_tensor(QF[:].rearrange("p h t -> p (h t)"), Fa[:],
                                      hq[:].rearrange("p h t -> p (h t)"), ALU.mult).then_inc(decay_ready, 1)
                    step.wait()
                elif what == "level" and i[0] < 8:
                    j, t = i
                    dve.wait_ge(level_done, 2 * j + t + 1)
                    if j == 0:
                        dve.wait_ge(att_zero, 1)
                        dve.wait_ge(mask_in, 16)
                    else:
                        dve.wait_ge(level_merged, 2 * j + t - 1)
                    dve.copy_predicated(att[:, :, t, :],
                                        level_mask[:, j, :].bitcast(U16).unsqueeze(1).broadcast_to([P, HH, P]),
                                        psM.rearrange("p (n t) -> p n t", t=P)).then_inc(level_merged, 1)
                    if t == 1 and j >= 1:
                        L = 1 << (j - 1)
                        n = HH * S // (2 * L)
                        F, F2 = (Fa, Fb) if j % 2 else (Fb, Fa)
                        fe = F[:, 0:2 * n].rearrange("p (n b) -> p n b", b=2)
                        if j == 1:
                            dve.wait_ge(decay_ready, 1)
                        else:
                            dve.wait_ge(factors_ready, j - 1)
                        q2 = QF[:].rearrange("p h t -> p (h t)").rearrange("p (n b l) -> p n b l", b=2, l=L)[:, :, 1, :]
                        k2 = KB[:].rearrange("p h t -> p (h t)").rearrange("p (n b l) -> p n b l", b=2, l=L)[:, :, 0, :]
                        dve.tensor_tensor(q2, q2, fe[:, :, 0].unsqueeze(2).broadcast_to([P, n, L]), ALU.mult)
                        dve.tensor_tensor(k2, k2, fe[:, :, 1].unsqueeze(2).broadcast_to([P, n, L]), ALU.mult)
                        dve.tensor_tensor(F2[:, 0:n], fe[:, :, 0], fe[:, :, 1], ALU.mult).then_inc(factors_ready, 1)
                elif what == "rms":
                    dve.wait_ge(read_out_ready, NT)
                    t3 = probs[:].rearrange("p (n e) -> p n e", e=P)
                    o3 = oh[:].rearrange("p t (h e) -> p (t h) e", e=P)
                    step(dve.tensor_tensor(t3, o3, o3, ALU.mult))
                    step.wait()
                    sd = std[:].rearrange("p t h -> p (t h)")
                    step(dve.tensor_reduce(sd, t3, AX.X, ALU.add))
                    step.wait()
                    dve.tensor_scalar(sd, sd, 1.0 / P, EPS, ALU.mult, ALU.add).then_inc(var_ready, 1)
                    dve.wait_ge(std_ready, 1)
                    dve.wait_ge(silu_ready, 1)
                    rs = rstd[:].rearrange("p t h -> p (t h)")
                    step(dve.reciprocal(rs, sd))
                    step.wait()
                    step(dve.tensor_tensor(o3, o3, rs.unsqueeze(2).broadcast_to([P, NT * HH, P]), ALU.mult))
                    step.wait()
                    dve.tensor_tensor(oh[:], oh[:], hg[:], ALU.mult).then_inc(rec_ready, 1)
                elif what == "turn":
                    t = i % 2
                    dst, rounded = (o_lo, o_hi) if i < 4 else (b_lo, b_hi)
                    for b in range(2):
                        dve.wait_ge(turn_hi, 2 * i + b + 1)
                        dve.tensor_tensor(dst[:, 4 * b:4 * b + 4, t * P:(t + 1) * P],
                                          (psS, psT)[t][:, b * 512:(b + 1) * 512].rearrange("p (k c) -> p k c", c=P),
                                          rounded[:, 4 * b:4 * b + 4, t * P:(t + 1) * P].bitcast(FP32), ALU.subtract)\
                            .then_inc(turn_lo, 1)
                elif what == "norm":
                    w, t = i
                    if t == 1:
                        add_residual((AT["wo"] + KD, AT["pq"])[w] - 1, (1,))
                    step.wait()
                    variance(t, stats, mv)
                    normalize(w, t, (x1, x2)[w][:, t, :], mv, std, rstd, ln_gb)

            LOWEST = -3.0e38
            PER = 27
            dve.wait_ge(subk_in, 32)
            dve.wait_ge(score_out, PH * NT)
            step(dve.memset(hold_v[:], 0.0))
            step.wait()
            c0 = step.count
            with dve.Fori(0, HALF // 8) as it:
                mark = {"n": 0}

                def did(instruction):
                    instruction.then_inc(dve_step, 1)
                    mark["n"] += 1

                def mine():
                    dve.wait_ge(dve_step, it * (2 * PER) + (c0 + mark["n"]))
                    dve.tensor_copy(hold_v[:, 0:1], hold_v[:, 1:2])

                def ahead(i):
                    rest_table(it * 8 + (N1 + AHEAD + i), i + AHEAD, (1,))

                def best(*lists):
                    for values, spare, out_v, out_i in lists:
                        did(dve.max(out_v[:, 0:8], values))
                    mine()
                    for values, spare, out_v, out_i in lists:
                        did(dve.max_index(out_i[:, 0:8], out_v[:, 0:8], values))
                        did(dve.match_replace(spare, out_v[:, 0:8], values, LOWEST))
                    mine()
                    for values, spare, out_v, out_i in lists:
                        did(dve.max(out_v[:, 8:16], spare))
                    mine()
                    for values, spare, out_v, out_i in lists:
                        did(dve.max_index(out_i[:, 8:16], out_v[:, 8:16], spare))

                def route(r):
                    u = it * 2 + r
                    ahead(4 * r)
                    did(dve.tensor_copy(unit_s[:].rearrange("p c n -> p (c n)"),
                                        route_s[:, bass.ds(u, 1), :].rearrange("p a n -> p (a n)")))
                    mine()
                    best(*((unit_s[:, c, :], unit_w[:, c, :], unit_m[:, c, :], unit_i[:, c, :]) for c in range(2)))
                    ahead(4 * r + 1)
                    mine()
                    did(dve.tensor_copy(unit_if[:], unit_i[:]))
                    cand = unit_c[:, 0, :, :]
                    did(dve.tensor_tensor(cand, unit_m[:, 0, :].unsqueeze(2).broadcast_to([P, TOPK, TOPK]),
                                          unit_m[:, 1, :].unsqueeze(1).broadcast_to([P, TOPK, TOPK]), ALU.add))
                    mine()
                    best((cand.rearrange("p a b -> p (a b)"), unit_w[:].rearrange("p c n -> p (c n)"),
                          unit_t[:], unit_p[:]))
                    ahead(4 * r + 2)
                    mine()
                    did(dve.tensor_copy(chosen_s[:, bass.ds(u, 1), :].rearrange("p a k -> p (a k)"), unit_t[:]))
                    did(dve.tensor_scalar(unit_ab[:, 0, :], unit_p[:], 4, None, ALU.logical_shift_right))
                    did(dve.tensor_scalar(unit_ab[:, 1, :], unit_p[:], 15, None, ALU.bitwise_and))
                    mine()
                    did(dve.tensor_copy(unit_abf[:], unit_ab[:]))
                    mine()
                    did(dve.tensor_tensor(unit_c[:].rearrange("p c k a -> p (c k) a"),
                                          iota16[:].unsqueeze(1).broadcast_to([P, 2 * TOPK, TOPK]),
                                          unit_abf[:].rearrange("p c k -> p (c k)").unsqueeze(2)
                                          .broadcast_to([P, 2 * TOPK, TOPK]), ALU.is_equal))
                    mine()
                    ahead(4 * r + 3)
                    for c in range(2):
                        did(dve.tensor_tensor(unit_c[:, c, :, :], unit_c[:, c, :, :],
                                              unit_if[:, c, :].unsqueeze(1).broadcast_to([P, TOPK, TOPK]), ALU.mult))
                    mine()
                    did(dve.tensor_reduce(chosen[:, 0, bass.ds(u, 1), :].rearrange("p a k -> p (a k)"),
                                          unit_c[:, 0, :, :], AX.X, ALU.add))
                    did(dve.tensor_reduce(chosen[:, 1, bass.ds(u, 1), :].rearrange("p a k -> p (a k)"),
                                          unit_c[:, 1, :, :], AX.X, ALU.add))
                    mine()
                route(0)
                route(1)
                assert mark["n"] == 2 * PER, mark
            step.count = c0 + PER * PH * NT

            step.wait()
            step(dve.tensor_copy(gate_z[:], chosen_s[:, :, 0]))
            step.wait()
            dve.tensor_tensor(chosen_s[:], chosen_s[:], gate_z[:].unsqueeze(2).broadcast_to([P, PH * NT, TOPK]),
                              ALU.subtract).then_inc(shifted, 1)
            rest_table(N1 + HALF + AHEAD, AHEAD)
            dve.wait_ge(gate_exp, 1)
            step(dve.tensor_reduce(gate_z[:], chosen_s[:], AX.X, ALU.add))
            step.wait()
            step(dve.reciprocal(gate_z[:], gate_z[:]))
            step.wait()
            dve.tensor_tensor(chosen_s[:], chosen_s[:], gate_z[:].unsqueeze(2).broadcast_to([P, PH * NT, TOPK]),
                              ALU.mult).then_inc(gate_ready, 1)
            for i in range(1, 4):
                rest_table(N1 + HALF + AHEAD + i, i + AHEAD)

            def one_hot(g, slot, half, first=False):
                if not first:
                    dve.wait_ge(gates_done, g - 1)
                t = g * 4 - half * S
                dve.tensor_tensor(one2[slot][:], iota[:].unsqueeze(1).broadcast_to([P, 4, NK]),
                                  i2T[:, bass.ds(t, 4)].unsqueeze(2).broadcast_to([P, 4, NK]), ALU.is_equal)
                dve.tensor_tensor(same1[slot][:],
                                  iota[:, half * HALF:(half + 1) * HALF].unsqueeze(1).broadcast_to([P, 4, HALF]),
                                  i1T[:, bass.ds(t, 4)].unsqueeze(2).broadcast_to([P, 4, HALF]), ALU.is_equal)\
                    .then_inc(same_ready, 1)
                dve.wait_ge(same_ready, g + 1)
                dve.tensor_tensor(one1_hi[slot][:], same1[slot][:],
                                  g_hi[:, bass.ds(t, 4)].unsqueeze(2).broadcast_to([P, 4, HALF]), ALU.mult)
                dve.tensor_tensor(one1_lo[slot][:], same1[slot][:],
                                  g_lo[:, bass.ds(t, 4)].unsqueeze(2).broadcast_to([P, 4, HALF]), ALU.mult)\
                    .then_inc(one_ready, 1)

            def apply_gates(g, slot, half):
                dve.wait_ge(gates_done, g + 1)
                h = H[:, half * HALF:(half + 1) * HALF, bass.ds(g * 4 - half * S, 4)].rearrange("p j t -> p t j")
                dve.tensor_tensor(h, psO[:, slot * 512:slot * 512 + 4 * HALF].rearrange("p (t j) -> p t j", j=HALF),
                                  h, ALU.mult).then_inc(gated, 1)
            dve.wait_ge(index_out, 4)
            step(dve.tensor_tensor(g_lo[:], gT[:], g_hi[:], ALU.subtract))
            step.wait()
            one_hot(0, 0, 0, True)
            for i in range(4):
                one_hot(i + 1, (i + 1) % 2, 0, i == 0)
                if i == 0:
                    dve.wait_ge(h_out, HALF)
                apply_gates(i, i % 2, 0)
                rest_table(N1 + HALF + DEPTH + AHEAD + i, i + AHEAD)
            with dve.Fori(1, EVEN // 4) as it:
                for i in range(4):
                    one_hot(it * 4 + (i + 1), (i + 1) % 2, 0)
                    apply_gates(it * 4 + i, i % 2, 0)
                    rest_table(it * 4 + (N1 + HALF + DEPTH + AHEAD + i), i + AHEAD)
            g = EVEN
            for k in range(HALF - 4 - EVEN):
                for x in range(1 + k % 2):
                    one_hot(g + 1, (g + 1) % 2, int(g + 1 == S // 4))
                    apply_gates(g, g % 2, 0)
                    g += 1
                    if x == 0:
                        rest_table(N1 + HALF + DEPTH + AHEAD + EVEN + k, k + AHEAD)

            dve.wait_ge(h_out, E_TILES)
            with dve.Fori(1, HALF // 4) as it:
                for i in range(4):
                    j = it * 4 + i
                    one_hot(j + (HALF - 3), (i + 1) % 2, 1)
                    apply_gates(j + (HALF - 4), i % 2, 1)
                    rest_table(j + (N1 + E_TILES - 1), i + AHEAD)
            for g in range(S // 2 - 4, S // 2):
                if g + 1 < S // 2:
                    one_hot(g + 1, (g + 1) % 2, 1)
                apply_gates(g, g % 2, 1)
            with dve.Fori(HALF // 4, E_TILES // 4) as it:
                for i in range(4):
                    j = it * 4 + i
                    rest_table(j + (N1 + E_TILES - 1), i + AHEAD)
            rest_table(N1 + 2 * E_TILES - 1, AHEAD)
            for t in range(NT):
                if t == 0:
                    dve.wait_ge(first_half, len(FIRST_HALVES) + 1)
                else:
                    dve.wait_ge(tile_used, N1 + 2 * E_TILES)
                for c in range(2):
                    z = x2[:, t, c * 512:(c + 1) * 512]
                    step(dve.scalar_tensor_tensor(out=z, in0=z, scalar=ALPHA * GATE_SCALE,
                                                  in1=(psS, psT)[t][:, c * 512:(c + 1) * 512],
                                                  op0=ALU.mult, op1=ALU.add))
                    step.wait()
                    step(dve.bn_stats(stats2[:, t, c, :], z))
                step.wait()
                variance(t, stats2, mv2, EPS * GATE_SCALE ** 2)
                normalize(2, t, x2[:, t, :], mv2, std2, rstd2, ln_last)

        @block.tensor
        def _(pe):
            def three(out, hi_l, lo_l, hi_r, lo_r, start, stop):
                pe.matmul(out, hi_l, hi_r, start=start, stop=False)
                pe.matmul(out, hi_l, lo_r, start=False, stop=False)
                return pe.matmul(out, lo_l, hi_r, start=False, stop=stop)

            def gemm(n):
                name, kind, i, k0, m, cols, first, last, use = TILES[n]
                act_hi_t, act_lo_t = (b_hi, b_lo) if name in ("mk", "mv", "xo", "pq") else (o_hi, o_lo)
                pe.wait_ge(lo_done, n + 1)
                if name == "mk" and i == 0:
                    pe.wait_ge(split_lo, 3)
                turned_in = 0
                if name in ("wo", "xq", "xo", "pq") and i == 0 and k0 == 0:
                    turned_in = 2 * NT * (1 + ("wo", "xq", "xo", "pq").index(name))
                if first:
                    for u in range(use, use + (1 if kind == "T" else NT)):
                        if BEFORE[u] is not None:
                            v, count = TAKEN[BEFORE[u]]
                            pe.wait_ge(took[v], count)
                    if BANK[use] == 2:
                        pe.wait_ge(*((read_out_ready, NT) if name == "wo" else (combined, XU + NT)))
                s = n % DEPTH
                if kind == "T":
                    wh = hi[s][:].rearrange("p (k c) -> p k c", c=P)
                    wl = lo[n % EARLY][:].rearrange("p (k c) -> p k c", c=P)
                    if turned_in:
                        pe.wait_ge(turn_lo, turned_in)
                    for k in range(KD):
                        mm = three(psG[use % 2][:, 0:S], wh[:, k, :], wl[:, k, :], act_hi_t[:, k, :],
                                   act_lo_t[:, k, :], k == 0, k == KD - 1)
                else:
                    for t in range(NT):
                        if turned_in:
                            pe.wait_ge(turn_lo, turned_in - NT * (1 - t))
                        for kk in range(m):
                            cut = slice(kk * cols, (kk + 1) * cols)
                            k = k0 + kk
                            mm = three(bank[BANK[use + t]][:, 0:cols], act_hi_t[:, k, t * P:(t + 1) * P],
                                       act_lo_t[:, k, t * P:(t + 1) * P], hi[s][:, cut], lo[n % EARLY][:, cut],
                                       k == 0, k == KD - 1)
                        if t == 0 and n in FIRST_HALVES:
                            mm.then_inc(first_half, 1)
                mm.then_inc(tile_used, 1)

            def scores(u):
                b, g, t, heads, keys = unit(u)
                if u == 0:
                    pe.wait_ge(const_in, 16 * 6)
                    pe.wait_ge(act_took, TAKEN[TILES[AT["vg"]][8] + 1][1])
                if b == 2:
                    pe.wait_ge(cmp_out, 1)
                    pe.wait_ge(exp_done, u)
                    for h in range(NH):
                        at = h // REP * HD
                        col = h // REP * 512 + h % REP * 16
                        mm = pe.matmul(psS[:, col:col + NC], qT[at:at + HD, h % REP, t * P:(t + 1) * P],
                                       kcmp[at:at + HD, :], start=True, stop=True)
                    mm.then_inc(s_done, 1)
                    return
                if u:
                    pe.wait_ge(exp_done, u)
                if b == 3:
                    if u == XU:
                        pe.wait_ge(turn_lo, 8)
                        pe.wait_ge(act_took, TAKEN[TILES[AT["xq"] + KD - 1][8]][1])
                    for h in range(XH):
                        for kk in range(2):
                            mm = pe.matmul(psS[:, h * S:(h + 1) * S], xq[:, 2 * h + kk, t * P:(t + 1) * P],
                                           xk[:, 2 * h + kk, :], start=kk == 0, stop=kk == 1)
                    mm.then_inc(s_done, 1)
                    return
                for r in range(REP):
                    for kb in range(t + 1):
                        out = psS[:, r * S + kb * P:r * S + (kb + 1) * P]
                        diagonal = kb == t
                        mm = pe.matmul(out, qT[g * HD:(g + 1) * HD, r, t * P:(t + 1) * P],
                                       kT[b][g * HD:(g + 1) * HD, kb * P:(kb + 1) * P], start=True, stop=not diagonal)
                        if diagonal:
                            mm = pe.matmul(out, identb[:], causal[:], start=False, stop=True)
                mm.then_inc(s_done, 1)

            def turn_probs(u):
                b, g, t, heads, keys = unit(u)
                pe.wait_ge(exp_done, u + 1)
                if u:
                    pe.wait_ge(probsT_ready, u)
                if u == XU:
                    pe.wait_ge(turn_lo, 8)
                if b == 2:
                    for h in range(NH):
                        mm = pe.transpose(psT[0:NC, h * P:(h + 1) * P], probs[:, h * NC:(h + 1) * NC], ident[:])
                else:
                    kbs = keys // P
                    for r in range(heads):
                        for kb in range(kbs):
                            at = (r * kbs + kb) * P
                            mm = pe.transpose(psT[:, at:at + P], probs[:, r * S + kb * P:r * S + (kb + 1) * P],
                                              ident[:])
                mm.then_inc(turned, 1)

            def values(u):
                b, g, t, heads, keys = unit(u)
                pe.wait_ge(probsT_ready, u + 1)
                if u:
                    pe.wait_ge(combined, u)
                if u == XU:
                    pe.wait_ge(read_out_ready, NT)
                if b == 2:
                    for h in range(NH):
                        gg = h // REP
                        mm = pe.matmul(psO[:, h * HD:(h + 1) * HD], probsT[0:NC, h * P:(h + 1) * P],
                                       vcmp[:, gg * HD:(gg + 1) * HD], start=True, stop=True)
                elif b == 3:
                    for h in range(XH):
                        for kb in range(2):
                            mm = pe.matmul(psO[:, h * 256:(h + 1) * 256],
                                           probsT[:, (h * 2 + kb) * P:(h * 2 + kb + 1) * P],
                                           xv[:, kb, h * 256:(h + 1) * 256], start=kb == 0, stop=kb == 1)
                else:
                    for r in range(REP):
                        for kb in range(t + 1):
                            at = (r * (t + 1) + kb) * P
                            mm = pe.matmul(psO[:, r * HD:(r + 1) * HD], probsT[:, at:at + P],
                                           vg[:, kb, b * P + g * HD:b * P + (g + 1) * HD],
                                           start=kb == 0, stop=kb == t)
                mm.then_inc(pv_done, 1)

            pe.wait_ge(split_lo, 2)
            for what, i in ORDER:
                if what == "gemm":
                    gemm(i)
                elif what == "hidden":
                    pe.wait_ge(blocks_ready, 1)
                    for kv in range(2):
                        for m in range(CB // 2):
                            mm = pe.matmul(psM[:, kv * G * NC:(kv + 1) * G * NC], w1[:, kv, m, :], blk[:, kv, m, :],
                                           start=m == 0, stop=m == CB // 2 - 1)
                    mm.then_inc(hidden_done, 1)
                elif what == "compressed":
                    pe.wait_ge(gelu_ready, 1)
                    for g in range(G):
                        pe.matmul(psM[g * HD:(g + 1) * HD, 128:128 + NC], w2[:, 0, :],
                                  hz[:, g * NC:(g + 1) * NC], start=True, stop=True)
                    for g in range(G):
                        mm = pe.matmul(psM[0:NC, 256 + g * HD:256 + (g + 1) * HD],
                                       hz[:, (G + g) * NC:(G + g + 1) * NC], w2[:, 1, :], start=True, stop=True)
                    mm.then_inc(cmp_done, 1)
                elif what == "scores":
                    scores(i)
                elif what == "turn_probs":
                    turn_probs(i)
                elif what == "values":
                    values(i)
                elif what == "level":
                    j, t = i
                    if j == 0 and t == 0:
                        pe.wait_ge(decay_ready, 1)
                        pe.wait_ge(cmp_out, 1)
                    else:
                        pe.wait_ge(level_merged, 2 * j + t)
                    if j >= 2:
                        pe.wait_ge(factors_ready, j - 1)
                    for h in range(HH):
                        if j == 8:
                            mm = pe.matmul(psM[:, h * P:(h + 1) * P], KB[:, h, 0:P], QF[:, h, P:S],
                                           start=True, stop=True)
                        else:
                            mm = pe.matmul(psM[:, h * P:(h + 1) * P], KB[:, h, t * P:(t + 1) * P],
                                           (hq if j == 0 else QF)[:, h, t * P:(t + 1) * P], start=True, stop=True)
                    mm.then_inc(level_done, 1)
                elif what == "read_out":
                    pe.wait_ge(level_merged, 16)
                    pe.wait_ge(off_ready, 1)
                    pe.wait_ge(combined, XU)
                    for h in range(HH):
                        out = psO[:, i * 512 + h * P:i * 512 + (h + 1) * P]
                        mm = pe.matmul(out, att[:, h, i, :], hv[:, i, h * P:(h + 1) * P], start=True, stop=i == 0)
                        if i == 1:
                            mm = pe.matmul(out, att_off[:, h, :], hv[:, 0, h * P:(h + 1) * P], start=False, stop=True)
                    mm.then_inc(read_done, 1)
                elif what == "route":
                    if i == 0:
                        pe.wait_ge(subk_in, 32)
                        pe.wait_ge(combined, XU + NT)
                    pe.wait_ge(act_took, TAKEN[TILES[AT["pq"] + i][8]][1])
                    for u in range(i * NT, (i + 1) * NT):
                        if u >= 4:
                            pe.wait_ge(score_out, u - 3)
                        t = u % NT
                        pe.matmul((psO, psS)[u % 4 // 2][:, u % 2 * 512:u % 2 * 512 + S],
                                  qryT[:, i, t * P:(t + 1) * P], subk[:, i, :], start=True, stop=True)\
                            .then_inc(score_done, 1)
                elif what == "turn":
                    t = i % 2
                    if i == 0:
                        pe.wait_ge(rec_ready, 1)
                        pe.wait_ge(exp_done, XU)
                        pe.wait_ge(probsT_ready, XU)
                    elif i in (2, 3):
                        pe.wait_ge(norm_ready, i - 1)
                        pe.wait_ge(turn_lo, 2 * (i - 1))
                    elif i in (4, 5):
                        pe.wait_ge(combined, XU + i - 3)
                        pe.wait_ge(exp_done, XU + NT)
                        pe.wait_ge(probsT_ready, XU + NT)
                    elif i in (6, 7):
                        pe.wait_ge(norm_ready, i - 3)
                        pe.wait_ge(turn_lo, 2 * (i - 1))
                    for k in range(KD):
                        if i < 2:
                            src = (o_acc if k < 4 else oh)[:, t, k % 4 * P:(k % 4 + 1) * P]
                        else:
                            src = (x1, xo, x2)[i // 2 - 1][:, t, k * P:(k + 1) * P]
                        mm = pe.transpose((psS, psT)[t][:, k * P:(k + 1) * P], src, ident[:])
                        if k % 4 == 3:
                            mm.then_inc(turn_done, 1)
            def down(j, i, first):
                s = (N1 + i) % DEPTH
                pe.wait_ge(table_lo[i], j + (DEPTH - i))
                if not first:
                    pe.wait_ge(h_out, j - 1)
                wh = hi[s][:].rearrange("p (k c) -> p k c", c=P)
                wl = lo[s][:].rearrange("p (k c) -> p k c", c=P)
                for k in range(KD):
                    mm = three(psG[i % 2][:, 0:S], wh[:, k, :], wl[:, k, :], b_hi[:, k, :], b_lo[:, k, :],
                               k == 0, k == KD - 1)
                mm.then_inc(tile_used, 1)
            def gates(g, slot, first=False):
                pe.wait_ge(one_ready, g + 1)
                if not first:
                    pe.wait_ge(gated, g - 1)
                for i in range(4):
                    out = psO[:, slot * 512 + i * HALF:slot * 512 + (i + 1) * HALF]
                    pe.matmul(out, one2[slot][:, i, :], one1_hi[slot][:, i, :], start=True, stop=False)
                    mm = pe.matmul(out, one2[slot][:, i, :], one1_lo[slot][:, i, :], start=False, stop=True)
                mm.then_inc(gates_done, 1)
            for j in range(4):
                down(j, j, j < 2)
            with pe.Fori(1, HALF // 4) as it:
                for i in range(4):
                    down(it * 4 + i, i, False)
            for i in range(4):
                down(HALF + i, i, False)
                if i == 3:
                    pe.wait_ge(gate_ready, 1)
                    pe.wait_ge(score_out, PH * NT)
                    for q in range(3):
                        for t in range(NT):
                            src = (chosen[:, 0], chosen[:, 1], chosen_s[:])[q]
                            mm = pe.transpose(psO[:, q * S + t * P:q * S + (t + 1) * P],
                                              src[:, t * PH:(t + 1) * PH, :].rearrange("p h k -> p (h k)"), ident[:])
                        mm.then_inc(index_done, 1)
            for i in range(4):
                down(HALF + 4 + i, i, False)
                if i == 0:
                    pe.wait_ge(index_out, 4)
                gates(i, i % 2, i < 2)
            with pe.Fori(1, EVEN // 4) as it:
                for i in range(4):
                    down(it * 4 + (HALF + 4 + i), i, False)
                    gates(it * 4 + i, i % 2)
            g = EVEN
            for k in range(HALF - 4 - EVEN):
                down(HALF + 4 + EVEN + k, k % 4, False)
                for _ in range(1 + k % 2):
                    gates(g, g % 2)
                    g += 1

            def up(j, i, start, stop):
                pe.wait_ge(table_lo[i], j + (E_TILES + DEPTH - i))
                pe.wait_ge(act_lo, j + 1)
                s = (N1 + i) % DEPTH
                for t in range(NT):
                    cut = slice(t * P, (t + 1) * P)
                    for left, right, st, sp in ((a_hi[i], hi[s], start, False), (a_hi[i], lo[s], False, False),
                                                (a_lo[i], hi[s], False, stop)):
                        for c in range(2):
                            mm = pe.matmul((psS, psT)[t][:, c * 512:(c + 1) * 512], left[:, cut],
                                           right[:, c * 512:(c + 1) * 512], start=st, stop=sp)
                    if t == 0 and stop:
                        mm.then_inc(first_half, 1)
                mm.then_inc(tile_used, 1)
            def round_of(it):
                for i in range(4):
                    up(it * 4 + i, i, False, False)
                    gates(it * 4 + (HALF + i), i % 2)
            for i in range(4):
                up(i, i, i == 0, False)
                gates(HALF + i, i % 2)
            with pe.Fori(1, HALF // 4 - 1) as it:
                round_of(it)
            for i in range(4):
                if i < 2:
                    gates(S // 2 - 4 + 2 * i, 0)
                    gates(S // 2 - 3 + 2 * i, 1)
                up(HALF - 4 + i, i, False, False)
            with pe.Fori(HALF // 4, E_TILES // 4 - 1) as it:
                for i in range(4):
                    up(it * 4 + i, i, False, False)
            for i in range(4):
                up(E_TILES - 4 + i, i, False, i == 3)


def tile_of(w):
    return w.reshape(KD, P, P).transpose(1, 0, 2).reshape(P, D)


def stream(w_in, w_out, xa_wq, xa_wkv, xa_wo, peer_wq):
    cuts = np.cumsum([512] + [P] * 6 + [24] + [512] * 4)
    qa, kc, vc, ks, vs, kw, vw, ga, qb, fb, ib, gb = np.split(w_in, cuts[:-1], axis=1)
    qa = qa.reshape(D, G, REP, HD).transpose(0, 2, 1, 3).reshape(D, 512)
    source = {"kc": kc, "vc": vc, "ks": ks, "kw": kw, "q": qa, "vg": np.concatenate([vs, vw, ga], axis=1),
              "hq": qb, "hf": fb, "hv": ib, "hg": gb, "mk": xa_wkv[:, :D], "mv": xa_wkv[:, D:], "wo": w_out,
              "xq": xa_wq, "xo": xa_wo, "pq": peer_wq}
    out = np.zeros((N1, P, D), np.float32)
    for n, (name, kind, i, k0, m, cols, first, last, use) in enumerate(TILES):
        w = source[name][:, i * cols:(i + 1) * cols]
        if kind == "T":
            out[n] = tile_of(w)
        else:
            out[n, :, :m * cols] = w[k0 * P:(k0 + m) * P].reshape(m, P, cols).transpose(1, 0, 2).reshape(P, m * cols)
    return out


def constants():
    bf = np.dtype("bfloat16")
    i = np.arange(P)
    s, t = i[:, None], i[None, :]
    masks = np.zeros((P, 8, P), np.float32)
    masks[:, 0] = s == t
    for j in range(1, 8):
        masks[:, j] = (((s ^ t) >> (j - 1)) == 1) & (t > s)
    tok = (np.arange(NT)[None, :] * P + i[:, None])
    valid = (np.arange(NC) * CS + CB - 1)[None, None, :] <= tok[:, :, None]
    return {"ident": np.eye(P, dtype=np.float32), "identb": np.eye(P).astype(bf),
            "iota": np.broadcast_to(i, (P, P)).astype(np.float16),
            "iota16": np.broadcast_to(np.arange(TOPK), (P, TOPK)).astype(np.float32),
            "causal": np.where(t > s, -1e30, 0.0).astype(bf),
            "cmp_mask": np.where(valid, 0.0, -1e30).astype(np.float32),
            "cmp_any": valid.any(-1).astype(np.float32),
            "level_mask": masks.astype(bf)}


def kernel(x, mem, w_in, cmp_pos, cmp_w1, cmp_w2, hgrn_lb_logits, hgrn_norm_w, w_out,
           xa_wq, xa_wkv, xa_wo, peer_wq, peer_subkeys, peer_down, peer_up, ln_g, ln_b):
    import concourse.bacc as bacc
    from concourse.bass_utils import run_bass_kernel_spmd

    f = lambda v: np.asarray(v)
    x, mem = f(x)[0], f(mem)[0]
    sub = f(peer_subkeys)[0]
    subk = np.zeros((P, PH, 2 * NK), np.float32)
    for c in range(2):
        subk[c * 64:(c + 1) * 64, :, c * NK:(c + 1) * NK] = sub[:, c].transpose(2, 0, 1)
    arrays = {
        "xT": x.T.reshape(KD, P, S).transpose(1, 0, 2),
        "memT": mem.T.reshape(KD, P, S).transpose(1, 0, 2),
        "x_tok": x.reshape(NT, P, D).transpose(1, 0, 2),
        "w_stream": stream(f(w_in)[0], f(w_out)[0], f(xa_wq)[0], f(xa_wkv)[0], f(xa_wo)[0], f(peer_wq)[0]),
        "down": f(peer_down)[0].reshape(E_TILES, P, KD, P).transpose(0, 3, 2, 1).reshape(E_TILES, P, D),
        "up": f(peer_up)[0].reshape(E_TILES, P, D),
        "w1": f(cmp_w1)[0].reshape(2, CB // 2, P, P).transpose(2, 0, 1, 3),
        "w2": f(cmp_w2)[0].transpose(1, 0, 2),
        "pos": f(cmp_pos)[0].reshape(2, CB // 2, P).transpose(2, 0, 1),
        "lb": f(hgrn_lb_logits).transpose(2, 0, 1),
        "norm_w": f(hgrn_norm_w)[0].reshape(1, 512),
        "subk": subk,
        "ln_g": f(ln_g)[0], "ln_b": f(ln_b)[0],
        **constants(),
    }
    arrays = {k: np.ascontiguousarray(v) for k, v in arrays.items()}
    nc = bacc.Bacc("TRN2", target_bir_lowering=False, num_devices=1)
    aps = {k: nc.dram_tensor(f"in_{k}", v.shape, mybir.dt.from_np(v.dtype), kind="ExternalInput").ap()
           for k, v in arrays.items()}
    aps["out"] = nc.dram_tensor("out_x", (S, D), FP32, kind="ExternalOutput").ap()
    build(nc, aps)
    r = run_bass_kernel_spmd(nc, [{f"in_{k}": v for k, v in arrays.items()}], core_ids=[0])
    return r.results[0]["out_x"].reshape(1, S, D)
```
